# Optimizing a Trainium2 kernel written in Bass

```python
import jax, jax.numpy as jnp
from jax import lax
import numpy as np

D_MODEL = 1024
BATCH = 1
SEQ = 512
DEPTH = 1
DEC_BATCH = 8
DEC_SEQ = 4
PAST_LEN = 4096
PAGE_SIZE = 128

W_POOL = D_MODEL // 2
POOL_WINDOWS = (2, 4, 8, 16)
N_POOL_GROUPS = len(POOL_WINDOWS)
POOL_GC = W_POOL // N_POOL_GROUPS
POOL_HIST = max(POOL_WINDOWS) - 1
W_SGU = D_MODEL // 2
SGU_HEADS = 4
SGU_HC = W_SGU // SGU_HEADS
CHUNK = 128
W_CONV = D_MODEL // 2
CONV_WIDTH = 31
CONV_HIST = CONV_WIDTH - 1
N_BRANCH = 3
IN_COLS = W_POOL + 2 * W_SGU + 2 * W_CONV + N_BRANCH * D_MODEL
N_GROUPS = 4
EXPERTS_PER_GROUP = 8
N_EXPERTS = N_GROUPS * EXPERTS_PER_GROUP
TOP_K_INNER = 2
D_EXPERT = D_MODEL // 2
MOE_BLOCK = 128
EPS = 1e-6

kernel_name = 'hybrid_pool_sgu_conv_hmoe_step'

def rms_norm(x, g):
    xf = x.astype(jnp.float32)
    y = xf * lax.rsqrt(jnp.mean(xf * xf, axis=-1, keepdims=True) + EPS)
    return (y * g.astype(jnp.float32)).astype(x.dtype)

def layer_norm(x, g, b):
    xf = x.astype(jnp.float32)
    mu = jnp.mean(xf, axis=-1, keepdims=True)
    var = jnp.mean(jnp.square(xf - mu), axis=-1, keepdims=True)
    y = (xf - mu) * lax.rsqrt(var + EPS)
    return (y * g.astype(jnp.float32) + b.astype(jnp.float32)).astype(x.dtype)

def pool_branch(p, prev, pos, pool_w, pool_scale):
    bsz, t, _ = p.shape
    ext = jnp.concatenate([prev, p], axis=1)
    cs = jnp.cumsum(ext.astype(jnp.float32), axis=1)
    cs = jnp.concatenate([jnp.zeros((bsz, 1, W_POOL), jnp.float32), cs], axis=1)
    top = cs[:, POOL_HIST + 1:]
    means = []
    for gi, w in enumerate(POOL_WINDOWS):
        sl = slice(gi * POOL_GC, (gi + 1) * POOL_GC)
        lo = cs[:, POOL_HIST + 1 - w: POOL_HIST + 1 - w + t, sl]
        cnt = jnp.minimum(pos + 1, w).astype(jnp.float32)[None, :, None]
        means.append((top[..., sl] - lo) / cnt)
    mean = jnp.concatenate(means, axis=-1)
    d = (mean - p.astype(jnp.float32)).astype(p.dtype).reshape(bsz, t, N_POOL_GROUPS, POOL_GC)
    y = jnp.einsum('btgc,gcd->btgd', d, pool_w).reshape(bsz, t, W_POOL) * pool_scale
    return y, ext[:, -POOL_HIST:]

def sgu_branch(u, v, g, b, w_s, b_s):
    bsz, t, _ = v.shape
    vn = layer_norm(v, g, b)
    ln = min(t, CHUNK)
    nc = t // ln
    ws = jnp.tril(w_s[:, :ln, :ln])
    vh = vn.reshape(bsz, nc, ln, SGU_HEADS, SGU_HC)
    s = jnp.einsum('hts,bnshc->bnthc', ws, vh) + b_s[:, :ln].T[:, :, None]
    return u * s.reshape(bsz, t, W_SGU), vn

def conv_branch(a, gate, prev, conv_w, conv_b, g, b):
    c = a * jax.nn.sigmoid(gate)
    ext = jnp.concatenate([prev, c], axis=1)
    y = lax.conv_general_dilated(ext, conv_w[:, None, :], (1,), 'VALID',
                                 dimension_numbers=('NWC', 'WIO', 'NWC'),
                                 feature_group_count=W_CONV) + conv_b
    y = jax.nn.silu(layer_norm(y, g, b))
    return y, ext[:, -CONV_HIST:]

def mixer_block(xn, pool_prev, conv_prev, pos, w_in, pool_w, pool_scale, sgu_g, sgu_bn, sgu_w, sgu_b,
                conv_w, conv_b, cn_g, cn_b, wb_pool, wb_sgu, wb_conv, w_out):
    h = xn @ w_in
    o1 = W_POOL
    o2 = o1 + W_SGU
    o3 = o2 + W_SGU
    o4 = o3 + W_CONV
    o5 = o4 + W_CONV
    p, u, v, ca, cg, gl = jnp.split(h, [o1, o2, o3, o4, o5], axis=-1)
    ya, new_pool = pool_branch(p, pool_prev, pos, pool_w, pool_scale)
    yb, vn = sgu_branch(u, v, sgu_g, sgu_bn, sgu_w, sgu_b)
    yc, new_conv = conv_branch(ca, cg, conv_prev, conv_w, conv_b, cn_g, cn_b)
    ga, gb, gc = jnp.split(jax.nn.sigmoid(gl), N_BRANCH, axis=-1)
    merged = ga * (ya @ wb_pool) + gb * (yb @ wb_sgu) + gc * (yc @ wb_conv)
    return merged @ w_out, new_pool, new_conv, vn

def moe_ffn(xn, w_group, b_group, w_router, b_router, w_gate_e, w_up_e, w_down_e):
    bsz, t, d = xn.shape
    n = bsz * t
    xt = xn.reshape(n, d)
    grp_logits = (xt @ w_group).astype(jnp.float32) + b_group.astype(jnp.float32)
    grp_prob = jax.nn.softmax(grp_logits, axis=-1)
    grp = jnp.argmax(grp_prob, axis=-1).astype(jnp.int32)
    grp_w = jnp.max(grp_prob, axis=-1)
    exp_logits = ((xt @ w_router).astype(jnp.float32) + b_router.astype(jnp.float32)).reshape(
        n, N_GROUPS, EXPERTS_PER_GROUP)
    in_grp = jnp.take_along_axis(exp_logits, grp[:, None, None], axis=1)[:, 0]
    top_val, top_idx = lax.top_k(in_grp, TOP_K_INNER)
    gate = grp_w[:, None] * jax.nn.softmax(top_val, axis=-1)
    expert = grp[:, None] * EXPERTS_PER_GROUP + top_idx.astype(jnp.int32)
    a = n * TOP_K_INNER
    e_flat = expert.reshape(a)
    tok = jnp.arange(a, dtype=jnp.int32) // TOP_K_INNER
    g_flat = gate.reshape(a).astype(xn.dtype)
    order = jnp.argsort(e_flat)
    e_sorted = e_flat[order]
    counts = jnp.bincount(e_flat, length=N_EXPERTS).astype(jnp.int32)
    starts = jnp.cumsum(counts) - counts
    padded = (counts + MOE_BLOCK - 1) // MOE_BLOCK * MOE_BLOCK
    pends = jnp.cumsum(padded)
    pstarts = pends - padded
    dest = pstarts[e_sorted] + jnp.arange(a, dtype=jnp.int32) - starts[e_sorted]
    n_blocks = -(-a // MOE_BLOCK) + N_EXPERTS
    rows = n_blocks * MOE_BLOCK
    row_tok = jnp.full((rows,), n, jnp.int32).at[dest].set(tok[order])
    row_gate = jnp.zeros((rows,), xn.dtype).at[dest].set(g_flat[order])
    block_start = jnp.arange(n_blocks, dtype=jnp.int32) * MOE_BLOCK
    block_expert = jnp.minimum(jnp.searchsorted(pends, block_start, side='right'),
                               N_EXPERTS - 1).astype(jnp.int32)
    x_pad = jnp.concatenate([xt, jnp.zeros((1, d), xt.dtype)], axis=0)

    def expert_block(args):
        tok_b, gate_b, e = args
        xb = x_pad[tok_b]
        hb = jax.nn.silu(xb @ w_gate_e[e]) * (xb @ w_up_e[e])
        return (hb @ w_down_e[e]) * gate_b[:, None]

    out = lax.map(expert_block, (row_tok.reshape(n_blocks, MOE_BLOCK),
                                 row_gate.reshape(n_blocks, MOE_BLOCK), block_expert))
    y = jnp.zeros((n + 1, d), xn.dtype).at[row_tok].add(out.reshape(rows, d))
    return y[:n].reshape(bsz, t, d)

def setup_inputs(seed: int = 0) -> dict:
    key = jax.random.key(seed)
    ks = jax.random.split(key, 32)
    f32 = jnp.float32

    def nrm(k, shape, scale):
        return jax.random.normal(k, shape, f32) * scale

    L = DEPTH
    return {
        'x_prompt': nrm(ks[0], (BATCH, SEQ, D_MODEL), 1.0),
        'x_sample': nrm(ks[1], (DEC_BATCH, DEC_SEQ, D_MODEL), 1.0),
        'state_pool': nrm(ks[2], (L, DEC_BATCH, POOL_HIST, W_POOL), 1.0),
        'state_conv': nrm(ks[3], (L, DEC_BATCH, CONV_HIST, W_CONV), 0.5),
        'mix_norm_g': 1.0 + nrm(ks[4], (L, D_MODEL), 0.05),
        'w_in': nrm(ks[5], (L, D_MODEL, IN_COLS), D_MODEL ** -0.5),
        'pool_w': nrm(ks[6], (L, N_POOL_GROUPS, POOL_GC, POOL_GC), POOL_GC ** -0.5),
        'pool_scale': 1.0 + nrm(ks[7], (L, W_POOL), 0.1),
        'sgu_norm_g': 1.0 + nrm(ks[8], (L, W_SGU), 0.05),
        'sgu_norm_b': nrm(ks[9], (L, W_SGU), 0.02),
        'sgu_w': nrm(ks[10], (L, SGU_HEADS, CHUNK, CHUNK), CHUNK ** -0.5),
        'sgu_b': 1.0 + nrm(ks[11], (L, SGU_HEADS, CHUNK), 0.1),
        'conv_w': nrm(ks[12], (L, CONV_WIDTH, W_CONV), CONV_WIDTH ** -0.5),
        'conv_b': nrm(ks[13], (L, W_CONV), 0.02),
        'conv_norm_g': 1.0 + nrm(ks[14], (L, W_CONV), 0.05),
        'conv_norm_b': nrm(ks[15], (L, W_CONV), 0.02),
        'w_branch_pool': nrm(ks[16], (L, W_POOL, D_MODEL), W_POOL ** -0.5),
        'w_branch_sgu': nrm(ks[17], (L, W_SGU, D_MODEL), W_SGU ** -0.5),
        'w_branch_conv': nrm(ks[18], (L, W_CONV, D_MODEL), W_CONV ** -0.5),
        'w_out': nrm(ks[19], (L, D_MODEL, D_MODEL), D_MODEL ** -0.5),
        'ffn_norm_g': 1.0 + nrm(ks[20], (L, D_MODEL), 0.05),
        'w_group': nrm(ks[21], (L, D_MODEL, N_GROUPS), D_MODEL ** -0.5),
        'b_group': nrm(ks[22], (L, N_GROUPS), 0.01),
        'w_router': nrm(ks[23], (L, D_MODEL, N_EXPERTS), D_MODEL ** -0.5),
        'b_router': nrm(ks[24], (L, N_EXPERTS), 0.01),
        'w_gate_e': nrm(ks[25], (L, N_EXPERTS, D_MODEL, D_EXPERT), D_MODEL ** -0.5),
        'w_up_e': nrm(ks[26], (L, N_EXPERTS, D_MODEL, D_EXPERT), D_MODEL ** -0.5),
        'w_down_e': nrm(ks[27], (L, N_EXPERTS, D_EXPERT, D_MODEL), D_EXPERT ** -0.5),
        'final_norm_g': 1.0 + nrm(ks[28], (D_MODEL,), 0.05),
    }

def reference(x_prompt, x_sample, state_pool, state_conv, mix_norm_g, w_in, pool_w, pool_scale,
              sgu_norm_g, sgu_norm_b, sgu_w, sgu_b, conv_w, conv_b, conv_norm_g, conv_norm_b,
              w_branch_pool, w_branch_sgu, w_branch_conv, w_out, ffn_norm_g, w_group, b_group,
              w_router, b_router, w_gate_e, w_up_e, w_down_e, final_norm_g):
    bp, tp, _ = x_prompt.shape
    bs, ts, _ = x_sample.shape
    pos_p = jnp.arange(tp, dtype=jnp.int32)
    pos_s = PAST_LEN + jnp.arange(ts, dtype=jnp.int32)
    pool_prev_p = jnp.zeros((bp, POOL_HIST, W_POOL), x_prompt.dtype)
    conv_prev_p = jnp.zeros((bp, CONV_HIST, W_CONV), x_prompt.dtype)
    xp, xs = x_prompt, x_sample
    pool_p, pool_s, conv_p, conv_s, chunk_v = [], [], [], [], []
    for l in range(DEPTH):
        mix_w = (w_in[l], pool_w[l], pool_scale[l], sgu_norm_g[l], sgu_norm_b[l], sgu_w[l], sgu_b[l],
                 conv_w[l], conv_b[l], conv_norm_g[l], conv_norm_b[l], w_branch_pool[l],
                 w_branch_sgu[l], w_branch_conv[l], w_out[l])
        moe_w = (w_group[l], b_group[l], w_router[l], b_router[l], w_gate_e[l], w_up_e[l], w_down_e[l])
        m, npool, nconv, _ = mixer_block(rms_norm(xp, mix_norm_g[l]), pool_prev_p, conv_prev_p, pos_p, *mix_w)
        xp = xp + m
        xp = xp + moe_ffn(rms_norm(xp, ffn_norm_g[l]), *moe_w)
        pool_p.append(npool)
        conv_p.append(nconv)
        m, npool, nconv, vn = mixer_block(rms_norm(xs, mix_norm_g[l]), state_pool[l], state_conv[l], pos_s, *mix_w)
        xs = xs + m
        xs = xs + moe_ffn(rms_norm(xs, ffn_norm_g[l]), *moe_w)
        pool_s.append(npool)
        conv_s.append(nconv)
        chunk_v.append(vn)
    y_prompt = rms_norm(xp, final_norm_g)
    y_sample = rms_norm(xs, final_norm_g)
    return (y_prompt, y_sample, jnp.stack(pool_p), jnp.stack(pool_s), jnp.stack(conv_p),
            jnp.stack(conv_s), jnp.stack(chunk_v))


_drawn_inputs = setup_inputs


def setup_inputs(seed=0):
    import zlib

    import numpy as np

    out = dict(_drawn_inputs(seed))
    spreads = {}
    factors = {'b_router': 4.28}
    for name, (base, spread) in spreads.items():
        noise = np.random.default_rng([zlib.crc32(name.encode()), seed]).standard_normal(out[name].shape)
        drawn = base * np.exp(spread * noise) if base else spread * noise
        out[name] = __import__('jax').numpy.asarray(drawn.astype(out[name].dtype))
    for name, factor in factors.items():
        out[name] = (out[name] * factor).astype(out[name].dtype)
    return out
```

```python
from contextlib import ExitStack

import concourse.bass as bass
import concourse.mybir as mybir
import numpy as np
from concourse.alu_op_type import AluOpType as ALU

F32 = mybir.dt.float32
F32R = mybir.dt.float32r
I32 = mybir.dt.int32
ACT = mybir.ActivationFunctionType
AX = mybir.AxisListType.X

P = 128
D = 1024
KD = D // P
W = 512
KW = W // P
SEQ = 512
NSEQ, STEP = 8, 4
NS = NSEQ * STEP
T = SEQ + NS
HT = T // 2
NCH = SEQ // P + 1
PH, CH = 15, 30
TAPS = 31
WINDOWS = (2, 4, 8, 16)
NG, EPG, NE = 4, 8, 32
DE = 512
CAP = 64
MAXB = T // CAP
NOVF = (2 * T - 1) // CAP
NBLK = NE + NOVF
EPS = 1e-6
OFF = 8192.0
PEXT = PH + SEQ + NSEQ * (PH + STEP)
CEXT = CH + SEQ + NSEQ * (CH + STEP)
IN_COLS = W * 5 + 3 * D


def chunk_rows(c):
    return P if c < NCH - 1 else NS


def _columns(parts):
    at, out = 0, {}
    for name, n in parts:
        out[name] = slice(at, at + n)
        at += n
    return out, at


CONST, NCONST = _columns([
    ("ident", P), ("causal", P), ("before", P), ("ones", P), ("blocks", NS),
    ("expert", NE), ("group_of", NE), ("group", NG), ("place", P), ("block", NBLK), ("token2", NCH),
    ("valid", NCH), ("half", 1), ("steps", MAXB), ("further", NOVF), ("count", NG * 16), ("pad", 1),
])


def shape_constants():
    c = np.zeros((P, NCONST), np.float32)
    p = np.arange(P)
    c[:, CONST["ident"]] = np.eye(P)
    c[:, CONST["causal"]] = p[:, None] <= p[None, :]
    c[:, CONST["before"]] = p[:, None] < p[None, :]
    c[:, CONST["ones"]] = 1
    s = np.arange(NS)
    c[:NS, CONST["blocks"]] = (s[:, None] // STEP == s[None, :] // STEP) & (s[:, None] <= s[None, :])
    c[:, CONST["expert"]] = np.arange(NE)
    c[:, CONST["group_of"]] = np.arange(NE) // EPG
    c[:, CONST["group"]] = np.arange(NG)
    c[:, CONST["place"]] = p % CAP
    c[:, CONST["block"]] = np.arange(NBLK)
    token = np.arange(NCH)[None, :] * P + p[:, None]
    c[:, CONST["token2"]] = 2 * token
    c[:, CONST["valid"]] = token < T
    c[:, CONST["half"]] = (p >= CAP)[:, None]
    c[:, CONST["steps"]] = CAP * np.arange(1, MAXB + 1)
    c[:, CONST["further"]] = np.arange(NOVF)
    for g, w in enumerate(WINDOWS):
        c[:, CONST["count"].start + 16 * g:][:, :16] = 1 / np.minimum(np.arange(16) + 1, w)
    return c


def build(nc, d, out):
    ctx = ExitStack()
    with ctx:
        program(nc, d, out, ctx)


def program(nc, d, out, ctx):
    def sb(name, shape, dt=F32):
        return ctx.enter_context(nc.sbuf_tensor(name, shape, dt))

    def next_place():
        return (nc.sbuf_base + 31) // 32 * 32

    def over(name, shape, dt, tensor_at, first=0):
        return nc.alloc_sbuf_tensor_at(name, shape, dt, offset=tensor_at + 4 * first)

    def sem(name):
        return ctx.enter_context(nc.semaphore(name))

    ctx.enter_context(nc.allow_non_contiguous_dma(reason="block-diagonal corner of the SGU weights"))

    gu0_at = next_place()
    gu0 = sb("gu0", [P, 2, KD, DE])
    ring = sb("ring", [P, 4 * D])
    slot1 = sb("slot1", [P, 12 * D])
    xx_at = next_place()
    xx = sb("xx", [P, 2 * KD * T])
    xh = sb("xh", [P, NCH * D])
    ybr = sb("ybr", [P, 3, KW, T])
    mid = sb("mid", [P, 4736])
    cst = sb("cst", [P, NCONST])
    bias_rows = sb("bias_rows", [P, KW, P])
    pool_w = sb("pool_w", [P, KW, P])
    param = sb("param", [P, 160])
    row_a = sb("row_a", [P, T])
    router = sb("router", [P, KD, NG + NE])
    router_b = sb("router_b", [P, NG + NE])
    stat = sb("stat", [P, 112])
    gate_of = sb("gate_of", [P, 2, NCH])
    gidx = sb("gidx", [P, NBLK], I32)
    sidx = sb("sidx", [P, NBLK], I32)
    idx_now = sb("idx_now", [P, 4], I32)
    ovf = sb("ovf", [P, NOVF + 1], I32)
    ps = ctx.enter_context(nc.psum_tensor("ps", [P, 8, 512], F32))

    w_high = [over(f"w_high{s}", [P, KD, 256], F32R, gu0_at, s * 2 * D) for s in range(2)]
    w_low = [over(f"w_low{s}", [P, KD, 256], F32R, gu0_at, (2 + s) * 2 * D) for s in range(2)]
    x_high = over("x_high", [P, KD, T], F32R, xx_at)
    x_low = over("x_low", [P, KD, T], F32R, xx_at, KD * T)

    wring = [ring[:, s * 2 * D:(s + 1) * 2 * D].rearrange("p (k n) -> p k n", k=KD) for s in range(2)]
    gu = [gu0[:], slot1[:, 0:8 * D].rearrange("p (m k f) -> p m k f", m=2, k=KD)]
    dn = [x.rearrange("p (k n) -> p k n", n=D) for x in (ring[:], slot1[:, 8 * D:12 * D])]
    proj = slot1[:, 0:16 * T].rearrange("p (q t) -> p q t", t=T)
    cext = slot1[:, 16 * T:16 * T + KW * CEXT].rearrange("p (q t) -> p q t", t=CEXT)
    step_w = slot1[0:NS, 16 * T + KW * CEXT:][:, 0:KW * NS].rearrange("p (h s) -> p h s", s=NS)
    states = slot1[:, KW * T:KW * T + 4 * W].rearrange("p (q t) -> p q t", t=W)
    x = xh[:].rearrange("p (c n) -> p c n", n=D)
    gates = xh[:, 0:6 * T].rearrange("p (q t) -> p q t", t=T)
    tmp = [xh[:, 6 * T + i * PEXT:][:, 0:PEXT] for i in range(2)]
    pool_hist = xh[:, 6 * T + 2 * PEXT:][:, 0:KW * NSEQ * PH].rearrange("p (q t) -> p q t", t=NSEQ * PH)
    xT = xx[:, 0:KD * T].rearrange("p (k t) -> p k t", t=T)
    late_rows = xx[:, KD * T:]
    ffn_row, final_row = (late_rows[:, i * D:(i + 1) * D] for i in range(2))
    pool_d = mid[:, 0:KW * T].rearrange("p (q t) -> p q t", t=T)
    vn = mid[:, KW * T:KW * T + NCH * W].rearrange("p (c n) -> p c n", n=W)
    merged = mid[:, 0:KD * T].rearrange("p (q t) -> p q t", t=T)
    conv_rows = mid[:, 0:2 * W].rearrange("p (a n) -> p a n", n=W)
    pool_rows = mid[:, 2 * W:3 * W]
    sgu_w_rows = mid[:, 3 * W:4 * W].rearrange("p (h s) -> p h s", s=P)
    param_rows = mid[:, 4 * W:4 * W + 2 * P].rearrange("p (a n) -> p a n", n=P)
    junk = mid[:, 4 * W + 2 * P:4 * W + 2 * P + D]
    ya, yb, yc = (ybr[:, n] for n in range(3))
    sgu_rows = ybr[:, 1].rearrange("p q t -> p (q t)")[:, 0:2 * W].rearrange("p (a n) -> p a n", n=W)
    wsT = ybr[:, 1, KW - 1, 0:KW * P].rearrange("p (h t) -> p h t", t=P)
    flat_y = ybr[:].rearrange("p a q t -> p (a q t)")
    xn2 = flat_y[:, 0:NCH * D].rearrange("p (c n) -> p c n", n=D)
    at = [0]

    def scratch(*shape):
        n = int(np.prod(shape))
        v = mid[:, at[0]:at[0] + n]
        at[0] += n
        assert at[0] <= 4736
        if len(shape) == 2:
            v = v.rearrange("p (a b) -> p a b", b=shape[1])
        return v

    flat_x = xx[:, 0:KD * T]
    xg = [flat_x[:, s * 512:(s + 1) * 512] for s in range(2)]
    yo = [flat_x[:, 1024 + s * 512:][:, 0:512] for s in range(2)]
    hid = [flat_x[:, 2048 + s * 256:][:, 0:256] for s in range(2)]
    hT = [flat_x[:, 2560 + s * 256:][:, 0:256].rearrange("p (c m) -> p c m", c=2) for s in range(2)]
    sig = [flat_x[:, 3072 + s * 256:][:, 0:256] for s in range(2)]
    xgT = [flat_y[:, 5120 + s * 512:][:, 0:512].rearrange("p (c m) -> p c m", c=4) for s in range(2)]

    const = {k: cst[:, v] for k, v in CONST.items()}
    ident = const["ident"]
    MG, PSC, CB, CG, CNB, TAP = 0, 8, 12, 16, 20, 24

    xn2_dram = nc.dram_tensor("xn2_rows", (T, D), F32, kind="Internal").ap()
    y_dram = nc.dram_tensor("expert_rows", (T * 2 * 2, W), F32, kind="Internal").ap()

    def slot(r):
        return ps[:, 2 * r:2 * r + 2, 0:HT]

    def slot_flat(r, n=T):
        return ps[:, 2 * r:2 * r + 2, :].rearrange("p b n -> p (b n)")[:, 0:n]

    def halves(v):
        return v.rearrange("p (b n) -> p b n", b=2)

    def y_place(c):
        if c < 4:
            return gu0[:].rearrange("p m k f -> p (m k f)")[:, c * 2 * D:(c + 1) * 2 * D]
        return slot1[:, 0:2 * D]

    def halves_at(t, q):
        return t[:, bass.ds(q, 1)].rearrange("p a (b n) -> p (a b) n", b=2)

    logits = scratch(NCH, NG + NE)
    group_exp = scratch(NCH, NG)
    cand = scratch(NCH, NE)
    masked = scratch(NCH, NE)
    one_hot = [scratch(NCH, NE) for _ in range(2)]
    chosen_mask = scratch(NCH, NE)
    rank = scratch(NCH, NE)
    before_chunk = scratch(NCH + 1, NE)
    small = scratch(40, NCH)
    pair_exp = small[:, 0]
    at_place = [scratch(NCH, P) for _ in range(2)]
    in_block = [late_rows[:, 2 * D + i * NCH * 2 * NBLK:][:, 0:NCH * 2 * NBLK].rearrange("p (c n) -> p c n", c=NCH)
                for i in range(2)]
    junk_h = bias_rows[:].rearrange("p h t -> p (h t)")
    further = scratch(4, NE)
    compare = scratch(NE, MAXB)
    compare_e = scratch(NOVF, NE)
    at_further = scratch(1, NOVF)[:, 0]
    cand_b = scratch(NCH, NBLK)
    by_step = scratch(NCH, MAXB)

    x_loaded = sem("x_loaded")
    const_loaded = sem("const_loaded")
    param_loaded = sem("param_loaded")
    rows_loaded = sem("rows_loaded")
    late_loaded = sem("late_loaded")
    norm_rows_loaded = sem("norm_rows_loaded")
    high_ready = sem("high_ready")
    low_ready = sem("low_ready")
    step_loaded = sem("step_loaded")
    zeroed = sem("zeroed")
    wring_loaded = [sem(f"wring_loaded{s}") for s in range(2)]
    half_rows = sem("half_rows")
    product = sem("product")
    act_took = sem("act_took")
    dve_took = sem("dve_took")
    act_step = sem("act_step")
    dve_step = sem("dve_step")
    pool_step = sem("pool_step")
    mean_sq = sem("mean_sq")
    root = sem("root")
    root_in = sem("root_in")
    x_normed = sem("x_normed")
    glu_gate = sem("glu_gate")
    glu_done = sem("glu_done")
    conv_done = sem("conv_done")
    pool_done = sem("pool_done")
    v_normed = sem("v_normed")
    sgu_done = sem("sgu_done")
    centred = sem("centred")
    squared = sem("squared")
    swish_in = sem("swish_in")
    swish_sig = sem("swish_sig")
    yc_done = sem("yc_done")
    merged_done = sem("merged_done")
    x_again = sem("x_again")
    merged_part = sem("merged_part")
    xn2_done = sem("xn2_done")
    xn2_stored = sem("xn2_stored")
    logits_in = sem("logits_in")
    exp_in = sem("exp_in")
    exp_done = sem("exp_done")
    chosen = sem("chosen")
    tables_in = sem("tables_in")
    routed = sem("routed")
    states_stored = sem("states_stored")
    outs_stored = sem("outs_stored")
    gu_loaded = [sem(f"gu_loaded{s}") for s in range(2)]
    dn_loaded = [sem(f"dn_loaded{s}") for s in range(2)]
    xg_loaded = [sem(f"xg_loaded{s}") for s in range(2)]
    waits_met = sem("waits_met")
    scattered = [sem(f"scattered{s}") for s in range(2)]
    xg_turned = sem("xg_turned")
    xgT_ready = sem("xgT_ready")
    gu_done = sem("gu_done")
    sig_ready = sem("sig_ready")
    hid_ready = sem("hid_ready")
    hid_turned = sem("hid_turned")
    hT_ready = sem("hT_ready")
    dn_done = sem("dn_done")
    yo_ready = sem("yo_ready")
    gather_idx = [sem(f"gather_idx{s}") for s in range(2)]
    scatter_idx = [sem(f"scatter_idx{s}") for s in range(2)]
    y_loaded = [sem(f"y_loaded{c}") for c in range(NCH)]
    summed = sem("summed")
    final_sq = sem("final_sq")
    final_in = sem("final_in")
    final_root = sem("final_root")
    final_done = sem("final_done")

    block = ctx.enter_context(nc.Block())

    N_SETUP = 12
    A_SETUP, D_SETUP = KD + 2, KD + 2
    N_PROJ, A_PROJ = N_SETUP + 16, A_SETUP + 16
    N_V, A_V = N_PROJ + NCH, A_PROJ + NCH
    N_G0, A_G0 = N_V + 6, A_V + 6
    N_SPAT = 7
    N_S, A_S, D_S = N_G0 + N_SPAT + 6, A_G0 + 6, D_SETUP + N_SPAT
    NJ = D // (2 * P)
    N_B, A_B, D_B = N_S + 12 * NJ - 6, A_S + 6 * (NJ - 1), D_S + 6 * NJ
    N_O, D_O = N_B + 2 * NCH, D_B + 2 * NCH
    N_T, A_T, D_T = N_O + KD, A_B + KD // 2, D_O + KD // 2
    N_L, D_L = N_T + 1, D_T + 1

    w_in = d["w_in"][0]
    proj_cols = [3 * W, 3 * W + 256, 4 * W, 4 * W + 256, 0, 256, W, W + 256, 2 * W, 2 * W + 256]

    def gate_pairs(j):
        return [w_in[:, 5 * W + n * D + j * 256:][:, 0:256] for n in range(3)]

    def branch_pairs(j):
        return [d[b][0][:, j * 256:(j + 1) * 256] for b in ("w_branch_pool", "w_branch_sgu", "w_branch_conv")]

    pairs = [w_in[:, c:c + 256] for c in proj_cols] + gate_pairs(0)
    for j in range(NJ):
        pairs += branch_pairs(j) + (gate_pairs(j + 1) if j + 1 < NJ else [])
    pairs += [d["w_out"][0][:, j * 256:(j + 1) * 256] for j in range(4)]
    FIRST_G0, FIRST_B0 = 10, 13
    FIRST_OUT = len(pairs) - 4
    assert FIRST_B0 % 2 == 1 and FIRST_OUT % 2 == 0

    def is_split(n):
        return n < FIRST_B0 or n < FIRST_OUT and (n - FIRST_B0) % 6 >= 3

    def pair_free(n):
        if is_split(n):
            return low_ready, sum(is_split(i) for i in range(n + 1))
        if n < FIRST_OUT:
            return product, N_S + 2 * (n - FIRST_B0 + 1)
        if (n - FIRST_OUT) % 2 == 0:
            return half_rows, (n - FIRST_OUT) // 2 + 2
        return product, N_B + NCH * ((n - FIRST_OUT) // 2 + 1)

    def expert_gu(m, e):
        w = d["w_gate_e" if m == 0 else "w_up_e"][0]
        return w[bass.ds(e, 1)].rearrange("e (h p c) f -> p (e h) (c f)", h=2, c=4)

    def expert_dn(e):
        return d["w_down_e"][0][bass.ds(e, 1)].rearrange("e (h p c) n -> p (e h) (c n)", h=2, c=2)

    @block.sync
    def _(sp):
        sp.dma_start(x[:, 0:4], d["x_prompt"][0].rearrange("(c p) n -> p c n", p=P)).then_inc(x_loaded, 16)
        sp.dma_start(x[0:NS, 4], d["x_sample"].rearrange("b i n -> (b i) n")).then_inc(x_loaded, 16)
        sp.dma_start(cst[:], d["shape_constants"]).then_inc(const_loaded, 16)
        sp.dma_start(param_rows[0:124, 0], d["conv_w"][0].rearrange("k (q c) -> (k q) c", c=P)).then_inc(param_loaded, 16)
        for first, name in ((MG, "mix_norm_g"), (PSC, "pool_scale"), (CB, "conv_b"), (CG, "conv_norm_g"), (CNB, "conv_norm_b")):
            rows = d[name][0].rearrange("(k c) -> k c", c=P)
            sp.dma_start(param_rows[first:first + rows.shape[0], 1], rows).then_inc(param_loaded, 16)
        for n in range(2):
            sp.dma_start(wring[n], pairs[n].rearrange("(k p) n -> p k n", p=P)).then_inc(wring_loaded[n], 16)
        for a in range(2):
            sp.dma_start(conv_rows[0:120, a], d["state_conv"][0][4 * a:4 * a + 4].rearrange("b i c -> (b i) c")).then_inc(rows_loaded, 16)
        sp.dma_start(pool_rows[0:120], d["state_pool"][0].rearrange("b i c -> (b i) c")).then_inc(rows_loaded, 16)
        sp.dma_start(sgu_w_rows, d["sgu_w"][0].rearrange("h t s -> t h s")).then_inc(rows_loaded, 16)
        sp.wait_ge(zeroed, 1)
        for b in range(NSEQ):
            for h in range(KW):
                sp.dma_start(step_w[b * STEP:(b + 1) * STEP, h, b * STEP:(b + 1) * STEP],
                             d["sgu_w"][0][h, 0:STEP, 0:STEP].rearrange("t s -> s t")).then_inc(step_loaded, 16)
        late = [
            (pool_w[:], d["pool_w"][0].rearrange("g c n -> c g n")),
            (sgu_rows[:, 0], d["sgu_norm_g"][0].partition_broadcast(P)),
            (sgu_rows[:, 1], d["sgu_norm_b"][0].partition_broadcast(P)),
            (bias_rows[:], d["sgu_b"][0].partition_broadcast(P)),
            (router[:, :, 0:NG], d["w_group"][0].rearrange("(k p) n -> p k n", p=P)),
            (router[:, :, NG:], d["w_router"][0].rearrange("(k p) n -> p k n", p=P)),
            (router_b[:, 0:NG], d["b_group"][0].partition_broadcast(P)),
            (router_b[:, NG:], d["b_router"][0].partition_broadcast(P)),
        ]
        for dst, src in late:
            sp.dma_start(dst, src).then_inc(late_loaded, 16)
        sp.dma_start(out["pool_sample"][0][:, 0:PH - STEP], d["state_pool"][0][:, STEP:PH]).then_inc(states_stored, 16)
        sp.dma_start(out["conv_sample"][0][:, 0:CH - STEP], d["state_conv"][0][:, STEP:CH]).then_inc(states_stored, 16)
        for n in range(2, len(pairs)):
            if n == FIRST_B0 + 3:
                sp.wait_ge(act_took, A_S)
                sp.dma_start(out["pool_prompt"][0][0], states[0:PH, 0]).then_inc(states_stored, 16)
                sp.dma_start(out["conv_prompt"][0][0], states[0:CH, 2]).then_inc(states_stored, 16)
                for b in range(NSEQ):
                    r = slice(b * STEP, (b + 1) * STEP)
                    sp.dma_start(out["pool_sample"][0][b, PH - STEP:PH], states[r, 1]).then_inc(states_stored, 16)
                    sp.dma_start(out["conv_sample"][0][b, CH - STEP:CH], states[r, 3]).then_inc(states_stored, 16)
            if n == FIRST_B0:
                sp.wait_ge(v_normed, NCH)
                sp.dma_start(out["chunk_v_sample"][0].rearrange("b i c -> (b i) c"), vn[0:NS, NCH - 1]).then_inc(outs_stored, 16)
            if n == FIRST_B0 + 9:
                sp.wait_ge(states_stored, 16 * (4 + 2 * NSEQ))
                sp.wait_ge(dve_took, D_S)
                sp.wait_ge(sgu_done, 2 * KW)
            if n in (FIRST_B0 + 9, FIRST_B0 + 10):
                m = n - FIRST_B0 - 9
                sp.dma_start(gu[1][:, m].rearrange("p (h c) f -> p h (c f)", h=2), expert_gu(m, 1)).then_inc(gu_loaded[1], 16)
            if n == FIRST_B0 + 11:
                sp.dma_start(dn[1].rearrange("p (h c) n -> p h (c n)", h=2), expert_dn(1)).then_inc(dn_loaded[1], 16)
            if n == FIRST_OUT - 1:
                sp.wait_ge(product, N_B - 6)
                sp.dma_start(ffn_row, d["ffn_norm_g"][0].partition_broadcast(P)).then_inc(norm_rows_loaded, 16)
                sp.dma_start(final_row, d["final_norm_g"].partition_broadcast(P)).then_inc(norm_rows_loaded, 16)
            if n in (FIRST_OUT, FIRST_OUT + 1):
                m = n - FIRST_OUT
                sp.dma_start(gu[0][:, m].rearrange("p (h c) f -> p h (c f)", h=2), expert_gu(m, 0)).then_inc(gu_loaded[0], 16)
            if n == FIRST_OUT + 2:
                sp.wait_ge(merged_done, 2 * NJ)
                sp.dma_start(x[:, 0:4], d["x_prompt"][0].rearrange("(c p) n -> p c n", p=P)).then_inc(x_again, 16)
                sp.dma_start(x[0:NS, 4], d["x_sample"].rearrange("b i n -> (b i) n")).then_inc(x_again, 16)
            sp.wait_ge(*pair_free(n - 2))
            rows = pairs[n].rearrange("(k p) n -> p k n", p=P)
            sp.dma_start(wring[n % 2][:, 0:rows.shape[1]], rows).then_inc(wring_loaded[n % 2], 16)
        sp.wait_ge(product, N_O)
        sp.dma_start(dn[0].rearrange("p (h c) n -> p h (c n)", h=2), expert_dn(0)).then_inc(dn_loaded[0], 16)
        for c in range(NCH):
            sp.wait_ge(xn2_done, c + 1)
            n = chunk_rows(c)
            sp.dma_start(xn2_dram[c * P:c * P + n], xn2[0:n, c]).then_inc(xn2_stored, 16)

        def load_expert(e, s, after):
            sp.wait_ge(gu_done, after)
            for m in range(2):
                sp.dma_start(gu[s][:, m].rearrange("p (h c) f -> p h (c f)", h=2), expert_gu(m, e)).then_inc(gu_loaded[s], 16)
            sp.wait_ge(dn_done, after)
            sp.dma_start(dn[s].rearrange("p (h c) n -> p h (c n)", h=2), expert_dn(e)).then_inc(dn_loaded[s], 16)

        with sp.Fori(1, NE // 2) as i:
            for s in range(2):
                load_expert(2 * i + s, s, 2 * i + s - 1)
        sp.wait_ge(routed, 1)
        n_over = sp.value_load(ovf[0:1, NOVF:NOVF + 1], min_val=0, max_val=NOVF)
        with sp.Fori(0, NOVF) as j:
            with sp.If(n_over > j):
                e = sp.value_load(ovf[0:1, bass.ds(j, 1)], min_val=0, max_val=NE - 1)
                load_expert(e, 0, NE + j)
        sp.wait_ge(gu_done, n_over + NE)
        sp.wait_ge(dn_done, n_over + NE)
        sp.wait_ge(scattered[0], n_over * 16 + 16 * (NE // 2))
        sp.wait_ge(scattered[1], 16 * (NE // 2))
        y_rows = y_dram.rearrange("(t f) n -> t (f n)", f=4)
        for c in range(NCH):
            n = chunk_rows(c)
            sp.dma_start(y_place(c)[0:n], y_rows[c * P:c * P + n]).then_inc(y_loaded[c], 16)
        for c in range(NCH):
            sp.wait_ge(final_done, c + 1)
            n = chunk_rows(c)
            dst = out["y_prompt"][0][c * P:(c + 1) * P] if c < NCH - 1 else out["y_sample"].rearrange("b i n -> (b i) n")
            sp.dma_start(dst, x[0:n, c]).then_inc(outs_stored, 16)
        sp.wait_ge(outs_stored, 16 * (1 + NCH))
        sp.wait_ge(states_stored, 16 * (4 + 2 * NSEQ))

    @block.tensor
    def _(pe):
        pe.wait_ge(const_loaded, 16)
        pe.wait_ge(param_loaded, 16 * 6)
        pe.transpose(ps[:, 6, 0:124], param_rows[0:124, 0], ident[0:124, 0:124])
        pe.transpose(ps[:, 6, 124:148], param_rows[0:24, 1], ident[0:24, 0:24]).then_inc(product, 1)
        for k in range(KD):
            if k == 0:
                pe.wait_ge(x_normed, NCH)
            if k == 3:
                pe.wait_ge(act_took, 1)
            if k >= 4:
                pe.wait_ge(dve_took, k - 3)
            for c in range(NCH):
                n = chunk_rows(c)
                last = pe.transpose(ps[:, 2 * (k % 4) + c // 4, (c % 4) * P:(c % 4) * P + n],
                                    x[0:n, c, k * P:(k + 1) * P], ident[0:n, 0:n])
            last.then_inc(product, 1)
        pe.wait_ge(rows_loaded, 16 * 4)
        pe.wait_ge(dve_took, 5)
        for q in range(KW):
            for a in range(2):
                last = pe.transpose(ps[:, q // 2, (q % 2) * 240 + a * 120:][:, 0:120],
                                    conv_rows[0:120, a, q * P:(q + 1) * P], ident[0:120, 0:120])
        last.then_inc(product, 1)
        pe.wait_ge(dve_took, 6)
        for q in range(KW):
            last = pe.transpose(ps[:, 2, q * 120:(q + 1) * 120], pool_rows[0:120, q * P:(q + 1) * P], ident[0:120, 0:120])
        last.then_inc(product, 1)
        pe.wait_ge(dve_took, 7)
        for h in range(KW):
            last = pe.transpose(ps[:, 4, h * P:(h + 1) * P], sgu_w_rows[:, h], ident)
        last.then_inc(product, 1)

        def column_tiles(w, rhs, kt, r, c):
            for half in range(2):
                for k in range(kt):
                    last = pe.matmul(ps[:, 2 * r + half, 0:HT], w[:, k, c * P:(c + 1) * P],
                                     rhs[:, k, half * HT:(half + 1) * HT], start=(k == 0), stop=(k == kt - 1))
            return last

        def split_tiles(s, r, c):
            for k in range(KD):
                for w, xs in ((w_high[s], (x_high, x_low)), (w_low[s], (x_high,))):
                    for half in range(2):
                        for rhs in xs:
                            last = pe.matmul(ps[:, 2 * r + half, 0:HT], w[:, k, c * P:(c + 1) * P],
                                             rhs[:, k, half * HT:(half + 1) * HT], start=(k == 0 and w is w_high[s] and rhs is x_high),
                                             stop=(k == KD - 1 and w is w_low[s]))
            return last

        pe.wait_ge(act_took, A_SETUP)
        pe.wait_ge(dve_took, D_SETUP)
        with pe.Fori(0, 4) as i:
            for s in range(2):
                pe.wait_ge(low_ready, i * 2 + (s + 1))
                for c in range(2):
                    r = 2 * s + c
                    pe.wait_ge(act_took, i * 4 + (A_SETUP - 3 + r))
                    last = split_tiles(s, r, c)
                    last.then_inc(product, 1)

        def token_chunks(lhs, w, s):
            for c in range(NCH):
                n = chunk_rows(c)
                for k in range(KD):
                    last = pe.matmul(ps[0:n, c, s * 256:(s + 1) * 256], lhs[:, k, c * P:c * P + n], w[:, k],
                                     start=(k == 0), stop=(k == KD - 1))
                if s == 1:
                    last.then_inc(product, 1)
            if s == 0:
                last.then_inc(half_rows, 1)

        pe.wait_ge(act_took, A_PROJ)
        for s in range(2):
            pe.wait_ge(low_ready, 8 + s + 1)
            for c in range(NCH):
                n = chunk_rows(c)
                parts = [(k, xs, w) for k in range(KD)
                         for xs, w in ((x_high, w_high[s]), (x_high, w_low[s]), (x_low, w_high[s]))]
                for i, (k, xs, w) in enumerate(parts):
                    last = pe.matmul(ps[0:n, c, s * 256:(s + 1) * 256], xs[:, k, c * P:c * P + n], w[:, k],
                                     start=(i == 0), stop=(i == len(parts) - 1))
                if s == 1:
                    last.then_inc(product, 1)
            if s == 0:
                last.then_inc(half_rows, 1)

        pe.wait_ge(act_took, A_V)
        for g in range(6):
            s = (FIRST_G0 + g // 2) % 2
            if g % 2 == 0:
                pe.wait_ge(low_ready, FIRST_G0 + g // 2 + 1)
            if g >= 4:
                pe.wait_ge(act_took, A_V + g - 3)
            last = split_tiles(s, (g + 1) % 4, g % 2)
            last.then_inc(product, 1)

        pe.wait_ge(act_took, A_G0)
        pe.wait_ge(v_normed, NCH)
        pe.wait_ge(step_loaded, 16 * NSEQ * KW)
        for h in range(KW):
            for c in range(NCH - 1):
                last = pe.matmul(ps[:, 2 * ((h + 3) % 4), c * P:(c + 1) * P], vn[:, c, h * P:(h + 1) * P], wsT[:, h],
                                 start=True, stop=True)
            last.then_inc(product, 1)
        pe.wait_ge(dve_took, D_SETUP + 1)
        for h in range(KW):
            last = pe.matmul(ps[:, 6, h * NS:(h + 1) * NS], vn[0:NS, NCH - 1, h * P:(h + 1) * P], step_w[:, h],
                             start=True, stop=True)
        last.then_inc(product, 1)
        pe.wait_ge(conv_done, 1)
        pe.wait_ge(dve_took, D_SETUP + 2)
        for half in range(2):
            for q in range(KW):
                last = pe.matmul(ps[:, half, 0:HT], const["ones"], yc[:, q, half * HT:(half + 1) * HT],
                                 start=(q == 0), stop=(q == KW - 1))
        last.then_inc(product, 1)
        pe.wait_ge(squared, KW)
        pe.wait_ge(dve_took, D_SETUP + 3)
        for half in range(2):
            for q in range(KW):
                last = pe.matmul(ps[:, 2 + half, 0:HT], const["ones"], ya[:, q, half * HT:(half + 1) * HT],
                                 start=(q == 0), stop=(q == KW - 1))
        last.then_inc(product, 1)
        pe.wait_ge(pool_done, KW)
        pe.wait_ge(late_loaded, 16 * 8)
        for g in range(KW):
            r = (7 + g + 3) % 4
            pe.wait_ge(dve_took, D_SETUP + min(4 + g, 7))
            for half in range(2):
                last = pe.matmul(ps[:, 2 * r + half, 0:HT], pool_w[:, g], pool_d[:, g, half * HT:(half + 1) * HT],
                                 start=True, stop=True)
            last.then_inc(product, 1)
        for n, (rows, prompt, sample) in enumerate([
            (PH, lambda q: proj[:, 8 + q, SEQ - PH:SEQ], lambda q: proj[:, 8 + q, SEQ:T]),
            (CH, lambda q: cext[:, q, SEQ:SEQ + CH],
             lambda q: proj[:, q, SEQ:T]),
        ]):
            pe.wait_ge(act_took, A_G0 + 1 + n)
            for q in range(KW):
                pe.transpose(ps[0:rows, 2 * (2 + n), q * P:(q + 1) * P], prompt(q), ident)
                last = pe.transpose(ps[0:NS, 2 * (2 + n) + 1, q * P:(q + 1) * P], sample(q), ident)
            last.then_inc(product, 1)

        def branches(i, first_pair):
            for b in range(6):
                s = (FIRST_B0 + b // 2) % 2
                if b % 2 == 0:
                    pe.wait_ge(wring_loaded[s], first_pair * 8 + 16 * ((FIRST_B0 + b // 2) // 2 + 1))
                if b == 4:
                    pe.wait_ge(yc_done, KW)
                if b < 4:
                    pe.wait_ge(act_took, i * 6 + (A_S - 3 + b))
                else:
                    pe.wait_ge(dve_took, i * 6 + (D_S + b - 3))
                last = column_tiles(wring[s], (ya, yb, yc)[b // 2], KW, b % 4, b % 2)
                last.then_inc(product, 1)

        def gates_of_next(i):
            for g in range(6):
                s = (FIRST_B0 + 3 + g // 2) % 2
                if g % 2 == 0:
                    pe.wait_ge(low_ready, i * 3 + (FIRST_B0 + g // 2 + 1))
                if g < 4:
                    pe.wait_ge(dve_took, i * 6 + (D_S + 3 + g))
                else:
                    pe.wait_ge(act_took, i * 6 + (A_S + g - 3))
                last = split_tiles(s, (g + 2) % 4, g % 2)
                last.then_inc(product, 1)

        pe.wait_ge(act_took, A_G0 + 4)
        pe.wait_ge(sgu_done, 2 * KW)
        with pe.Fori(0, NJ - 1) as i:
            branches(i, i * 6)
            gates_of_next(i)
        branches(NJ - 1, (NJ - 1) * 6)

        pe.wait_ge(merged_done, 2 * NJ)
        pe.wait_ge(dve_took, D_B)
        with pe.Fori(0, 2) as i:
            for s in range(2):
                pe.wait_ge(wring_loaded[s], i * 16 + 16 * (FIRST_OUT // 2 + 1))
                if s == 0:
                    pe.wait_ge(dve_took, i * NCH + D_B)
                token_chunks(merged, wring[s], s)

        pe.wait_ge(dve_took, D_O)
        pe.wait_ge(xn2_done, NCH)
        for k in range(KD):
            if k >= 4:
                pe.wait_ge(*((act_took, A_B + (k - 4) // 2 + 1) if k % 2 == 0 else (dve_took, D_O + (k - 4) // 2 + 1)))
            for c in range(NCH):
                n = chunk_rows(c)
                last = pe.transpose(ps[:, 2 * (k % 4) + c // 4, (c % 4) * P:(c % 4) * P + n],
                                    xn2[0:n, c, k * P:(k + 1) * P], ident[0:n, 0:n])
            last.then_inc(product, 1)
        pe.wait_ge(act_took, A_T)
        pe.wait_ge(dve_took, D_T)
        for c in range(NCH):
            n = chunk_rows(c)
            for k in range(KD):
                last = pe.matmul(ps[0:n, 0, c * (NG + NE):(c + 1) * (NG + NE)], xT[:, k, c * P:c * P + n],
                                 router[:, k], start=(k == 0), stop=(k == KD - 1))
        last.then_inc(product, 1)
        pe.wait_ge(chosen, 1)
        pe.matmul(ps[:, 2, 0:NCH * NE], const["before"], chosen_mask.rearrange("p c e -> p (c e)"), start=True, stop=True)
        pe.matmul(ps[:, 3, 0:NCH * NE], const["ones"], chosen_mask.rearrange("p c e -> p (c e)"),
                  start=True, stop=True).then_inc(product, 1)
        pe.wait_ge(tables_in, 2)
        for n, (pl, bl) in enumerate((at_place[k], in_block[k]) for k in range(2)):
            for c in range(NCH):
                last = pe.matmul(ps[:, 4, 0:2 * NBLK], pl[:, c], bl[:, c], start=(n == 0 and c == 0),
                                 stop=(n == 1 and c == NCH - 1))
        last.then_inc(product, 1)

        def turn_rows(e, s, turn, free):
            pe.wait_ge(xg_loaded[s], turn * 16 + 16)
            if free is not None:
                pe.wait_ge(xgT_ready, free)
            v = xg[s].rearrange("p (m c) -> p m c", c=4)
            for c in range(4):
                last = pe.transpose(ps[:, s, c * P:(c + 1) * P], v[:, :, c], ident)
            last.then_inc(xg_turned, 1)

        def gate_up(e, s, turn, free):
            pe.wait_ge(xgT_ready, e + 1)
            pe.wait_ge(gu_loaded[s], turn * 32 + 32)
            if free is not None:
                pe.wait_ge(hid_ready, free)
            for k in range(KD):
                for g in range(2):
                    last = pe.matmul(ps[g * CAP:(g + 1) * CAP, 2 + s].rearrange("p (m f) -> p m f", m=2),
                                     xgT[s][:, k % 4, (k // 4) * CAP:(k // 4 + 1) * CAP],
                                     gu[s][:, :, k, g * 256:(g + 1) * 256], start=(k == 0), stop=(k == KD - 1))
            last.then_inc(gu_done, 1)

        def turn_hidden(e, s, turn, free):
            pe.wait_ge(hid_ready, e + 1)
            if free is not None:
                pe.wait_ge(hT_ready, free)
            v = hid[s].rearrange("p (m c) -> p m c", c=2)
            for c in range(2):
                last = pe.transpose(ps[:, 4 + s, c * P:(c + 1) * P], v[:, :, c], ident)
            last.then_inc(hid_turned, 1)

        def down(e, s, turn, free):
            pe.wait_ge(hT_ready, e + 1)
            pe.wait_ge(dn_loaded[s], turn * 16 + 16)
            if free is not None:
                pe.wait_ge(yo_ready, free)
            for k in range(4):
                for g in range(2):
                    last = pe.matmul(ps[g * CAP:(g + 1) * CAP, 6 + s], hT[s][:, k % 2, (k // 2) * CAP:(k // 2 + 1) * CAP],
                                     dn[s][:, k, g * W:(g + 1) * W], start=(k == 0), stop=(k == 3))
            last.then_inc(dn_done, 1)

        pe.wait_ge(routed, 1)
        turn_rows(0, 0, 0, None)
        for e in range(2):
            gate_up(e, e, 0, None)
            turn_rows(e + 1, 1 - e, e, None if e == 0 else 1)
            turn_hidden(e, e, 0, None)
            down(e, e, 0, None)
        with pe.Fori(1, NE // 2 - 1) as i:
            for s in range(2):
                e, free = 2 * i + s, 2 * i + s - 1
                gate_up(e, s, i, free)
                turn_rows(e + 1, 1 - s, i + s, free + 1)
                turn_hidden(e, s, i, free)
                down(e, s, i, free)
        i = NE // 2 - 1
        for s in range(2):
            e, free = 2 * i + s, 2 * i + s - 1
            gate_up(e, s, i, free)
            if s == 0:
                turn_rows(e + 1, 1, i, free + 1)
            turn_hidden(e, s, i, free)
            down(e, s, i, free)
        n_over = pe.value_load(ovf[0:1, NOVF:NOVF + 1], min_val=0, max_val=NOVF)
        with pe.Fori(0, NOVF) as j:
            with pe.If(n_over > j):
                for stage in (turn_rows, gate_up, turn_hidden, down):
                    stage(NE + j, 0, NE // 2 + j, NE + j)

    @block.scalar
    def _(act):
        n_own = [0]

        def own(instruction):
            n_own[0] += 1
            instruction.then_inc(act_step, 1)
            act.wait_ge(act_step, n_own[0])

        def high_part(s, turn):
            act.wait_ge(wring_loaded[s], turn * 16 + 16)
            nc.scalar.copy(w_high[s][:], wring[s]).then_inc(high_ready, 1)

        act.wait_ge(x_loaded, 32)
        act.wait_ge(zeroed, 2)
        for c in range(NCH):
            n = chunk_rows(c)
            own(nc.scalar.activation(junk[0:n], x[0:n, c], ACT.Square, accum_out=stat[0:n, c:c + 1]))
        nc.scalar.copy(stat[:, 10:10 + NCH], stat[:, 0:NCH]).then_inc(mean_sq, 1)
        act.wait_ge(root_in, 1)
        nc.scalar.activation(stat[:, 5:5 + NCH], stat[:, 0:NCH], ACT.Sqrt).then_inc(root, 1)
        high_part(0, 0)
        high_part(1, 0)
        act.wait_ge(product, 1)
        nc.scalar.copy(param[:, TAP:TAP + 124], ps[:, 6, 0:124])
        nc.scalar.copy(param[:, 0:24], ps[:, 6, 124:148]).then_inc(act_took, 1)
        act.wait_ge(act_took, 1)
        for k in range(KD):
            act.wait_ge(product, 2 + k)
            nc.scalar.activation(x_high[:, k], slot_flat(k % 4), ACT.Identity, scale=param[:, MG + k:MG + k + 1]).then_inc(act_took, 1)
        act.wait_ge(product, 10)
        for q in range(KW):
            last = nc.scalar.copy(
                cext[:, q, CH + SEQ:].rearrange("p (b i) -> p b i", i=CH + STEP)[:, :, 0:CH],
                ps[:, q // 2, (q % 2) * 240:(q % 2) * 240 + 240].rearrange("p (b i) -> p b i", i=CH))
        last.then_inc(act_took, 1)

        def take_projections(lo, hi):
            with act.Fori(lo, hi) as i:
                for r in range(4):
                    act.wait_ge(product, i * 4 + (N_SETUP + r + 1))
                    nc.scalar.copy(halves_at(proj, i * 4 + r), slot(r)).then_inc(act_took, 1)
                    if r % 2 == 1:
                        high_part(r // 2, i + 1)

        take_projections(0, 2)
        act.wait_ge(act_took, A_SETUP + 8)
        for q in range(KW):
            nc.scalar.activation(proj[:, KW + q], proj[:, KW + q], ACT.Sigmoid).then_inc(glu_gate, 1)
        take_projections(2, 4)
        act.wait_ge(half_rows, 1)
        high_part(0, 5)
        for c in range(NCH):
            n = chunk_rows(c)
            act.wait_ge(product, N_PROJ + c + 1)
            nc.scalar.copy(vn[0:n, c], ps[0:n, c]).then_inc(act_took, 1)

        high_part(1, 5)

        def take_gate(g, r):
            return nc.scalar.activation(halves(gates[:, g]), slot(r), ACT.Sigmoid).then_inc(act_took, 1)

        for g in range(6):
            act.wait_ge(product, N_V + g + 1)
            take_gate(g, (g + 1) % 4)
            if g == 1:
                high_part(0, 6)
            if g == 2:
                act.wait_ge(root_in, 2)
                nc.scalar.activation(stat[:, 20:20 + NCH], stat[:, 15:15 + NCH], ACT.Sqrt).then_inc(root, 1)
        for q in range(KW):
            act.wait_ge(*((centred, q + 1) if q < KW - 1 else (dve_took, D_S - 1)))
            nc.scalar.activation(ya[:, q], yc[:, q], ACT.Square).then_inc(squared, 1)
        act.wait_ge(dve_took, D_S)
        nc.scalar.activation(row_a[:], row_a[:], ACT.Sqrt).then_inc(root, 1)
        for g in range(KW):
            act.wait_ge(product, N_G0 + N_SPAT + g + 1)
            nc.scalar.activation(halves(ya[:, g]), slot((7 + g + 3) % 4), ACT.Identity,
                                 scale=param[:, PSC + g:PSC + g + 1]).then_inc(act_took, 1)
        for n, rows in enumerate((PH, CH)):
            act.wait_ge(product, N_G0 + N_SPAT + KW + n + 1)
            nc.scalar.copy(states[0:rows, 2 * n], ps[0:rows, 2 * (2 + n)])
            nc.scalar.copy(states[0:NS, 2 * n + 1], ps[0:NS, 2 * (2 + n) + 1]).then_inc(act_took, 1)
        act.wait_ge(pool_done, KW)
        for q in range(KW):
            act.wait_ge(swish_in, q + 1)
            if q >= 2:
                act.wait_ge(yc_done, q - 1)
            nc.scalar.activation(tmp[q % 2][:, 0:T], yc[:, q], ACT.Sigmoid).then_inc(swish_sig, 1)
        with act.Fori(0, NJ - 1) as i:
            act.wait_ge(product, i * 12 + N_S)
            high_part(0, i * 3 + 8)
            high_part(1, i * 3 + 8)
            for g in range(6):
                if g == 2:
                    high_part(0, i * 3 + 9)
                act.wait_ge(product, i * 12 + (N_S + 6 + g + 1))
                act.wait_ge(dve_took, i * 6 + (D_S + g + 1))
                take_gate(g, (g + 2) % 4)

        for i in range(2):
            for c in range(NCH):
                n = chunk_rows(c)
                act.wait_ge(dve_took, D_B + i * NCH + c + 1)
                own(nc.scalar.activation(junk_h[0:n], x[0:n, c, i * W:(i + 1) * W], ACT.Square,
                                         accum_out=stat[0:n, 30 + i * NCH + c:][:, 0:1]))
        nc.scalar.copy(stat[:, 40:50], stat[:, 30:40]).then_inc(mean_sq, 1)
        act.wait_ge(root_in, 3)
        nc.scalar.activation(stat[:, 55:60], stat[:, 50:55], ACT.Sqrt).then_inc(root, 1)
        for k in range(0, KD, 2):
            act.wait_ge(product, N_O + k + 1)
            nc.scalar.copy(xT[:, k], slot_flat(k % 4)).then_inc(act_took, 1)
        act.wait_ge(exp_in, 1)
        nc.scalar.activation(group_exp, group_exp, ACT.Exp).then_inc(exp_done, 1)
        act.wait_ge(exp_in, 2)
        nc.scalar.activation(pair_exp, pair_exp, ACT.Exp).then_inc(exp_done, 1)

        def silu(e, s, turn, free):
            act.wait_ge(gu_done, e + 1)
            if free is not None:
                act.wait_ge(hid_ready, free)
            nc.scalar.activation(sig[s], ps[:, 2 + s, 0:256], ACT.Silu).then_inc(sig_ready, 1)

        def take_hidden(e, s, turn, free):
            act.wait_ge(hid_turned, e + 1)
            if free is not None:
                act.wait_ge(dn_done, free)
            nc.scalar.copy(hT[s].rearrange("p c m -> p (c m)"), ps[:, 4 + s, 0:256]).then_inc(hT_ready, 1)

        def take_output(e, s, turn, free):
            act.wait_ge(dn_done, e + 1)
            if free is not None:
                act.wait_ge(scattered[s], turn * 16)
            nc.scalar.copy(yo[s], ps[:, 6 + s]).then_inc(yo_ready, 1)

        for e in range(2):
            for stage in (silu, take_hidden, take_output):
                stage(e, e, 0, None)
        with act.Fori(1, NE // 2) as i:
            for s in range(2):
                for stage in (silu, take_hidden, take_output):
                    stage(2 * i + s, s, i, 2 * i + s - 1)
        act.wait_ge(routed, 1)
        n_over = act.value_load(ovf[0:1, NOVF:NOVF + 1], min_val=0, max_val=NOVF)
        with act.Fori(0, NOVF) as j:
            with act.If(n_over > j):
                for stage in (silu, take_hidden, take_output):
                    stage(NE + j, 0, NE // 2 + j, NE + j)

        for c in range(NCH):
            n = chunk_rows(c)
            act.wait_ge(summed, c + 1)
            own(nc.scalar.activation(flat_y[0:n, 0:D], x[0:n, c], ACT.Square, accum_out=stat[0:n, 60 + c:61 + c]))
            nc.scalar.activation(stat[0:n, 65 + c:66 + c], stat[0:n, 60 + c:61 + c], ACT.Sqrt,
                                 scale=1.0 / D, bias=stat[0:n, 95:96]).then_inc(final_root, 1)

    @block.vector
    def _(dve):
        v = nc.vector
        n_own = [0]

        def own(instruction):
            n_own[0] += 1
            instruction.then_inc(dve_step, 1)
            dve.wait_ge(dve_step, n_own[0])

        def wide(a, shape):
            return a.broadcast_to(shape)

        dve.wait_ge(mean_sq, 1)
        v.tensor_scalar(stat[:, 0:NCH], stat[:, 10:10 + NCH], 1.0 / D, EPS, ALU.mult, ALU.add).then_inc(root_in, 1)
        dve.wait_ge(root, 1)
        own(v.reciprocal(stat[:, 10:10 + NCH], stat[:, 5:5 + NCH]))
        for c in range(NCH):
            n = chunk_rows(c)
            v.tensor_scalar(x[0:n, c], x[0:n, c], stat[0:n, 10 + c:11 + c], None, ALU.mult).then_inc(x_normed, 1)
        for k in range(KD):
            dve.wait_ge(act_took, 1 + k + 1)
            v.scalar_tensor_tensor(x_low[:, k], slot_flat(k % 4), param[:, MG + k:MG + k + 1], x_high[:, k].bitcast(F32),
                                   ALU.mult, ALU.subtract).then_inc(dve_took, 1)
        dve.wait_ge(product, 11)
        v.tensor_copy(pool_hist.rearrange("p q t -> p (q t)"), ps[:, 2, 0:480]).then_inc(dve_took, 1)
        dve.wait_ge(product, 12)
        v.tensor_tensor(wsT, ps[:, 4].rearrange("p (h t) -> p h t", h=KW),
                        wide(const["causal"].unsqueeze(1), [P, KW, P]), ALU.mult).then_inc(dve_took, 1)
        dve.wait_ge(step_loaded, 16 * NSEQ * KW)
        own(v.tensor_tensor(step_w, step_w, wide(const["blocks"][0:NS].unsqueeze(1), [NS, KW, NS]), ALU.mult))

        dve.wait_ge(zeroed, 3)
        for q in range(KW):
            dve.wait_ge(glu_gate, q + 1)
            v.tensor_tensor(cext[:, q, CH:CH + SEQ], proj[:, q, 0:SEQ], proj[:, KW + q, 0:SEQ], ALU.mult).then_inc(glu_done, 1)
            v.tensor_tensor(proj[:, q, SEQ:T], proj[:, q, SEQ:T], proj[:, KW + q, SEQ:T], ALU.mult).then_inc(glu_done, 1)
            dve.wait_ge(glu_done, 2 * q + 2)
            own(v.tensor_copy(cext[:, q, CH + SEQ:].rearrange("p (b i) -> p b i", i=CH + STEP)[:, :, CH:],
                              proj[:, q, SEQ:T].rearrange("p (b i) -> p b i", i=STEP)))
        for k in range(TAPS):
            for q in range(KW):
                tap = param[:, TAP + k * KW + q:][:, 0:1]
                for src, acc in (
                    (cext[:, q, k:k + SEQ], yc[:, q, 0:SEQ]),
                    (cext[:, q, CH + SEQ:].rearrange("p (b i) -> p b i", i=CH + STEP)[:, :, k:k + STEP],
                     yc[:, q, SEQ:T].rearrange("p (b i) -> p b i", i=STEP)),
                ):
                    if k == 0:
                        last = v.tensor_scalar(acc, src, tap, param[:, CB + q:CB + q + 1], ALU.mult, ALU.add)
                    else:
                        dve.wait_ge(dve_step, n_own[0] - 2 * KW + 1)
                        last = v.scalar_tensor_tensor(acc, src, tap, acc, ALU.mult, ALU.add)
                    if k == TAPS - 1 and q == KW - 1 and acc.shape[1] == NSEQ:
                        last.then_inc(conv_done, 1)
                    else:
                        last.then_inc(dve_step, 1)
                        n_own[0] += 1

        mv = stat[:, 96:106].rearrange("p (c m) -> p c m", m=2)
        bn6 = stat[:, 106:112]
        for c in range(NCH):
            n = chunk_rows(c)
            dve.wait_ge(act_took, A_PROJ + c + 1)
            own(v.bn_stats(bn6[0:n], vn[0:n, c]))
            own(v.bn_aggr(mv[0:n, c], bn6[0:n]))
        v.tensor_scalar(stat[:, 15:15 + NCH], mv[:, :, 1], EPS, None, ALU.add).then_inc(root_in, 1)
        dve.wait_ge(late_loaded, 16 * 8)
        dve.wait_ge(root, 2)
        own(v.reciprocal(stat[:, 25:25 + NCH], stat[:, 20:20 + NCH]))
        for c in range(NCH):
            n = chunk_rows(c)
            own(v.tensor_scalar(vn[0:n, c], vn[0:n, c], mv[0:n, c, 0:1], stat[0:n, 25 + c:26 + c], ALU.subtract, ALU.mult))
            own(v.tensor_tensor(vn[0:n, c], vn[0:n, c], sgu_rows[0:n, 0], ALU.mult))
            v.tensor_tensor(vn[0:n, c], vn[0:n, c], sgu_rows[0:n, 1], ALU.add).then_inc(v_normed, 1)

        for h in range(KW):
            dve.wait_ge(product, N_G0 + h + 1)
            v.tensor_tensor(yb[:, h, 0:SEQ].rearrange("p (c t) -> p c t", t=P),
                                ps[:, 2 * ((h + 3) % 4)].rearrange("p (c t) -> p c t", t=P),
                                wide(bias_rows[:, h:h + 1], [P, SEQ // P, P]), ALU.add).then_inc(dve_took, 1)
            dve.wait_ge(dve_took, D_SETUP + h + 1)
            v.tensor_tensor(yb[:, h, 0:SEQ], yb[:, h, 0:SEQ], proj[:, 3 * KW + h, 0:SEQ], ALU.mult).then_inc(sgu_done, 1)
        dve.wait_ge(product, N_G0 + KW + 1)
        for h in range(KW):
            last = (v.tensor_tensor(yb[:, h, SEQ:T].rearrange("p (b i) -> p b i", i=STEP),
                                ps[:, 6, h * NS:(h + 1) * NS].rearrange("p (b i) -> p b i", i=STEP),
                                wide(bias_rows[:, h:h + 1, 0:STEP], [P, NSEQ, STEP]), ALU.add))
        last.then_inc(dve_took, 1)
        dve.wait_ge(dve_took, D_SETUP + KW + 1)
        for h in range(KW):
            v.tensor_tensor(yb[:, h, SEQ:T], yb[:, h, SEQ:T], proj[:, 3 * KW + h, SEQ:T], ALU.mult).then_inc(sgu_done, 1)
        dve.wait_ge(sgu_done, 2 * KW)

        dve.wait_ge(product, N_G0 + KW + 2)
        for q in range(KW):
            v.scalar_tensor_tensor(halves(yc[:, q]), slot(0), -1.0 / W, halves(yc[:, q]), ALU.mult, ALU.add).then_inc(
                centred if q < KW - 1 else dve_took, 1)
        dve.wait_ge(product, N_G0 + KW + 3)
        v.tensor_scalar(halves(row_a[:]), slot(1), 1.0 / W, EPS, ALU.mult, ALU.add).then_inc(dve_took, 1)
        dve.wait_ge(root, 3)
        own(v.reciprocal(row_a[:], row_a[:]))
        dve.wait_ge(squared, KW)
        for q in range(KW):
            own(v.tensor_tensor(yc[:, q], yc[:, q], row_a[:], ALU.mult))
            v.tensor_scalar(yc[:, q], yc[:, q], param[:, CG + q:CG + q + 1], param[:, CNB + q:CNB + q + 1],
                            ALU.mult, ALU.add).then_inc(swish_in, 1)
        for q in range(KW):
            dve.wait_ge(swish_sig, q + 1)
            dve.wait_ge(swish_in, q + 1)
            v.tensor_tensor(yc[:, q], yc[:, q], tmp[q % 2][:, 0:T], ALU.mult).then_inc(yc_done, 1)
        dve.wait_ge(yc_done, KW)

        def merge(i):
            dve.wait_ge(act_took, i * 6 + A_S)
            for b in range(6):
                c = b % 2
                m = halves_at(merged, i * 2 + c)
                t = halves(tmp[c][:, 0:T])
                dve.wait_ge(product, i * 12 + (N_S + b + 1))
                if b >= 4:
                    dve.wait_ge(merged_part, i * 2 + c + 1)
                v.tensor_tensor(m if b < 2 else t, slot(b % 4), halves(gates[:, b]), ALU.mult).then_inc(dve_took, 1)
                if b >= 2:
                    dve.wait_ge(dve_took, i * 6 + (D_S + b + 1))
                    v.tensor_tensor(m, m, t, ALU.add).then_inc(merged_part if b < 4 else merged_done, 1)
            dve.wait_ge(merged_done, i * 2 + 2)

        dve.wait_ge(outs_stored, 16)
        with dve.Fori(0, NJ - 1) as i:
            merge(i)
        merge(NJ - 1)

        dve.wait_ge(merged_done, 2 * NJ)
        dve.wait_ge(x_again, 32)
        for i in range(2):
            for c in range(NCH):
                n = chunk_rows(c)
                dve.wait_ge(product, N_B + i * NCH + c + 1)
                v.tensor_tensor(x[0:n, c, i * W:(i + 1) * W], ps[0:n, c], x[0:n, c, i * W:(i + 1) * W],
                                ALU.add).then_inc(dve_took, 1)
        dve.wait_ge(mean_sq, 2)
        own(v.tensor_tensor(stat[:, 50:55], stat[:, 40:45], stat[:, 45:50], ALU.add))
        v.tensor_scalar(stat[:, 50:55], stat[:, 50:55], 1.0 / D, EPS, ALU.mult, ALU.add).then_inc(root_in, 1)
        dve.wait_ge(root, 4)
        own(v.reciprocal(stat[:, 60:65], stat[:, 55:60]))
        dve.wait_ge(dve_took, D_O)
        dve.wait_ge(norm_rows_loaded, 32)
        for c in range(NCH):
            n = chunk_rows(c)
            v.scalar_tensor_tensor(xn2[0:n, c], x[0:n, c], stat[0:n, 60 + c:61 + c], ffn_row[0:n],
                                   ALU.mult, ALU.mult).then_inc(xn2_done, 1)
        own(v.memset(logits, 0.0))
        for k in range(1, KD, 2):
            dve.wait_ge(product, N_O + k + 1)
            v.tensor_copy(xT[:, k], slot_flat(k % 4)).then_inc(dve_took, 1)
        dve.wait_ge(product, N_T + 1)
        lg = ps[:, 0, 0:NCH * (NG + NE)].rearrange("p (c e) -> p c e", c=NCH)
        own(v.tensor_tensor(logits[:, 0:4], lg[:, 0:4], wide(router_b[:].unsqueeze(1), [P, 4, NG + NE]), ALU.add))
        own(v.tensor_tensor(logits[0:NS, 4], lg[0:NS, 4], router_b[0:NS], ALU.add))

        def s5(i):
            return small[:, i]

        def w5(i, n):
            return wide(small[:, i].unsqueeze(2), [P, NCH, n])

        def c5(name, n):
            return wide(const[name].unsqueeze(1), [P, NCH, n])

        gl, el = logits[:, :, 0:NG], logits[:, :, NG:]
        own(v.tensor_reduce(s5(1), gl, AX, ALU.max))
        v.tensor_tensor(group_exp, gl, w5(1, NG), ALU.subtract).then_inc(exp_in, 1)
        own(v.tensor_tensor(cand[:, :, 0:NG], gl, w5(1, NG), ALU.not_equal))
        own(v.scalar_tensor_tensor(cand[:, :, 0:NG], cand[:, :, 0:NG], 64.0, c5("group", NG), ALU.mult, ALU.add))
        own(v.tensor_reduce(s5(2), cand[:, :, 0:NG], AX, ALU.min))
        own(v.tensor_tensor(cand, c5("group_of", NE), w5(2, NE), ALU.is_equal))
        own(v.tensor_tensor(masked, el, cand, ALU.mult))
        own(v.tensor_scalar(cand, cand, -1.0, 1e30, ALU.add, ALU.mult))
        own(v.tensor_tensor(masked, masked, cand, ALU.add))
        for k in range(2):
            own(v.tensor_reduce(s5(3 + k), masked, AX, ALU.max))
            own(v.tensor_tensor(cand, masked, w5(3 + k, NE), ALU.not_equal))
            own(v.scalar_tensor_tensor(cand, cand, 64.0, c5("expert", NE), ALU.mult, ALU.add))
            own(v.tensor_reduce(s5(5 + k), cand, AX, ALU.min))
            own(v.tensor_tensor(one_hot[k], c5("expert", NE), w5(5 + k, NE), ALU.is_equal))
            if k == 0:
                own(v.scalar_tensor_tensor(masked, one_hot[0], -1e31, masked, ALU.mult, ALU.add))
        v.tensor_tensor(pair_exp, s5(4), s5(3), ALU.subtract).then_inc(exp_in, 1)
        own(v.tensor_tensor(chosen_mask, one_hot[0], one_hot[1], ALU.add))
        v.tensor_tensor(chosen_mask, chosen_mask, wide(const["valid"].unsqueeze(2), [P, NCH, NE]), ALU.mult).then_inc(chosen, 1)
        dve.wait_ge(exp_done, 2)
        own(v.tensor_reduce(s5(7), group_exp, AX, ALU.add))
        own(v.tensor_scalar(s5(8), pair_exp, 1.0, None, ALU.add))
        own(v.tensor_tensor(s5(7), s5(7), s5(8), ALU.mult))
        own(v.reciprocal(gate_of[:, 0], s5(7)))
        own(v.tensor_tensor(gate_of[:, 1], gate_of[:, 0], pair_exp, ALU.mult))
        dve.wait_ge(product, N_L + 1)
        own(v.memset(before_chunk[:, 0], 0.0))
        for c in range(NCH):
            own(v.tensor_tensor(before_chunk[:, c + 1], ps[:, 3, c * NE:(c + 1) * NE], before_chunk[:, c], ALU.add))
        own(v.tensor_tensor(rank, ps[:, 2, 0:NCH * NE].rearrange("p (c e) -> p c e", e=NE), before_chunk[:, 0:NCH], ALU.add))
        own(v.tensor_tensor(compare, wide(before_chunk[:, NCH].unsqueeze(2), [P, NE, MAXB]),
                            wide(const["steps"].unsqueeze(1), [P, NE, MAXB]), ALU.is_gt))
        own(v.tensor_reduce(further[:, 0], compare, AX, ALU.add))
        own(v.tensor_tensor_scan(further[:, 1], const["ones"][:, 0:NE], further[:, 0], 0.0, ALU.mult, ALU.add))
        own(v.tensor_tensor(further[:, 2], further[:, 1], further[:, 0], ALU.subtract))
        own(v.tensor_tensor(compare_e, wide(further[:, 1:2], [P, NOVF, NE]),
                            wide(const["further"].unsqueeze(2), [P, NOVF, NE]), ALU.is_le))
        own(v.tensor_reduce(at_further, compare_e, AX, ALU.add))
        own(v.tensor_scalar(ovf[:, 0:NOVF], at_further, float(NE - 1), None, ALU.min))
        own(v.tensor_copy(ovf[:, NOVF:], further[:, 1, NE - 1:NE]))
        for k in range(2):
            own(v.tensor_tensor(cand, one_hot[k], rank, ALU.mult))
            own(v.tensor_reduce(s5(9), cand, AX, ALU.add))
            own(v.tensor_tensor(cand, one_hot[k], wide(further[:, 2:3], [P, NCH, NE]), ALU.mult))
            own(v.tensor_reduce(s5(10), cand, AX, ALU.add))
            own(v.tensor_tensor(by_step, w5(9, MAXB), wide(const["steps"].unsqueeze(1), [P, NCH, MAXB]), ALU.is_ge))
            own(v.tensor_reduce(s5(11), by_step, AX, ALU.add))
            own(v.scalar_tensor_tensor(s5(12), s5(11), -float(CAP), s5(9), ALU.mult, ALU.add))
            own(v.tensor_tensor(s5(13), s5(10), s5(11), ALU.add))
            own(v.scalar_tensor_tensor(s5(13), s5(13), float(NE - 1), s5(5 + k), ALU.add, ALU.subtract))
            own(v.scalar_tensor_tensor(s5(13), s5(11), 0.0, s5(13), ALU.is_gt, ALU.mult))
            own(v.tensor_tensor(s5(13), s5(13), s5(5 + k), ALU.add))
            own(v.tensor_tensor(at_place[k], c5("place", P), w5(12, P), ALU.is_equal))
            if k == 0:
                own(v.tensor_scalar(s5(14), const["token2"], 2.0, -OFF, ALU.mult, ALU.add))
            else:
                own(v.tensor_scalar(s5(14), s5(14), 2.0, None, ALU.add))
            own(v.tensor_tensor(cand_b, c5("block", NBLK), w5(13, NBLK), ALU.is_equal))
            own(v.tensor_tensor(cand_b, cand_b, wide(const["valid"].unsqueeze(2), [P, NCH, NBLK]), ALU.mult))
            own(v.tensor_tensor(in_block[k][:, :, 0:NBLK], cand_b, wide(const["token2"].unsqueeze(2), [P, NCH, NBLK]), ALU.mult))
            v.tensor_tensor(in_block[k][:, :, NBLK:], cand_b, w5(14, NBLK), ALU.mult).then_inc(tables_in, 1)
            dve.wait_ge(tables_in, k + 1)
        dve.wait_ge(product, N_L + 2)
        own(v.tensor_scalar(gidx[:], ps[:, 4, 0:NBLK], const["half"], None, ALU.add))
        v.tensor_scalar(sidx[:], ps[:, 4, NBLK:2 * NBLK], const["half"], OFF, ALU.add, ALU.add).then_inc(routed, 1)

        def take_rows(e, s, turn, free):
            dve.wait_ge(xg_turned, e + 1)
            if free is not None:
                dve.wait_ge(gu_done, free)
            v.tensor_copy(xgT[s].rearrange("p c m -> p (c m)"), ps[:, s]).then_inc(xgT_ready, 1)

        def times_up(e, s, turn, free):
            dve.wait_ge(sig_ready, e + 1)
            if free is not None:
                dve.wait_ge(hid_turned, free)
            v.tensor_tensor(hid[s], sig[s], ps[:, 2 + s, 256:512], ALU.mult).then_inc(hid_ready, 1)

        dve.wait_ge(xn2_stored, 16 * NCH)
        take_rows(0, 0, 0, None)
        for e in range(2):
            take_rows(e + 1, 1 - e, e, None if e == 0 else 1)
            times_up(e, e, 0, None)
        with dve.Fori(1, NE // 2 - 1) as i:
            for s in range(2):
                take_rows(2 * i + s + 1, 1 - s, i + s, 2 * i + s)
                times_up(2 * i + s, s, i, 2 * i + s - 1)
        i = NE // 2 - 1
        take_rows(2 * i + 1, 1, i, 2 * i)
        times_up(2 * i, 0, i, 2 * i - 1)
        times_up(2 * i + 1, 1, i, 2 * i)
        n_over = dve.value_load(ovf[0:1, NOVF:NOVF + 1], min_val=0, max_val=NOVF)
        with dve.Fori(0, NOVF) as j:
            with dve.If(n_over > j):
                take_rows(NE + j, 0, NE // 2 + j, NE + j)
                times_up(NE + j, 0, NE // 2 + j, NE + j)

        own(v.memset(stat[:, 95:96], EPS))
        for c in range(NCH):
            n = chunk_rows(c)
            dve.wait_ge(y_loaded[c], 16)
            yr = y_place(c)[0:n].rearrange("p (k n) -> p k n", k=2)
            own(v.scalar_tensor_tensor(x[0:n, c], yr[:, 0], gate_of[0:n, 0, c:c + 1], x[0:n, c], ALU.mult, ALU.add))
            v.scalar_tensor_tensor(x[0:n, c], yr[:, 1], gate_of[0:n, 1, c:c + 1], x[0:n, c], ALU.mult, ALU.add).then_inc(summed, 1)
        for c in range(NCH):
            n = chunk_rows(c)
            dve.wait_ge(final_root, c + 1)
            own(v.reciprocal(stat[0:n, 70 + c:71 + c], stat[0:n, 65 + c:66 + c]))
            v.scalar_tensor_tensor(x[0:n, c], x[0:n, c], stat[0:n, 70 + c:71 + c], final_row[0:n], ALU.mult, ALU.mult).then_inc(final_done, 1)

    @block.gpsimd
    def _(pool):
        g = nc.gpsimd
        n_own = [0]

        def own(instruction):
            n_own[0] += 1
            instruction.then_inc(pool_step, 1)
            pool.wait_ge(pool_step, n_own[0])

        g.memset(step_w, 0.0).then_inc(zeroed, 1)
        g.memset(stat[:], 1.0).then_inc(zeroed, 1)
        g.memset(cext[:, :, 0:CH], 0.0).then_inc(zeroed, 1)

        def low_part(s, n):
            pool.wait_ge(high_ready, n + 1)
            g.tensor_tensor(w_low[s][:], wring[s], w_high[s][:].bitcast(F32), ALU.subtract).then_inc(low_ready, 1)

        def window_sums(q):
            pool.wait_ge(act_took, A_SETUP + 8 + q + 1)
            p_q = proj[:, 2 * KW + q]
            own(g.memset(tmp[0][:, 0:PH], 0.0))
            own(g.tensor_copy(tmp[0][:, PH:PH + SEQ], p_q[:, 0:SEQ]))
            ext = tmp[0][:, PH + SEQ:].rearrange("p (b i) -> p b i", i=PH + STEP)
            own(g.tensor_copy(ext[:, :, 0:PH], pool_hist[:, q].rearrange("p (b i) -> p b i", i=PH)))
            own(g.tensor_copy(ext[:, :, PH:], p_q[:, SEQ:T].rearrange("p (b i) -> p b i", i=STEP)))
            for level in range(q + 1):
                src, dst, shift = tmp[level % 2], tmp[(level + 1) % 2], 1 << level
                own(g.tensor_tensor(dst[:, shift:], src[:, shift:], src[:, 0:PEXT - shift], ALU.add))
                own(g.tensor_copy(dst[:, 0:shift], src[:, 0:shift]))

        def less_token(q):
            s = tmp[(q + 1) % 2]
            w = float(WINDOWS[q])
            own(g.tensor_scalar(pool_d[:, q, 0:SEQ], s[:, PH:PH + SEQ], 1 / w, None, ALU.mult))
            own(g.tensor_tensor(pool_d[:, q, 0:16], s[:, PH:PH + 16], const["count"][:, 16 * q:16 * q + 16], ALU.mult))
            own(g.tensor_scalar(pool_d[:, q, SEQ:T].rearrange("p (b i) -> p b i", i=STEP),
                                s[:, PH + SEQ:].rearrange("p (b i) -> p b i", i=PH + STEP)[:, :, PH:], 1 / w, None, ALU.mult))
            g.tensor_tensor(pool_d[:, q], pool_d[:, q], proj[:, 2 * KW + q], ALU.subtract).then_inc(pool_done, 1)

        for n in range(FIRST_B0):
            low_part(n % 2, n)
            if n == 6:
                pool.wait_ge(product, 12)
                pool.wait_ge(dve_took, D_SETUP)
            if n in (6, 7):
                window_sums(n - 6)
                less_token(n - 6)
            if n in (8, 10):
                window_sums(2 + (n - 8) // 2)
            if n in (9, 11):
                less_token(2 + (n - 9) // 2)
        with pool.Fori(0, NJ - 1) as i:
            for g_pair in range(3):
                low_part(g_pair % 2, i * 3 + (FIRST_B0 + g_pair))

        def gather(e, s, turn, free):
            if free is not None:
                pool.wait_ge(xg_turned, free)
                pool.sem_inc(waits_met, 1)
            g.tensor_copy(idx_now[:, s:s + 1], gidx[:, bass.ds(e, 1)]).then_inc(gather_idx[s], 1)
            pool.wait_ge(gather_idx[s], turn + 1)
            pool.sem_inc(waits_met, 1)
            pool.indirect_dma_start(xg[s], None, xn2_dram.rearrange("t (h n) -> (t h) n", h=2),
                                    bass.IndirectOffsetOnAxis(ap=idx_now[:, s:s + 1], axis=0)).then_inc(xg_loaded[s], 16)

        def scatter(e, s, turn, free):
            if free is not None:
                pool.wait_ge(scattered[s], turn * 16)
                pool.sem_inc(waits_met, 1)
            g.tensor_copy(idx_now[:, 2 + s:3 + s], sidx[:, bass.ds(e, 1)]).then_inc(scatter_idx[s], 1)
            pool.wait_ge(scatter_idx[s], turn + 1)
            pool.wait_ge(yo_ready, e + 1)
            pool.sem_inc(waits_met, 1)
            pool.indirect_dma_start(y_dram, bass.IndirectOffsetOnAxis(ap=idx_now[:, 2 + s:3 + s], axis=0), yo[s], None,
                                    bounds_check=4 * T - 1, oob_is_err=False).then_inc(scattered[s], 16)

        pool.wait_ge(routed, 1)
        pool.wait_ge(xn2_stored, 16 * NCH)
        gather(0, 0, 0, None)
        gather(1, 1, 0, None)
        scatter(0, 0, 0, None)
        gather(2, 0, 1, 1)
        scatter(1, 1, 0, None)
        with pool.Fori(1, NE // 2 - 1) as i:
            for s in range(2):
                gather(2 * i + s + 1, 1 - s, i + s, 2 * i + s)
                scatter(2 * i + s, s, i, True)
        i = NE // 2 - 1
        gather(2 * i + 1, 1, i, 2 * i)
        scatter(2 * i, 0, i, True)
        scatter(2 * i + 1, 1, i, True)
        n_over = pool.value_load(ovf[0:1, NOVF:NOVF + 1], min_val=0, max_val=NOVF)
        with pool.Fori(0, NOVF) as j:
            with pool.If(n_over > j):
                gather(NE + j, 0, NE // 2 + j, NE + j)
                scatter(NE + j, 0, NE // 2 + j, True)


INPUTS = [
    "x_prompt", "x_sample", "state_pool", "state_conv", "mix_norm_g", "w_in", "pool_w", "pool_scale", "sgu_norm_g",
    "sgu_norm_b", "sgu_w", "sgu_b", "conv_w", "conv_b", "conv_norm_g", "conv_norm_b", "w_branch_pool",
    "w_branch_sgu", "w_branch_conv", "w_out", "ffn_norm_g", "w_group", "b_group", "w_router", "b_router",
    "w_gate_e", "w_up_e", "w_down_e", "final_norm_g",
]
OUTPUTS = [
    ("y_prompt", (1, SEQ, D)), ("y_sample", (NSEQ, STEP, D)), ("pool_prompt", (1, 1, PH, W)),
    ("pool_sample", (1, NSEQ, PH, W)), ("conv_prompt", (1, 1, CH, W)), ("conv_sample", (1, NSEQ, CH, W)),
    ("chunk_v_sample", (1, NSEQ, STEP, W)),
]


def kernel(**inputs):
    import concourse.bacc as bacc
    from concourse.bass_utils import run_bass_kernel_spmd

    nc = bacc.Bacc("TRN2", target_bir_lowering=False, num_devices=1)
    arrays = {name: np.ascontiguousarray(inputs[name]) for name in INPUTS}
    arrays["shape_constants"] = shape_constants()
    d = {name: nc.dram_tensor("in_" + name, a.shape, F32, kind="ExternalInput").ap() for name, a in arrays.items()}
    out = {name: nc.dram_tensor("out_" + name, shape, F32, kind="ExternalOutput").ap() for name, shape in OUTPUTS}
    build(nc, d, out)
    result = run_bass_kernel_spmd(nc, [{"in_" + name: a for name, a in arrays.items()}], core_ids=[0]).results[0]
    return tuple(result["out_" + name] for name, _ in OUTPUTS)
```

```python
from contextlib import ExitStack

import concourse.bass as bass
import concourse.mybir as mybir
import numpy as np
from concourse.alu_op_type import AluOpType as ALU

F32 = mybir.dt.float32
F32R = mybir.dt.float32r
I32 = mybir.dt.int32
ACT = mybir.ActivationFunctionType
AX = mybir.AxisListType.X

P = 128
D = 1024
KD = D // P
W = 512
KW = W // P
SEQ = 512
NSEQ, STEP = 8, 4
NS = NSEQ * STEP
T = SEQ + NS
HT = T // 2
NCH = SEQ // P + 1
PH, CH = 15, 30
TAPS = 31
WINDOWS = (2, 4, 8, 16)
NG, EPG, NE = 4, 8, 32
DE = 512
CAP = 64
MAXB = T // CAP
NOVF = (2 * T - 1) // CAP
NBLK = NE + NOVF
EPS = 1e-6
OFF = 8192.0
PEXT = PH + SEQ + NSEQ * (PH + STEP)
CEXT = CH + SEQ + NSEQ * (CH + STEP)
IN_COLS = W * 5 + 3 * D


def chunk_rows(c):
    return P if c < NCH - 1 else NS


def _columns(parts):
    at, out = 0, {}
    for name, n in parts:
        out[name] = slice(at, at + n)
        at += n
    return out, at


CONST, NCONST = _columns([
    ("ident", P), ("causal", P), ("before", P), ("ones", P), ("blocks", NS),
    ("expert", NE), ("group_of", NE), ("group", NG), ("place", P), ("block", NBLK), ("token2", NCH),
    ("valid", NCH), ("half", 1), ("steps", MAXB), ("further", NOVF), ("count", NG * 16), ("pad", 1),
])


def shape_constants():
    c = np.zeros((P, NCONST), np.float32)
    p = np.arange(P)
    c[:, CONST["ident"]] = np.eye(P)
    c[:, CONST["causal"]] = p[:, None] <= p[None, :]
    c[:, CONST["before"]] = p[:, None] < p[None, :]
    c[:, CONST["ones"]] = 1
    s = np.arange(NS)
    c[:NS, CONST["blocks"]] = (s[:, None] // STEP == s[None, :] // STEP) & (s[:, None] <= s[None, :])
    c[:, CONST["expert"]] = np.arange(NE)
    c[:, CONST["group_of"]] = np.arange(NE) // EPG
    c[:, CONST["group"]] = np.arange(NG)
    c[:, CONST["place"]] = p % CAP
    c[:, CONST["block"]] = np.arange(NBLK)
    token = np.arange(NCH)[None, :] * P + p[:, None]
    c[:, CONST["token2"]] = 2 * token
    c[:, CONST["valid"]] = token < T
    c[:, CONST["half"]] = (p >= CAP)[:, None]
    c[:, CONST["steps"]] = CAP * np.arange(1, MAXB + 1)
    c[:, CONST["further"]] = np.arange(NOVF)
    for g, w in enumerate(WINDOWS):
        c[:, CONST["count"].start + 16 * g:][:, :16] = 1 / np.minimum(np.arange(16) + 1, w)
    return c


def build(nc, d, out):
    ctx = ExitStack()
    with ctx:
        program(nc, d, out, ctx)


def program(nc, d, out, ctx):
    def sb(name, shape, dt=F32):
        return ctx.enter_context(nc.sbuf_tensor(name, shape, dt))

    def next_place():
        return (nc.sbuf_base + 31) // 32 * 32

    def over(name, shape, dt, tensor_at, first=0):
        return nc.alloc_sbuf_tensor_at(name, shape, dt, offset=tensor_at + 4 * first)

    def sem(name):
        return ctx.enter_context(nc.semaphore(name))

    ctx.enter_context(nc.allow_non_contiguous_dma(reason="block-diagonal corner of the SGU weights"))

    gu0_at = next_place()
    gu0 = sb("gu0", [P, 2, KD, DE])
    ring = sb("ring", [P, 4 * D])
    slot1_at = next_place()
    slot1 = sb("slot1", [P, 12 * D])
    xx_at = next_place()
    xx = sb("xx", [P, 2 * KD * T])
    xh = sb("xh", [P, NCH * D])
    ybr_at = next_place()
    ybr = sb("ybr", [P, 3, KW, T])
    mid_at = next_place()
    mid = sb("mid", [P, 4736])
    cst = sb("cst", [P, NCONST])
    bias_rows = sb("bias_rows", [P, KW, P])
    pool_w = sb("pool_w", [P, KW, P])
    param = sb("param", [P, 160])
    row_a = sb("row_a", [P, T])
    router = sb("router", [P, KD, NG + NE])
    router_b = sb("router_b", [P, NG + NE])
    stat = sb("stat", [P, 112])
    gate_of = sb("gate_of", [P, 2, NCH])
    gidx = sb("gidx", [P, NBLK], I32)
    sidx = sb("sidx", [P, NBLK], I32)
    idx_now = sb("idx_now", [P, 4], I32)
    ovf = sb("ovf", [P, NOVF + 1], I32)
    ps = ctx.enter_context(nc.psum_tensor("ps", [P, 8, 512], F32))

    w_high = [over(f"w_high{s}", [P, KD, 256], F32R, gu0_at, s * 2 * D) for s in range(2)]
    w_low = [over(f"w_low{s}", [P, KD, 256], F32R, gu0_at, (2 + s) * 2 * D) for s in range(2)]
    x_high = over("x_high", [P, KD, T], F32R, xx_at)
    x_low = over("x_low", [P, KD, T], F32R, xx_at, KD * T)
    y_high = [over(f"y_high{b}", [P, KW, T], F32R, slot1_at, q * KW * T) for b, q in enumerate((2, 0, 1))]
    y_low = [over(f"y_low{b}", [P, KW, T], F32R, ybr_at, b * KW * T) for b in range(3)]
    m_high = over("m_high", [P, KD, T], F32R, slot1_at, 12 * D - KD * T)
    m_low = over("m_low", [P, KD, T], F32R, mid_at)

    wring = [ring[:, s * 2 * D:(s + 1) * 2 * D].rearrange("p (k n) -> p k n", k=KD) for s in range(2)]
    gu = [gu0[:], slot1[:, 0:8 * D].rearrange("p (m k f) -> p m k f", m=2, k=KD)]
    dn = [x.rearrange("p (k n) -> p k n", n=D) for x in (ring[:], slot1[:, 8 * D:12 * D])]
    proj = slot1[:, 0:16 * T].rearrange("p (q t) -> p q t", t=T)
    cext = slot1[:, 16 * T:16 * T + KW * CEXT].rearrange("p (q t) -> p q t", t=CEXT)
    step_w = slot1[0:NS, 16 * T + KW * CEXT:][:, 0:KW * NS].rearrange("p (h s) -> p h s", s=NS)
    states = slot1[:, KW * T:KW * T + 4 * W].rearrange("p (q t) -> p q t", t=W)
    x = xh[:].rearrange("p (c n) -> p c n", n=D)
    squares = proj[:, 3 * KW:4 * KW]
    gates = xh[:, 0:4 * T].rearrange("p (q t) -> p q t", t=T)
    tmp = [xh[:, 4 * T + i * PEXT:][:, 0:PEXT] for i in range(2)]
    pool_hist = xh[:, 4 * T + 2 * PEXT:][:, 0:KW * NSEQ * PH].rearrange("p (q t) -> p q t", t=NSEQ * PH)
    xT = xx[:, 0:KD * T].rearrange("p (k t) -> p k t", t=T)
    late_rows = xx[:, KD * T:]
    ffn_row, final_row = (late_rows[:, i * D:(i + 1) * D] for i in range(2))
    pool_d = mid[:, 0:KW * T].rearrange("p (q t) -> p q t", t=T)
    vn = mid[:, KW * T:KW * T + NCH * W].rearrange("p (c n) -> p c n", n=W)
    merged = mid[:, 0:KD * T].rearrange("p (q t) -> p q t", t=T)
    conv_rows = mid[:, 0:2 * W].rearrange("p (a n) -> p a n", n=W)
    pool_rows = mid[:, 2 * W:3 * W]
    sgu_w_rows = mid[:, 3 * W:4 * W].rearrange("p (h s) -> p h s", s=P)
    param_rows = mid[:, 4 * W:4 * W + 2 * P].rearrange("p (a n) -> p a n", n=P)
    junk = mid[:, 4 * W + 2 * P:4 * W + 2 * P + D]
    ya, yb, yc = (ybr[:, n] for n in range(3))
    sgu_rows = ybr[:, 1].rearrange("p q t -> p (q t)")[:, 0:2 * W].rearrange("p (a n) -> p a n", n=W)
    wsT = ybr[:, 1, KW - 1, 0:KW * P].rearrange("p (h t) -> p h t", t=P)
    flat_y = ybr[:].rearrange("p a q t -> p (a q t)")
    xn2 = flat_y[:, 0:NCH * D].rearrange("p (c n) -> p c n", n=D)
    at = [0]

    def scratch(*shape):
        n = int(np.prod(shape))
        v = mid[:, at[0]:at[0] + n]
        at[0] += n
        assert at[0] <= 4736
        if len(shape) == 2:
            v = v.rearrange("p (a b) -> p a b", b=shape[1])
        return v

    flat_x = xx[:, 0:KD * T]
    xg = [flat_x[:, s * 512:(s + 1) * 512] for s in range(2)]
    yo = [flat_x[:, 1024 + s * 512:][:, 0:512] for s in range(2)]
    hid = [flat_x[:, 2048 + s * 256:][:, 0:256] for s in range(2)]
    hT = [flat_x[:, 2560 + s * 256:][:, 0:256].rearrange("p (c m) -> p c m", c=2) for s in range(2)]
    sig = [flat_x[:, 3072 + s * 256:][:, 0:256] for s in range(2)]
    xgT = [flat_y[:, 5120 + s * 512:][:, 0:512].rearrange("p (c m) -> p c m", c=4) for s in range(2)]

    const = {k: cst[:, v] for k, v in CONST.items()}
    ident = const["ident"]
    MG, PSC, CB, CG, CNB, TAP = 0, 8, 12, 16, 20, 24

    xn2_dram = nc.dram_tensor("xn2_rows", (T, D), F32, kind="Internal").ap()
    y_dram = nc.dram_tensor("expert_rows", (T * 2 * 2, W), F32, kind="Internal").ap()

    def slot(r):
        return ps[:, 2 * r:2 * r + 2, 0:HT]

    def slot_flat(r, n=T):
        return ps[:, 2 * r:2 * r + 2, :].rearrange("p b n -> p (b n)")[:, 0:n]

    def halves(v):
        return v.rearrange("p (b n) -> p b n", b=2)

    def y_place(c):
        if c < 4:
            return gu0[:].rearrange("p m k f -> p (m k f)")[:, c * 2 * D:(c + 1) * 2 * D]
        return slot1[:, 0:2 * D]

    def halves_at(t, q):
        return t[:, bass.ds(q, 1)].rearrange("p a (b n) -> p (a b) n", b=2)

    logits = scratch(NCH, NG + NE)
    group_exp = scratch(NCH, NG)
    cand = scratch(NCH, NE)
    masked = scratch(NCH, NE)
    one_hot = [scratch(NCH, NE) for _ in range(2)]
    chosen_mask = scratch(NCH, NE)
    rank = scratch(NCH, NE)
    before_chunk = scratch(NCH + 1, NE)
    small = scratch(40, NCH)
    pair_exp = small[:, 0]
    at_place = [scratch(NCH, P) for _ in range(2)]
    in_block = [late_rows[:, 2 * D + i * NCH * 2 * NBLK:][:, 0:NCH * 2 * NBLK].rearrange("p (c n) -> p c n", c=NCH)
                for i in range(2)]
    junk_h = bias_rows[:].rearrange("p h t -> p (h t)")
    further = scratch(4, NE)
    compare = scratch(NE, MAXB)
    compare_e = scratch(NOVF, NE)
    at_further = scratch(1, NOVF)[:, 0]
    cand_b = scratch(NCH, NBLK)
    by_step = scratch(NCH, MAXB)

    x_loaded = sem("x_loaded")
    const_loaded = sem("const_loaded")
    param_loaded = sem("param_loaded")
    rows_loaded = sem("rows_loaded")
    late_loaded = sem("late_loaded")
    norm_rows_loaded = sem("norm_rows_loaded")
    high_ready = sem("high_ready")
    low_ready = sem("low_ready")
    step_loaded = sem("step_loaded")
    zeroed = sem("zeroed")
    wring_loaded = [sem(f"wring_loaded{s}") for s in range(2)]
    half_rows = sem("half_rows")
    product = sem("product")
    act_took = sem("act_took")
    dve_took = sem("dve_took")
    act_step = sem("act_step")
    dve_step = sem("dve_step")
    pool_step = sem("pool_step")
    mean_sq = sem("mean_sq")
    root = sem("root")
    root_in = sem("root_in")
    x_normed = sem("x_normed")
    glu_gate = sem("glu_gate")
    glu_done = sem("glu_done")
    conv_done = sem("conv_done")
    pool_done = sem("pool_done")
    v_normed = sem("v_normed")
    sgu_done = sem("sgu_done")
    centred = sem("centred")
    squared = sem("squared")
    swish_in = sem("swish_in")
    swish_sig = sem("swish_sig")
    yc_done = sem("yc_done")
    merged_done = sem("merged_done")
    x_again = sem("x_again")
    merged_part = sem("merged_part")
    merged_high = sem("merged_high")
    merged_low = sem("merged_low")
    sgu_high = sem("sgu_high")
    sgu_low = sem("sgu_low")
    conv_high = sem("conv_high")
    conv_low = sem("conv_low")
    tap_step = sem("tap_step")
    xn2_done = sem("xn2_done")
    xn2_stored = sem("xn2_stored")
    logits_in = sem("logits_in")
    exp_in = sem("exp_in")
    exp_done = sem("exp_done")
    chosen = sem("chosen")
    tables_in = sem("tables_in")
    routed = sem("routed")
    states_stored = sem("states_stored")
    outs_stored = sem("outs_stored")
    gu_loaded = [sem(f"gu_loaded{s}") for s in range(2)]
    dn_loaded = [sem(f"dn_loaded{s}") for s in range(2)]
    xg_loaded = [sem(f"xg_loaded{s}") for s in range(2)]
    waits_met = sem("waits_met")
    scattered = [sem(f"scattered{s}") for s in range(2)]
    xg_turned = sem("xg_turned")
    xgT_ready = sem("xgT_ready")
    gu_done = sem("gu_done")
    sig_ready = sem("sig_ready")
    hid_ready = sem("hid_ready")
    hid_turned = sem("hid_turned")
    hT_ready = sem("hT_ready")
    dn_done = sem("dn_done")
    yo_ready = sem("yo_ready")
    gather_idx = [sem(f"gather_idx{s}") for s in range(2)]
    scatter_idx = [sem(f"scatter_idx{s}") for s in range(2)]
    y_loaded = [sem(f"y_loaded{c}") for c in range(NCH)]
    summed = sem("summed")
    final_sq = sem("final_sq")
    final_in = sem("final_in")
    final_root = sem("final_root")
    final_done = sem("final_done")

    block = ctx.enter_context(nc.Block())

    N_SETUP = 12
    A_SETUP, D_SETUP = KD + 2, KD + 2
    N_PROJ, A_PROJ = N_SETUP + 16, A_SETUP + 16
    N_V, A_V = N_PROJ + NCH, A_PROJ + NCH
    N_G0, A_G0 = N_V + 4, A_V + 4
    N_S, A_S, D_S = N_G0 + 11, A_G0 + 2 + KW, D_SETUP + 5 + KW
    NJ = D // (2 * P)
    N_D1, A_D1, D_D1 = N_S + 8 * (NJ - 1), A_S + 4 * (NJ - 1), D_S + 4 * (NJ - 1)
    N_D2, D_D2 = N_D1 + 6, D_D1 + 6
    N_B, A_B, D_B = N_D2 + 16, A_D1 + 8, D_D2 + 8
    N_O, D_O = N_B + 2 * NCH, D_B + 2 * NCH
    N_T, A_T, D_T = N_O + KD, A_B + KD // 2, D_O + KD // 2
    N_L, D_L = N_T + 1, D_T + 1

    w_in = d["w_in"][0]
    proj_cols = [3 * W, 3 * W + 256, 4 * W, 4 * W + 256, 0, 256, W, W + 256, 2 * W, 2 * W + 256]

    def gate_pair(b, j):
        return w_in[:, 5 * W + b * D + j * 256:][:, 0:256]

    def branch_pair(b, j):
        return d[("w_branch_pool", "w_branch_sgu", "w_branch_conv")[b]][0][:, j * 256:(j + 1) * 256]

    pairs = [w_in[:, c:c + 256] for c in proj_cols] + [gate_pair(b, 0) for b in range(2)]
    for j in range(NJ):
        pairs += [branch_pair(b, j) for b in range(2)]
        if j + 1 < NJ:
            pairs += [gate_pair(b, j + 1) for b in range(2)]
    for i in range(NJ // 2):
        pairs += [gate_pair(2, 2 * i + c) for c in range(2)] + [branch_pair(2, 2 * i + c) for c in range(2)]
    pairs += [d["w_out"][0][:, j * 256:(j + 1) * 256] for j in range(4)]
    FIRST_G0, FIRST_D1, FIRST_D2 = 10, 12, 12 + 4 * NJ - 2
    FIRST_OUT = len(pairs) - 4
    LATE_TAPS = 3
    EARLY_TAPS = TAPS - LATE_TAPS * (NJ - 1)

    def expert_gu(m, e):
        w = d["w_gate_e" if m == 0 else "w_up_e"][0]
        return w[bass.ds(e, 1)].rearrange("e (h p c) f -> p (e h) (c f)", h=2, c=4)

    def expert_dn(e):
        return d["w_down_e"][0][bass.ds(e, 1)].rearrange("e (h p c) n -> p (e h) (c n)", h=2, c=2)

    @block.sync
    def _(sp):
        sp.dma_start(x[:, 0:4], d["x_prompt"][0].rearrange("(c p) n -> p c n", p=P)).then_inc(x_loaded, 16)
        sp.dma_start(x[0:NS, 4], d["x_sample"].rearrange("b i n -> (b i) n")).then_inc(x_loaded, 16)
        sp.dma_start(cst[:], d["shape_constants"]).then_inc(const_loaded, 16)
        sp.dma_start(param_rows[0:124, 0], d["conv_w"][0].rearrange("k (q c) -> (k q) c", c=P)).then_inc(param_loaded, 16)
        for first, name in ((MG, "mix_norm_g"), (PSC, "pool_scale"), (CB, "conv_b"), (CG, "conv_norm_g"), (CNB, "conv_norm_b")):
            rows = d[name][0].rearrange("(k c) -> k c", c=P)
            sp.dma_start(param_rows[first:first + rows.shape[0], 1], rows).then_inc(param_loaded, 16)
        for n in range(2):
            sp.dma_start(wring[n], pairs[n].rearrange("(k p) n -> p k n", p=P)).then_inc(wring_loaded[n], 16)
        for a in range(2):
            sp.dma_start(conv_rows[0:120, a], d["state_conv"][0][4 * a:4 * a + 4].rearrange("b i c -> (b i) c")).then_inc(rows_loaded, 16)
        sp.dma_start(pool_rows[0:120], d["state_pool"][0].rearrange("b i c -> (b i) c")).then_inc(rows_loaded, 16)
        sp.dma_start(sgu_w_rows, d["sgu_w"][0].rearrange("h t s -> t h s")).then_inc(rows_loaded, 16)
        sp.wait_ge(zeroed, 1)
        for b in range(NSEQ):
            for h in range(KW):
                sp.dma_start(step_w[b * STEP:(b + 1) * STEP, h, b * STEP:(b + 1) * STEP],
                             d["sgu_w"][0][h, 0:STEP, 0:STEP].rearrange("t s -> s t")).then_inc(step_loaded, 16)
        late = [
            (pool_w[:], d["pool_w"][0].rearrange("g c n -> c g n")),
            (sgu_rows[:, 0], d["sgu_norm_g"][0].partition_broadcast(P)),
            (sgu_rows[:, 1], d["sgu_norm_b"][0].partition_broadcast(P)),
            (bias_rows[:], d["sgu_b"][0].partition_broadcast(P)),
            (router[:, :, 0:NG], d["w_group"][0].rearrange("(k p) n -> p k n", p=P)),
            (router[:, :, NG:], d["w_router"][0].rearrange("(k p) n -> p k n", p=P)),
            (router_b[:, 0:NG], d["b_group"][0].partition_broadcast(P)),
            (router_b[:, NG:], d["b_router"][0].partition_broadcast(P)),
        ]
        for dst, src in late:
            sp.dma_start(dst, src).then_inc(late_loaded, 16)
        sp.dma_start(out["pool_sample"][0][:, 0:PH - STEP], d["state_pool"][0][:, STEP:PH]).then_inc(states_stored, 16)
        sp.dma_start(out["conv_sample"][0][:, 0:CH - STEP], d["state_conv"][0][:, STEP:CH]).then_inc(states_stored, 16)
        for n in range(2, len(pairs)):
            if n == FIRST_D1 + 2:
                sp.wait_ge(v_normed, NCH)
                sp.dma_start(out["chunk_v_sample"][0].rearrange("b i c -> (b i) c"), vn[0:NS, NCH - 1]).then_inc(outs_stored, 16)
                sp.wait_ge(act_took, A_G0 + 2)
                sp.dma_start(out["pool_prompt"][0][0], states[0:PH, 0]).then_inc(states_stored, 16)
                sp.dma_start(out["conv_prompt"][0][0], states[0:CH, 2]).then_inc(states_stored, 16)
                for b in range(NSEQ):
                    r = slice(b * STEP, (b + 1) * STEP)
                    sp.dma_start(out["pool_sample"][0][b, PH - STEP:PH], states[r, 1]).then_inc(states_stored, 16)
                    sp.dma_start(out["conv_sample"][0][b, CH - STEP:CH], states[r, 3]).then_inc(states_stored, 16)
            if n == FIRST_OUT + 2:
                sp.wait_ge(merged_done, KD)
                sp.dma_start(x[:, 0:4], d["x_prompt"][0].rearrange("(c p) n -> p c n", p=P)).then_inc(x_again, 16)
                sp.dma_start(x[0:NS, 4], d["x_sample"].rearrange("b i n -> (b i) n")).then_inc(x_again, 16)
                sp.dma_start(ffn_row, d["ffn_norm_g"][0].partition_broadcast(P)).then_inc(norm_rows_loaded, 16)
                sp.dma_start(final_row, d["final_norm_g"].partition_broadcast(P)).then_inc(norm_rows_loaded, 16)
            sp.wait_ge(low_ready, n - 1)
            rows = pairs[n].rearrange("(k p) n -> p k n", p=P)
            sp.dma_start(wring[n % 2][:, 0:rows.shape[1]], rows).then_inc(wring_loaded[n % 2], 16)

        def load_gate_up(e, s, m):
            sp.dma_start(gu[s][:, m].rearrange("p (h c) f -> p h (c f)", h=2), expert_gu(m, e)).then_inc(gu_loaded[s], 16)

        load_gate_up(1, 1, 0)
        sp.wait_ge(low_ready, len(pairs))
        sp.dma_start(dn[0].rearrange("p (h c) n -> p h (c n)", h=2), expert_dn(0)).then_inc(dn_loaded[0], 16)
        sp.wait_ge(product, N_O)
        load_gate_up(0, 0, 0)
        load_gate_up(0, 0, 1)
        for c in range(NCH):
            sp.wait_ge(xn2_done, c + 1)
            n = chunk_rows(c)
            sp.dma_start(xn2_dram[c * P:c * P + n], xn2[0:n, c]).then_inc(xn2_stored, 16)
        load_gate_up(1, 1, 1)
        sp.dma_start(dn[1].rearrange("p (h c) n -> p h (c n)", h=2), expert_dn(1)).then_inc(dn_loaded[1], 16)

        def load_expert(e, s, after):
            sp.wait_ge(gu_done, after)
            for m in range(2):
                sp.dma_start(gu[s][:, m].rearrange("p (h c) f -> p h (c f)", h=2), expert_gu(m, e)).then_inc(gu_loaded[s], 16)
            sp.wait_ge(dn_done, after)
            sp.dma_start(dn[s].rearrange("p (h c) n -> p h (c n)", h=2), expert_dn(e)).then_inc(dn_loaded[s], 16)

        with sp.Fori(1, NE // 2) as i:
            for s in range(2):
                load_expert(2 * i + s, s, 2 * i + s - 1)
        sp.wait_ge(routed, 1)
        n_over = sp.value_load(ovf[0:1, NOVF:NOVF + 1], min_val=0, max_val=NOVF)
        with sp.Fori(0, NOVF) as j:
            with sp.If(n_over > j):
                e = sp.value_load(ovf[0:1, bass.ds(j, 1)], min_val=0, max_val=NE - 1)
                load_expert(e, 0, NE + j)
        sp.wait_ge(gu_done, n_over + NE)
        sp.wait_ge(dn_done, n_over + NE)
        sp.wait_ge(scattered[0], n_over * 16 + 16 * (NE // 2))
        sp.wait_ge(scattered[1], 16 * (NE // 2))
        y_rows = y_dram.rearrange("(t f) n -> t (f n)", f=4)
        for c in range(NCH):
            n = chunk_rows(c)
            sp.dma_start(y_place(c)[0:n], y_rows[c * P:c * P + n]).then_inc(y_loaded[c], 16)
        for c in range(NCH):
            sp.wait_ge(final_done, c + 1)
            n = chunk_rows(c)
            dst = out["y_prompt"][0][c * P:(c + 1) * P] if c < NCH - 1 else out["y_sample"].rearrange("b i n -> (b i) n")
            sp.dma_start(dst, x[0:n, c]).then_inc(outs_stored, 16)
        sp.wait_ge(outs_stored, 16 * (1 + NCH))
        sp.wait_ge(states_stored, 16 * (4 + 2 * NSEQ))

    @block.tensor
    def _(pe):
        pe.wait_ge(const_loaded, 16)
        pe.wait_ge(param_loaded, 16 * 6)
        pe.transpose(ps[:, 6, 0:124], param_rows[0:124, 0], ident[0:124, 0:124])
        pe.transpose(ps[:, 6, 124:148], param_rows[0:24, 1], ident[0:24, 0:24]).then_inc(product, 1)
        for k in range(KD):
            if k == 0:
                pe.wait_ge(x_normed, NCH)
            if k == 3:
                pe.wait_ge(act_took, 1)
            if k >= 4:
                pe.wait_ge(dve_took, k - 3)
            for c in range(NCH):
                n = chunk_rows(c)
                last = pe.transpose(ps[:, 2 * (k % 4) + c // 4, (c % 4) * P:(c % 4) * P + n],
                                    x[0:n, c, k * P:(k + 1) * P], ident[0:n, 0:n])
            last.then_inc(product, 1)
        pe.wait_ge(rows_loaded, 16 * 4)
        pe.wait_ge(dve_took, 5)
        for q in range(KW):
            for a in range(2):
                last = pe.transpose(ps[:, q // 2, (q % 2) * 240 + a * 120:][:, 0:120],
                                    conv_rows[0:120, a, q * P:(q + 1) * P], ident[0:120, 0:120])
        last.then_inc(product, 1)
        pe.wait_ge(dve_took, 6)
        for q in range(KW):
            last = pe.transpose(ps[:, 2, q * 120:(q + 1) * 120], pool_rows[0:120, q * P:(q + 1) * P], ident[0:120, 0:120])
        last.then_inc(product, 1)
        pe.wait_ge(dve_took, 7)
        for h in range(KW):
            last = pe.transpose(ps[:, 4, h * P:(h + 1) * P], sgu_w_rows[:, h], ident)
        last.then_inc(product, 1)

        def column_tiles(s, rhs, kt, r, c):
            high, low = rhs
            for k in range(kt):
                for w, parts in ((w_high[s], (high, low)), (w_low[s], (high,))):
                    for half in range(2):
                        for part in parts:
                            last = pe.matmul(ps[:, 2 * r + half, 0:HT], w[:, k, c * P:(c + 1) * P],
                                             part[:, k, half * HT:(half + 1) * HT],
                                             start=(k == 0 and len(parts) == 2 and part is high),
                                             stop=(k == kt - 1 and len(parts) == 1))
            return last

        xs = (x_high, x_low)

        pe.wait_ge(act_took, A_SETUP)
        pe.wait_ge(dve_took, D_SETUP)
        with pe.Fori(0, 4) as i:
            for s in range(2):
                pe.wait_ge(low_ready, i * 2 + (s + 1))
                for c in range(2):
                    r = 2 * s + c
                    pe.wait_ge(act_took, i * 4 + (A_SETUP - 3 + r))
                    last = column_tiles(s, xs, KD, r, c)
                    last.then_inc(product, 1)

        def token_chunks(lhs, w, s):
            for c in range(NCH):
                n = chunk_rows(c)
                for k in range(KD):
                    last = pe.matmul(ps[0:n, c, s * 256:(s + 1) * 256], lhs[:, k, c * P:c * P + n], w[:, k],
                                     start=(k == 0), stop=(k == KD - 1))
                if s == 1:
                    last.then_inc(product, 1)
            if s == 0:
                last.then_inc(half_rows, 1)

        def token_chunks(lhs, s):
            high, low = lhs
            for c in range(NCH):
                n = chunk_rows(c)
                for k in range(KD):
                    for part, w in ((high, w_high[s]), (high, w_low[s]), (low, w_high[s])):
                        last = pe.matmul(ps[0:n, c, s * 256:(s + 1) * 256], part[:, k, c * P:c * P + n], w[:, k],
                                         start=(k == 0 and part is high and w is w_high[s]),
                                         stop=(k == KD - 1 and part is low))
                if s == 1:
                    last.then_inc(product, 1)
            if s == 0:
                last.then_inc(half_rows, 1)

        pe.wait_ge(act_took, A_PROJ)
        for s in range(2):
            pe.wait_ge(low_ready, 8 + s + 1)
            token_chunks(xs, s)

        for g in range(4):
            if g % 2 == 0:
                pe.wait_ge(low_ready, FIRST_G0 + g // 2 + 1)
            if g == 1:
                pe.wait_ge(act_took, A_V)
            column_tiles(g // 2, xs, KD, (g + 3) % 4, g % 2).then_inc(product, 1)

        for n, (rows, prompt, sample) in enumerate([
            (PH, lambda q: proj[:, 8 + q, SEQ - PH:SEQ], lambda q: proj[:, 8 + q, SEQ:T]),
            (CH, lambda q: cext[:, q, SEQ:SEQ + CH], lambda q: proj[:, q, SEQ:T]),
        ]):
            pe.wait_ge(act_took, A_V + 1 + n)
            if n == 1:
                pe.wait_ge(glu_done, 2 * KW)
            bank = (6, 0)[n]
            for q in range(KW):
                pe.transpose(ps[0:rows, bank, q * P:(q + 1) * P], prompt(q), ident)
                last = pe.transpose(ps[0:NS, bank + 1, q * P:(q + 1) * P], sample(q), ident)
            last.then_inc(product, 1)

        pe.wait_ge(act_took, A_G0)
        pe.wait_ge(v_normed, NCH)
        pe.wait_ge(step_loaded, 16 * NSEQ * KW)
        for h in range(KW):
            if h >= 2:
                pe.wait_ge(act_took, A_G0 + h - 1)
            for c in range(NCH - 1):
                last = pe.matmul(ps[:, 2 * ((h + 1) % 4), c * P:(c + 1) * P], vn[:, c, h * P:(h + 1) * P], wsT[:, h],
                                 start=True, stop=True)
            last.then_inc(product, 1)
        pe.wait_ge(dve_took, D_SETUP + 1)
        for h in range(KW):
            last = pe.matmul(ps[:, 2, h * NS:(h + 1) * NS], vn[0:NS, NCH - 1, h * P:(h + 1) * P], step_w[:, h],
                             start=True, stop=True)
        last.then_inc(product, 1)
        pe.wait_ge(pool_done, KW)
        pe.wait_ge(late_loaded, 16 * 8)
        for g in range(KW):
            r = (g + 2) % 4
            pe.wait_ge(dve_took, D_SETUP + g + 2)
            for half in range(2):
                last = pe.matmul(ps[:, 2 * r + half, 0:HT], pool_w[:, g], pool_d[:, g, half * HT:(half + 1) * HT],
                                 start=True, stop=True)
            last.then_inc(product, 1)

        def branches(i, first_slot):
            for b in range(4):
                if b % 2 == 0:
                    pe.wait_ge(low_ready, i * 4 + (FIRST_D1 + b // 2 + 1))
                if b == 2:
                    pe.wait_ge(sgu_low, KW)
                if first_slot == 0:
                    pe.wait_ge(act_took, i * 4 + (A_S - 3 + b))
                elif b < 3:
                    pe.wait_ge(act_took, A_D1 - 2 + b)
                else:
                    pe.wait_ge(dve_took, D_D1 + 1)
                column_tiles(b // 2, (y_high[b // 2], y_low[b // 2]), KW, (first_slot + b) % 4, b % 2).then_inc(product, 1)

        def channel_sum(r, src):
            for half in range(2):
                for q in range(KW):
                    last = pe.matmul(ps[:, 2 * r + half, 0:HT], const["ones"], src[:, q, half * HT:(half + 1) * HT],
                                     start=(q == 0), stop=(q == KW - 1))
            last.then_inc(product, 1)

        pe.wait_ge(dve_took, D_S)
        with pe.Fori(0, NJ - 1) as i:
            branches(i, 0)
            for g in range(4):
                if g % 2 == 0:
                    pe.wait_ge(low_ready, i * 4 + (FIRST_D1 + 2 + g // 2 + 1))
                pe.wait_ge(dve_took, i * 4 + (D_S + g + 1))
                column_tiles(g // 2, xs, KD, g, g % 2).then_inc(product, 1)
        pe.wait_ge(conv_done, 1)
        pe.wait_ge(act_took, A_D1 - 3)
        channel_sum(0, yc)
        branches(NJ - 1, 1)
        pe.wait_ge(squared, KW)
        pe.wait_ge(dve_took, D_D1 + 2)
        channel_sum(1, squares)

        with pe.Fori(0, NJ // 2) as i:
            for g in range(4):
                if g % 2 == 0:
                    pe.wait_ge(low_ready, i * 4 + (FIRST_D2 + g // 2 + 1))
                pe.wait_ge(dve_took, i * 4 + (D_D2 - 3 + g))
                column_tiles(g // 2, xs, KD, (g + 2) % 4, g % 2).then_inc(product, 1)
            pe.wait_ge(conv_low, KW)
            for b in range(4):
                if b % 2 == 0:
                    pe.wait_ge(low_ready, i * 4 + (FIRST_D2 + 2 + b // 2 + 1))
                pe.wait_ge(act_took, i * 4 + (A_D1 + b + 1))
                column_tiles(b // 2, (y_high[2], y_low[2]), KW, (b + 2) % 4, b % 2).then_inc(product, 1)

        pe.wait_ge(merged_low, KD)
        with pe.Fori(0, 2) as i:
            for s in range(2):
                pe.wait_ge(low_ready, i * 2 + (FIRST_OUT + s + 1))
                if s == 0:
                    pe.wait_ge(dve_took, i * NCH + D_B)
                token_chunks((m_high, m_low), s)

        pe.wait_ge(dve_took, D_O)
        pe.wait_ge(xn2_done, NCH)
        for k in range(KD):
            if k >= 4:
                pe.wait_ge(*((act_took, A_B + (k - 4) // 2 + 1) if k % 2 == 0 else (dve_took, D_O + (k - 4) // 2 + 1)))
            for c in range(NCH):
                n = chunk_rows(c)
                last = pe.transpose(ps[:, 2 * (k % 4) + c // 4, (c % 4) * P:(c % 4) * P + n],
                                    xn2[0:n, c, k * P:(k + 1) * P], ident[0:n, 0:n])
            last.then_inc(product, 1)
        pe.wait_ge(act_took, A_T)
        pe.wait_ge(dve_took, D_T)
        for c in range(NCH):
            n = chunk_rows(c)
            for k in range(KD):
                last = pe.matmul(ps[0:n, 0, c * (NG + NE):(c + 1) * (NG + NE)], xT[:, k, c * P:c * P + n],
                                 router[:, k], start=(k == 0), stop=(k == KD - 1))
        last.then_inc(product, 1)
        pe.wait_ge(chosen, 1)
        pe.matmul(ps[:, 2, 0:NCH * NE], const["before"], chosen_mask.rearrange("p c e -> p (c e)"), start=True, stop=True)
        pe.matmul(ps[:, 3, 0:NCH * NE], const["ones"], chosen_mask.rearrange("p c e -> p (c e)"),
                  start=True, stop=True).then_inc(product, 1)
        pe.wait_ge(tables_in, 2)
        for n, (pl, bl) in enumerate((at_place[k], in_block[k]) for k in range(2)):
            for c in range(NCH):
                last = pe.matmul(ps[:, 4, 0:2 * NBLK], pl[:, c], bl[:, c], start=(n == 0 and c == 0),
                                 stop=(n == 1 and c == NCH - 1))
        last.then_inc(product, 1)

        def turn_rows(e, s, turn, free):
            pe.wait_ge(xg_loaded[s], turn * 16 + 16)
            if free is not None:
                pe.wait_ge(xgT_ready, free)
            v = xg[s].rearrange("p (m c) -> p m c", c=4)
            for c in range(4):
                last = pe.transpose(ps[:, s, c * P:(c + 1) * P], v[:, :, c], ident)
            last.then_inc(xg_turned, 1)

        def gate_up(e, s, turn, free):
            pe.wait_ge(xgT_ready, e + 1)
            pe.wait_ge(gu_loaded[s], turn * 32 + 32)
            if free is not None:
                pe.wait_ge(hid_ready, free)
            for k in range(KD):
                for g in range(2):
                    last = pe.matmul(ps[g * CAP:(g + 1) * CAP, 2 + s].rearrange("p (m f) -> p m f", m=2),
                                     xgT[s][:, k % 4, (k // 4) * CAP:(k // 4 + 1) * CAP],
                                     gu[s][:, :, k, g * 256:(g + 1) * 256], start=(k == 0), stop=(k == KD - 1))
            last.then_inc(gu_done, 1)

        def turn_hidden(e, s, turn, free):
            pe.wait_ge(hid_ready, e + 1)
            if free is not None:
                pe.wait_ge(hT_ready, free)
            v = hid[s].rearrange("p (m c) -> p m c", c=2)
            for c in range(2):
                last = pe.transpose(ps[:, 4 + s, c * P:(c + 1) * P], v[:, :, c], ident)
            last.then_inc(hid_turned, 1)

        def down(e, s, turn, free):
            pe.wait_ge(hT_ready, e + 1)
            pe.wait_ge(dn_loaded[s], turn * 16 + 16)
            if free is not None:
                pe.wait_ge(yo_ready, free)
            for k in range(4):
                for g in range(2):
                    last = pe.matmul(ps[g * CAP:(g + 1) * CAP, 6 + s], hT[s][:, k % 2, (k // 2) * CAP:(k // 2 + 1) * CAP],
                                     dn[s][:, k, g * W:(g + 1) * W], start=(k == 0), stop=(k == 3))
            last.then_inc(dn_done, 1)

        pe.wait_ge(routed, 1)
        turn_rows(0, 0, 0, None)
        for e in range(2):
            gate_up(e, e, 0, None)
            turn_rows(e + 1, 1 - e, e, None if e == 0 else 1)
            turn_hidden(e, e, 0, None)
            down(e, e, 0, None)
        with pe.Fori(1, NE // 2 - 1) as i:
            for s in range(2):
                e, free = 2 * i + s, 2 * i + s - 1
                gate_up(e, s, i, free)
                turn_rows(e + 1, 1 - s, i + s, free + 1)
                turn_hidden(e, s, i, free)
                down(e, s, i, free)
        i = NE // 2 - 1
        for s in range(2):
            e, free = 2 * i + s, 2 * i + s - 1
            gate_up(e, s, i, free)
            if s == 0:
                turn_rows(e + 1, 1, i, free + 1)
            turn_hidden(e, s, i, free)
            down(e, s, i, free)
        n_over = pe.value_load(ovf[0:1, NOVF:NOVF + 1], min_val=0, max_val=NOVF)
        with pe.Fori(0, NOVF) as j:
            with pe.If(n_over > j):
                for stage in (turn_rows, gate_up, turn_hidden, down):
                    stage(NE + j, 0, NE // 2 + j, NE + j)

    @block.scalar
    def _(act):
        n_own = [0]

        def own(instruction):
            n_own[0] += 1
            instruction.then_inc(act_step, 1)
            act.wait_ge(act_step, n_own[0])

        def high_part(s, turn, kt=KD):
            act.wait_ge(wring_loaded[s], turn * 16 + 16)
            nc.scalar.copy(w_high[s][:, 0:kt], wring[s][:, 0:kt]).then_inc(high_ready, 1)

        act.wait_ge(x_loaded, 32)
        act.wait_ge(zeroed, 2)
        for c in range(NCH):
            n = chunk_rows(c)
            own(nc.scalar.activation(junk[0:n], x[0:n, c], ACT.Square, accum_out=stat[0:n, c:c + 1]))
        nc.scalar.copy(stat[:, 10:10 + NCH], stat[:, 0:NCH]).then_inc(mean_sq, 1)
        act.wait_ge(root_in, 1)
        nc.scalar.activation(stat[:, 5:5 + NCH], stat[:, 0:NCH], ACT.Sqrt).then_inc(root, 1)
        high_part(0, 0)
        high_part(1, 0)
        act.wait_ge(product, 1)
        nc.scalar.copy(param[:, TAP:TAP + 124], ps[:, 6, 0:124])
        nc.scalar.copy(param[:, 0:24], ps[:, 6, 124:148]).then_inc(act_took, 1)
        act.wait_ge(act_took, 1)
        for k in range(KD):
            act.wait_ge(product, 2 + k)
            nc.scalar.activation(x_high[:, k], slot_flat(k % 4), ACT.Identity, scale=param[:, MG + k:MG + k + 1]).then_inc(act_took, 1)
        act.wait_ge(product, 10)
        for q in range(KW):
            last = nc.scalar.copy(
                cext[:, q, CH + SEQ:].rearrange("p (b i) -> p b i", i=CH + STEP)[:, :, 0:CH],
                ps[:, q // 2, (q % 2) * 240:(q % 2) * 240 + 240].rearrange("p (b i) -> p b i", i=CH))
        last.then_inc(act_took, 1)

        def take_projections(lo, hi):
            with act.Fori(lo, hi) as i:
                for r in range(4):
                    act.wait_ge(product, i * 4 + (N_SETUP + r + 1))
                    nc.scalar.copy(halves_at(proj, i * 4 + r), slot(r)).then_inc(act_took, 1)
                    if r % 2 == 1:
                        high_part(r // 2, i + 1)

        take_projections(0, 2)
        act.wait_ge(act_took, A_SETUP + 8)
        for q in range(KW):
            nc.scalar.activation(proj[:, KW + q], proj[:, KW + q], ACT.Sigmoid).then_inc(glu_gate, 1)
        take_projections(2, 4)
        act.wait_ge(half_rows, 1)
        high_part(0, 5)
        for c in range(NCH):
            n = chunk_rows(c)
            act.wait_ge(product, N_PROJ + c + 1)
            nc.scalar.copy(vn[0:n, c], ps[0:n, c]).then_inc(act_took, 1)

        high_part(1, 5)

        def take_gate(g, r):
            return nc.scalar.activation(halves(gates[:, g]), slot(r), ACT.Sigmoid).then_inc(act_took, 1)

        for g in range(4):
            act.wait_ge(product, N_V + g + 1)
            take_gate(g, (g + 3) % 4)
            if g % 2 == 1:
                high_part(g // 2, 6, KW)
            if g == 0:
                act.wait_ge(root_in, 2)
                nc.scalar.activation(stat[:, 20:20 + NCH], stat[:, 15:15 + NCH], ACT.Sqrt).then_inc(root, 1)
        for n, rows in enumerate((PH, CH)):
            act.wait_ge(product, N_G0 + n + 1)
            bank = (6, 0)[n]
            nc.scalar.copy(states[0:rows, 2 * n], ps[0:rows, bank])
            nc.scalar.copy(states[0:NS, 2 * n + 1], ps[0:NS, bank + 1]).then_inc(act_took, 1)
        for g in range(KW):
            act.wait_ge(product, N_G0 + 7 + g + 1)
            nc.scalar.activation(halves(y_high[0][:, g]), slot((g + 2) % 4), ACT.Identity,
                                 scale=param[:, PSC + g:PSC + g + 1]).then_inc(act_took, 1)
        act.wait_ge(sgu_done, 2 * KW)
        for h in range(KW):
            nc.scalar.copy(y_high[1][:, h], yb[:, h]).then_inc(sgu_high, 1)
        with act.Fori(0, NJ - 1) as i:
            for b in range(2):
                act.wait_ge(product, i * 8 + (N_S + 2 * b + 2))
                high_part(b, i * 2 + 7)
            for g in range(4):
                act.wait_ge(product, i * 8 + (N_S + 4 + g + 1))
                act.wait_ge(dve_took, i * 4 + (D_S + g + 1))
                take_gate(g, g)
                if g % 2 == 1:
                    high_part(g // 2, i * 2 + 8, KW)
        for q in range(KW):
            act.wait_ge(*((centred, q + 1) if q < KW - 1 else (dve_took, D_D1 + 1)))
            nc.scalar.activation(squares[:, q], yc[:, q], ACT.Square).then_inc(squared, 1)
        for b in range(2):
            act.wait_ge(product, N_D1 + 1 + 2 * b + 2)
            high_part(b, FIRST_D2 // 2)
        act.wait_ge(dve_took, D_D2)
        nc.scalar.activation(row_a[:], row_a[:], ACT.Sqrt).then_inc(root, 1)
        for q in range(KW):
            act.wait_ge(swish_in, q + 1)
            if q >= 2:
                act.wait_ge(yc_done, q - 1)
            nc.scalar.activation(tmp[q % 2][:, 0:T], yc[:, q], ACT.Sigmoid).then_inc(swish_sig, 1)
        act.wait_ge(states_stored, 16 * (4 + 2 * NSEQ))
        for q in range(KW):
            act.wait_ge(yc_done, q + 1)
            nc.scalar.copy(y_high[2][:, q], yc[:, q]).then_inc(conv_high, 1)
        with act.Fori(0, NJ // 2) as i:
            for g in range(4):
                act.wait_ge(product, i * 8 + (N_D2 + g + 1))
                act.wait_ge(dve_took, i * 4 + (D_D2 - 3 + g))
                take_gate(g, (g + 2) % 4)
                if g % 2 == 1:
                    high_part(g // 2, i * 2 + (FIRST_D2 // 2 + 1), KW)
            for b in range(4):
                if b % 2 == 1:
                    act.wait_ge(product, i * 8 + (N_D2 + 4 + b + 1))
                    high_part(b // 2, i * 2 + (FIRST_D2 // 2 + 2))
                act.wait_ge(merged_done, i * 4 + b + 1)
                nc.scalar.copy(m_high[:, bass.ds(i * 4 + b, 1)].rearrange("p a t -> p (a t)"),
                               merged[:, bass.ds(i * 4 + b, 1)].rearrange("p a t -> p (a t)")).then_inc(merged_high, 1)
        act.wait_ge(half_rows, 2)
        high_part(0, FIRST_OUT // 2 + 1)
        act.wait_ge(product, N_B + NCH)
        high_part(1, FIRST_OUT // 2 + 1)

        for i in range(2):
            for c in range(NCH):
                n = chunk_rows(c)
                act.wait_ge(dve_took, D_B + i * NCH + c + 1)
                own(nc.scalar.activation(junk_h[0:n], x[0:n, c, i * W:(i + 1) * W], ACT.Square,
                                         accum_out=stat[0:n, 30 + i * NCH + c:][:, 0:1]))
        nc.scalar.copy(stat[:, 40:50], stat[:, 30:40]).then_inc(mean_sq, 1)
        act.wait_ge(root_in, 3)
        nc.scalar.activation(stat[:, 55:60], stat[:, 50:55], ACT.Sqrt).then_inc(root, 1)
        for k in range(0, KD, 2):
            act.wait_ge(product, N_O + k + 1)
            nc.scalar.copy(xT[:, k], slot_flat(k % 4)).then_inc(act_took, 1)
        act.wait_ge(exp_in, 1)
        nc.scalar.activation(group_exp, group_exp, ACT.Exp).then_inc(exp_done, 1)
        act.wait_ge(exp_in, 2)
        nc.scalar.activation(pair_exp, pair_exp, ACT.Exp).then_inc(exp_done, 1)

        def silu(e, s, turn, free):
            act.wait_ge(gu_done, e + 1)
            if free is not None:
                act.wait_ge(hid_ready, free)
            nc.scalar.activation(sig[s], ps[:, 2 + s, 0:256], ACT.Silu).then_inc(sig_ready, 1)

        def take_hidden(e, s, turn, free):
            act.wait_ge(hid_turned, e + 1)
            if free is not None:
                act.wait_ge(dn_done, free)
            nc.scalar.copy(hT[s].rearrange("p c m -> p (c m)"), ps[:, 4 + s, 0:256]).then_inc(hT_ready, 1)

        def take_output(e, s, turn, free):
            act.wait_ge(dn_done, e + 1)
            if free is not None:
                act.wait_ge(scattered[s], turn * 16)
            nc.scalar.copy(yo[s], ps[:, 6 + s]).then_inc(yo_ready, 1)

        for e in range(2):
            for stage in (silu, take_hidden, take_output):
                stage(e, e, 0, None)
        with act.Fori(1, NE // 2) as i:
            for s in range(2):
                for stage in (silu, take_hidden, take_output):
                    stage(2 * i + s, s, i, 2 * i + s - 1)
        act.wait_ge(routed, 1)
        n_over = act.value_load(ovf[0:1, NOVF:NOVF + 1], min_val=0, max_val=NOVF)
        with act.Fori(0, NOVF) as j:
            with act.If(n_over > j):
                for stage in (silu, take_hidden, take_output):
                    stage(NE + j, 0, NE // 2 + j, NE + j)

        for c in range(NCH):
            n = chunk_rows(c)
            act.wait_ge(summed, c + 1)
            own(nc.scalar.activation(flat_y[0:n, 0:D], x[0:n, c], ACT.Square, accum_out=stat[0:n, 60 + c:61 + c]))
            nc.scalar.activation(stat[0:n, 65 + c:66 + c], stat[0:n, 60 + c:61 + c], ACT.Sqrt,
                                 scale=1.0 / D, bias=stat[0:n, 95:96]).then_inc(final_root, 1)

    @block.vector
    def _(dve):
        v = nc.vector
        n_own = [0]

        def own(instruction):
            n_own[0] += 1
            instruction.then_inc(dve_step, 1)
            dve.wait_ge(dve_step, n_own[0])

        def wide(a, shape):
            return a.broadcast_to(shape)

        dve.wait_ge(mean_sq, 1)
        v.tensor_scalar(stat[:, 0:NCH], stat[:, 10:10 + NCH], 1.0 / D, EPS, ALU.mult, ALU.add).then_inc(root_in, 1)
        dve.wait_ge(root, 1)
        own(v.reciprocal(stat[:, 10:10 + NCH], stat[:, 5:5 + NCH]))
        for c in range(NCH):
            n = chunk_rows(c)
            v.tensor_scalar(x[0:n, c], x[0:n, c], stat[0:n, 10 + c:11 + c], None, ALU.mult).then_inc(x_normed, 1)
        for k in range(KD):
            dve.wait_ge(act_took, 1 + k + 1)
            v.scalar_tensor_tensor(x_low[:, k], slot_flat(k % 4), param[:, MG + k:MG + k + 1], x_high[:, k].bitcast(F32),
                                   ALU.mult, ALU.subtract).then_inc(dve_took, 1)
        dve.wait_ge(product, 11)
        v.tensor_copy(pool_hist.rearrange("p q t -> p (q t)"), ps[:, 2, 0:480]).then_inc(dve_took, 1)
        dve.wait_ge(product, 12)
        v.tensor_tensor(wsT, ps[:, 4].rearrange("p (h t) -> p h t", h=KW),
                        wide(const["causal"].unsqueeze(1), [P, KW, P]), ALU.mult).then_inc(dve_took, 1)
        dve.wait_ge(step_loaded, 16 * NSEQ * KW)
        own(v.tensor_tensor(step_w, step_w, wide(const["blocks"][0:NS].unsqueeze(1), [NS, KW, NS]), ALU.mult))

        dve.wait_ge(zeroed, 3)
        for q in range(KW):
            dve.wait_ge(glu_gate, q + 1)
            v.tensor_tensor(cext[:, q, CH:CH + SEQ], proj[:, q, 0:SEQ], proj[:, KW + q, 0:SEQ], ALU.mult).then_inc(glu_done, 1)
            v.tensor_tensor(proj[:, q, SEQ:T], proj[:, q, SEQ:T], proj[:, KW + q, SEQ:T], ALU.mult).then_inc(glu_done, 1)
            dve.wait_ge(glu_done, 2 * q + 2)
            own(v.tensor_copy(cext[:, q, CH + SEQ:].rearrange("p (b i) -> p b i", i=CH + STEP)[:, :, CH:],
                              proj[:, q, SEQ:T].rearrange("p (b i) -> p b i", i=STEP)))
        def tap(k, n_before):
            for q in range(KW):
                w = param[:, bass.ds(k * KW + (TAP + q), 1)]
                for part, (src, acc) in enumerate((
                    (cext[:, q, bass.ds(k, SEQ)], yc[:, q, 0:SEQ]),
                    (cext[:, q, CH + SEQ:].rearrange("p (b i) -> p b i", i=CH + STEP)[:, :, bass.ds(k, STEP)],
                     yc[:, q, SEQ:T].rearrange("p (b i) -> p b i", i=STEP)),
                )):
                    if n_before is None:
                        last = v.tensor_scalar(acc, src, w, param[:, CB + q:CB + q + 1], ALU.mult, ALU.add)
                    else:
                        dve.wait_ge(tap_step, n_before * (2 * KW) + (1 - 2 * KW + 2 * q + part))
                        last = v.scalar_tensor_tensor(acc, src, w, acc, ALU.mult, ALU.add)
                    last.then_inc(tap_step, 1)

        for k in range(EARLY_TAPS):
            tap(k, k if k else None)

        mv = stat[:, 96:106].rearrange("p (c m) -> p c m", m=2)
        bn6 = stat[:, 106:112]
        for c in range(NCH):
            n = chunk_rows(c)
            dve.wait_ge(act_took, A_PROJ + c + 1)
            own(v.bn_stats(bn6[0:n], vn[0:n, c]))
            own(v.bn_aggr(mv[0:n, c], bn6[0:n]))
        v.tensor_scalar(stat[:, 15:15 + NCH], mv[:, :, 1], EPS, None, ALU.add).then_inc(root_in, 1)
        dve.wait_ge(late_loaded, 16 * 8)
        dve.wait_ge(root, 2)
        own(v.reciprocal(stat[:, 25:25 + NCH], stat[:, 20:20 + NCH]))
        for c in range(NCH):
            n = chunk_rows(c)
            own(v.tensor_scalar(vn[0:n, c], vn[0:n, c], mv[0:n, c, 0:1], stat[0:n, 25 + c:26 + c], ALU.subtract, ALU.mult))
            own(v.tensor_tensor(vn[0:n, c], vn[0:n, c], sgu_rows[0:n, 0], ALU.mult))
            v.tensor_tensor(vn[0:n, c], vn[0:n, c], sgu_rows[0:n, 1], ALU.add).then_inc(v_normed, 1)

        for h in range(KW):
            dve.wait_ge(product, N_G0 + 2 + h + 1)
            v.tensor_tensor(yb[:, h, 0:SEQ].rearrange("p (c t) -> p c t", t=P),
                                ps[:, 2 * ((h + 1) % 4)].rearrange("p (c t) -> p c t", t=P),
                                wide(bias_rows[:, h:h + 1], [P, SEQ // P, P]), ALU.add).then_inc(dve_took, 1)
            dve.wait_ge(dve_took, D_SETUP + h + 1)
            v.tensor_tensor(yb[:, h, 0:SEQ], yb[:, h, 0:SEQ], proj[:, 3 * KW + h, 0:SEQ], ALU.mult).then_inc(sgu_done, 1)
        dve.wait_ge(product, N_G0 + 2 + KW + 1)
        for h in range(KW):
            last = (v.tensor_tensor(yb[:, h, SEQ:T].rearrange("p (b i) -> p b i", i=STEP),
                                ps[:, 2, h * NS:(h + 1) * NS].rearrange("p (b i) -> p b i", i=STEP),
                                wide(bias_rows[:, h:h + 1, 0:STEP], [P, NSEQ, STEP]), ALU.add))
        last.then_inc(dve_took, 1)
        dve.wait_ge(dve_took, D_SETUP + KW + 1)
        for h in range(KW):
            v.tensor_tensor(yb[:, h, SEQ:T], yb[:, h, SEQ:T], proj[:, 3 * KW + h, SEQ:T], ALU.mult).then_inc(sgu_done, 1)
        for g in range(KW):
            dve.wait_ge(act_took, A_S - KW + g + 1)
            v.scalar_tensor_tensor(halves(y_low[0][:, g]), slot((g + 2) % 4), param[:, PSC + g:PSC + g + 1],
                                   halves(y_high[0][:, g].bitcast(F32)), ALU.mult, ALU.subtract).then_inc(dve_took, 1)

        def merge(i, first_slot, taken):
            dve.wait_ge(act_took, i * 4 + A_S)
            for b in range(4):
                m = halves_at(merged, i * 2 + b % 2)
                t = halves(tmp[b % 2][:, 0:T])
                dve.wait_ge(product, i * 8 + (N_S + b + 1) if first_slot == 0 else N_D1 + 1 + b + 1)
                v.tensor_tensor(m if b < 2 else t, slot((first_slot + b) % 4), halves(gates[:, b]), ALU.mult).then_inc(dve_took, 1)
                if b >= 2:
                    dve.wait_ge(dve_took, i * 4 + (taken + b + 1))
                    v.tensor_tensor(m, m, t, ALU.add).then_inc(merged_part, 1)
            dve.wait_ge(merged_part, i * 2 + 2)

        dve.wait_ge(outs_stored, 16)
        with dve.Fori(0, NJ - 1) as i:
            merge(i, 0, D_S)
            for k in range(LATE_TAPS):
                tap(i * LATE_TAPS + (EARLY_TAPS + k), i * LATE_TAPS + (EARLY_TAPS + k))
        dve.wait_ge(tap_step, 2 * KW * TAPS)
        v.memset(stat[:, 95:96], EPS).then_inc(conv_done, 1)

        dve.wait_ge(product, N_D1 + 1)
        for q in range(KW):
            v.scalar_tensor_tensor(halves(yc[:, q]), slot(0), -1.0 / W, halves(yc[:, q]), ALU.mult, ALU.add).then_inc(
                centred if q < KW - 1 else dve_took, 1)
        merge(NJ - 1, 1, D_S + 1)
        dve.wait_ge(product, N_D2)
        v.tensor_scalar(halves(row_a[:]), slot(1), 1.0 / W, EPS, ALU.mult, ALU.add).then_inc(dve_took, 1)
        dve.wait_ge(root, 3)
        own(v.reciprocal(row_a[:], row_a[:]))
        for q in range(KW):
            own(v.tensor_tensor(yc[:, q], yc[:, q], row_a[:], ALU.mult))
            v.tensor_scalar(yc[:, q], yc[:, q], param[:, CG + q:CG + q + 1], param[:, CNB + q:CNB + q + 1],
                            ALU.mult, ALU.add).then_inc(swish_in, 1)
        for q in range(KW):
            dve.wait_ge(swish_sig, q + 1)
            dve.wait_ge(swish_in, q + 1)
            v.tensor_tensor(yc[:, q], yc[:, q], tmp[q % 2][:, 0:T], ALU.mult).then_inc(yc_done, 1)
        for q in range(KW):
            dve.wait_ge(conv_high, q + 1)
            v.tensor_tensor(y_low[2][:, q], yc[:, q], y_high[2][:, q].bitcast(F32), ALU.subtract).then_inc(conv_low, 1)
        with dve.Fori(0, NJ // 2) as i:
            for b in range(4):
                m = halves_at(merged, i * 4 + b)
                t = halves(tmp[b % 2][:, 0:T])
                dve.wait_ge(act_took, i * 4 + (A_D1 + b + 1))
                dve.wait_ge(product, i * 8 + (N_D2 + 4 + b + 1))
                v.tensor_tensor(t, slot((b + 2) % 4), halves(gates[:, b]), ALU.mult).then_inc(dve_took, 1)
                dve.wait_ge(dve_took, i * 4 + (D_D2 + b + 1))
                v.tensor_tensor(m, m, t, ALU.add).then_inc(merged_done, 1)
                dve.wait_ge(merged_high, i * 4 + b + 1)
                v.tensor_tensor(halves_at(m_low, i * 4 + b), m, halves_at(m_high, i * 4 + b).bitcast(F32),
                                ALU.subtract).then_inc(merged_low, 1)

        dve.wait_ge(merged_done, KD)
        dve.wait_ge(x_again, 32)
        for i in range(2):
            for c in range(NCH):
                n = chunk_rows(c)
                dve.wait_ge(product, N_B + i * NCH + c + 1)
                v.tensor_tensor(x[0:n, c, i * W:(i + 1) * W], ps[0:n, c], x[0:n, c, i * W:(i + 1) * W],
                                ALU.add).then_inc(dve_took, 1)
        dve.wait_ge(mean_sq, 2)
        own(v.tensor_tensor(stat[:, 50:55], stat[:, 40:45], stat[:, 45:50], ALU.add))
        v.tensor_scalar(stat[:, 50:55], stat[:, 50:55], 1.0 / D, EPS, ALU.mult, ALU.add).then_inc(root_in, 1)
        dve.wait_ge(root, 4)
        own(v.reciprocal(stat[:, 60:65], stat[:, 55:60]))
        dve.wait_ge(dve_took, D_O)
        dve.wait_ge(norm_rows_loaded, 32)
        for c in range(NCH):
            n = chunk_rows(c)
            v.scalar_tensor_tensor(xn2[0:n, c], x[0:n, c], stat[0:n, 60 + c:61 + c], ffn_row[0:n],
                                   ALU.mult, ALU.mult).then_inc(xn2_done, 1)
        own(v.memset(logits, 0.0))
        for k in range(1, KD, 2):
            dve.wait_ge(product, N_O + k + 1)
            v.tensor_copy(xT[:, k], slot_flat(k % 4)).then_inc(dve_took, 1)
        dve.wait_ge(product, N_T + 1)
        lg = ps[:, 0, 0:NCH * (NG + NE)].rearrange("p (c e) -> p c e", c=NCH)
        own(v.tensor_tensor(logits[:, 0:4], lg[:, 0:4], wide(router_b[:].unsqueeze(1), [P, 4, NG + NE]), ALU.add))
        own(v.tensor_tensor(logits[0:NS, 4], lg[0:NS, 4], router_b[0:NS], ALU.add))

        def s5(i):
            return small[:, i]

        def w5(i, n):
            return wide(small[:, i].unsqueeze(2), [P, NCH, n])

        def c5(name, n):
            return wide(const[name].unsqueeze(1), [P, NCH, n])

        gl, el = logits[:, :, 0:NG], logits[:, :, NG:]
        own(v.tensor_reduce(s5(1), gl, AX, ALU.max))
        v.tensor_tensor(group_exp, gl, w5(1, NG), ALU.subtract).then_inc(exp_in, 1)
        own(v.tensor_tensor(cand[:, :, 0:NG], gl, w5(1, NG), ALU.not_equal))
        own(v.scalar_tensor_tensor(cand[:, :, 0:NG], cand[:, :, 0:NG], 64.0, c5("group", NG), ALU.mult, ALU.add))
        own(v.tensor_reduce(s5(2), cand[:, :, 0:NG], AX, ALU.min))
        own(v.tensor_tensor(cand, c5("group_of", NE), w5(2, NE), ALU.is_equal))
        own(v.tensor_tensor(masked, el, cand, ALU.mult))
        own(v.tensor_scalar(cand, cand, -1.0, 1e30, ALU.add, ALU.mult))
        own(v.tensor_tensor(masked, masked, cand, ALU.add))
        for k in range(2):
            own(v.tensor_reduce(s5(3 + k), masked, AX, ALU.max))
            own(v.tensor_tensor(cand, masked, w5(3 + k, NE), ALU.not_equal))
            own(v.scalar_tensor_tensor(cand, cand, 64.0, c5("expert", NE), ALU.mult, ALU.add))
            own(v.tensor_reduce(s5(5 + k), cand, AX, ALU.min))
            own(v.tensor_tensor(one_hot[k], c5("expert", NE), w5(5 + k, NE), ALU.is_equal))
            if k == 0:
                own(v.scalar_tensor_tensor(masked, one_hot[0], -1e31, masked, ALU.mult, ALU.add))
        v.tensor_tensor(pair_exp, s5(4), s5(3), ALU.subtract).then_inc(exp_in, 1)
        own(v.tensor_tensor(chosen_mask, one_hot[0], one_hot[1], ALU.add))
        v.tensor_tensor(chosen_mask, chosen_mask, wide(const["valid"].unsqueeze(2), [P, NCH, NE]), ALU.mult).then_inc(chosen, 1)
        dve.wait_ge(exp_done, 2)
        own(v.tensor_reduce(s5(7), group_exp, AX, ALU.add))
        own(v.tensor_scalar(s5(8), pair_exp, 1.0, None, ALU.add))
        own(v.tensor_tensor(s5(7), s5(7), s5(8), ALU.mult))
        own(v.reciprocal(gate_of[:, 0], s5(7)))
        own(v.tensor_tensor(gate_of[:, 1], gate_of[:, 0], pair_exp, ALU.mult))
        dve.wait_ge(product, N_L + 1)
        own(v.memset(before_chunk[:, 0], 0.0))
        for c in range(NCH):
            own(v.tensor_tensor(before_chunk[:, c + 1], ps[:, 3, c * NE:(c + 1) * NE], before_chunk[:, c], ALU.add))
        own(v.tensor_tensor(rank, ps[:, 2, 0:NCH * NE].rearrange("p (c e) -> p c e", e=NE), before_chunk[:, 0:NCH], ALU.add))
        own(v.tensor_tensor(compare, wide(before_chunk[:, NCH].unsqueeze(2), [P, NE, MAXB]),
                            wide(const["steps"].unsqueeze(1), [P, NE, MAXB]), ALU.is_gt))
        own(v.tensor_reduce(further[:, 0], compare, AX, ALU.add))
        own(v.tensor_tensor_scan(further[:, 1], const["ones"][:, 0:NE], further[:, 0], 0.0, ALU.mult, ALU.add))
        own(v.tensor_tensor(further[:, 2], further[:, 1], further[:, 0], ALU.subtract))
        own(v.tensor_tensor(compare_e, wide(further[:, 1:2], [P, NOVF, NE]),
                            wide(const["further"].unsqueeze(2), [P, NOVF, NE]), ALU.is_le))
        own(v.tensor_reduce(at_further, compare_e, AX, ALU.add))
        own(v.tensor_scalar(ovf[:, 0:NOVF], at_further, float(NE - 1), None, ALU.min))
        own(v.tensor_copy(ovf[:, NOVF:], further[:, 1, NE - 1:NE]))
        for k in range(2):
            own(v.tensor_tensor(cand, one_hot[k], rank, ALU.mult))
            own(v.tensor_reduce(s5(9), cand, AX, ALU.add))
            own(v.tensor_tensor(cand, one_hot[k], wide(further[:, 2:3], [P, NCH, NE]), ALU.mult))
            own(v.tensor_reduce(s5(10), cand, AX, ALU.add))
            own(v.tensor_tensor(by_step, w5(9, MAXB), wide(const["steps"].unsqueeze(1), [P, NCH, MAXB]), ALU.is_ge))
            own(v.tensor_reduce(s5(11), by_step, AX, ALU.add))
            own(v.scalar_tensor_tensor(s5(12), s5(11), -float(CAP), s5(9), ALU.mult, ALU.add))
            own(v.tensor_tensor(s5(13), s5(10), s5(11), ALU.add))
            own(v.scalar_tensor_tensor(s5(13), s5(13), float(NE - 1), s5(5 + k), ALU.add, ALU.subtract))
            own(v.scalar_tensor_tensor(s5(13), s5(11), 0.0, s5(13), ALU.is_gt, ALU.mult))
            own(v.tensor_tensor(s5(13), s5(13), s5(5 + k), ALU.add))
            own(v.tensor_tensor(at_place[k], c5("place", P), w5(12, P), ALU.is_equal))
            if k == 0:
                own(v.tensor_scalar(s5(14), const["token2"], 2.0, -OFF, ALU.mult, ALU.add))
            else:
                own(v.tensor_scalar(s5(14), s5(14), 2.0, None, ALU.add))
            own(v.tensor_tensor(cand_b, c5("block", NBLK), w5(13, NBLK), ALU.is_equal))
            own(v.tensor_tensor(cand_b, cand_b, wide(const["valid"].unsqueeze(2), [P, NCH, NBLK]), ALU.mult))
            own(v.tensor_tensor(in_block[k][:, :, 0:NBLK], cand_b, wide(const["token2"].unsqueeze(2), [P, NCH, NBLK]), ALU.mult))
            v.tensor_tensor(in_block[k][:, :, NBLK:], cand_b, w5(14, NBLK), ALU.mult).then_inc(tables_in, 1)
            dve.wait_ge(tables_in, k + 1)
        dve.wait_ge(product, N_L + 2)
        own(v.tensor_scalar(gidx[:], ps[:, 4, 0:NBLK], const["half"], None, ALU.add))
        v.tensor_scalar(sidx[:], ps[:, 4, NBLK:2 * NBLK], const["half"], OFF, ALU.add, ALU.add).then_inc(routed, 1)

        def take_rows(e, s, turn, free):
            dve.wait_ge(xg_turned, e + 1)
            if free is not None:
                dve.wait_ge(gu_done, free)
            v.tensor_copy(xgT[s].rearrange("p c m -> p (c m)"), ps[:, s]).then_inc(xgT_ready, 1)

        def times_up(e, s, turn, free):
            dve.wait_ge(sig_ready, e + 1)
            if free is not None:
                dve.wait_ge(hid_turned, free)
            v.tensor_tensor(hid[s], sig[s], ps[:, 2 + s, 256:512], ALU.mult).then_inc(hid_ready, 1)

        dve.wait_ge(xn2_stored, 16 * NCH)
        take_rows(0, 0, 0, None)
        for e in range(2):
            take_rows(e + 1, 1 - e, e, None if e == 0 else 1)
            times_up(e, e, 0, None)
        with dve.Fori(1, NE // 2 - 1) as i:
            for s in range(2):
                take_rows(2 * i + s + 1, 1 - s, i + s, 2 * i + s)
                times_up(2 * i + s, s, i, 2 * i + s - 1)
        i = NE // 2 - 1
        take_rows(2 * i + 1, 1, i, 2 * i)
        times_up(2 * i, 0, i, 2 * i - 1)
        times_up(2 * i + 1, 1, i, 2 * i)
        n_over = dve.value_load(ovf[0:1, NOVF:NOVF + 1], min_val=0, max_val=NOVF)
        with dve.Fori(0, NOVF) as j:
            with dve.If(n_over > j):
                take_rows(NE + j, 0, NE // 2 + j, NE + j)
                times_up(NE + j, 0, NE // 2 + j, NE + j)

        own(v.memset(stat[:, 95:96], EPS))
        for c in range(NCH):
            n = chunk_rows(c)
            dve.wait_ge(y_loaded[c], 16)
            yr = y_place(c)[0:n].rearrange("p (k n) -> p k n", k=2)
            own(v.scalar_tensor_tensor(x[0:n, c], yr[:, 0], gate_of[0:n, 0, c:c + 1], x[0:n, c], ALU.mult, ALU.add))
            v.scalar_tensor_tensor(x[0:n, c], yr[:, 1], gate_of[0:n, 1, c:c + 1], x[0:n, c], ALU.mult, ALU.add).then_inc(summed, 1)
        for c in range(NCH):
            n = chunk_rows(c)
            dve.wait_ge(final_root, c + 1)
            own(v.reciprocal(stat[0:n, 70 + c:71 + c], stat[0:n, 65 + c:66 + c]))
            v.scalar_tensor_tensor(x[0:n, c], x[0:n, c], stat[0:n, 70 + c:71 + c], final_row[0:n], ALU.mult, ALU.mult).then_inc(final_done, 1)

    @block.gpsimd
    def _(pool):
        g = nc.gpsimd
        n_own = [0]

        def own(instruction):
            n_own[0] += 1
            instruction.then_inc(pool_step, 1)
            pool.wait_ge(pool_step, n_own[0])

        g.memset(step_w, 0.0).then_inc(zeroed, 1)
        g.memset(stat[:], 1.0).then_inc(zeroed, 1)
        g.memset(cext[:, :, 0:CH], 0.0).then_inc(zeroed, 1)

        def low_part(s, n, kt=KD):
            pool.wait_ge(high_ready, n + 1)
            g.tensor_tensor(w_low[s][:, 0:kt], wring[s][:, 0:kt], w_high[s][:, 0:kt].bitcast(F32), ALU.subtract).then_inc(low_ready, 1)

        def window_sums(q):
            pool.wait_ge(act_took, A_SETUP + 8 + q + 1)
            p_q = proj[:, 2 * KW + q]
            own(g.memset(tmp[0][:, 0:PH], 0.0))
            own(g.tensor_copy(tmp[0][:, PH:PH + SEQ], p_q[:, 0:SEQ]))
            ext = tmp[0][:, PH + SEQ:].rearrange("p (b i) -> p b i", i=PH + STEP)
            own(g.tensor_copy(ext[:, :, 0:PH], pool_hist[:, q].rearrange("p (b i) -> p b i", i=PH)))
            own(g.tensor_copy(ext[:, :, PH:], p_q[:, SEQ:T].rearrange("p (b i) -> p b i", i=STEP)))
            for level in range(q + 1):
                src, dst, shift = tmp[level % 2], tmp[(level + 1) % 2], 1 << level
                own(g.tensor_tensor(dst[:, shift:], src[:, shift:], src[:, 0:PEXT - shift], ALU.add))
                own(g.tensor_copy(dst[:, 0:shift], src[:, 0:shift]))

        def less_token(q):
            s = tmp[(q + 1) % 2]
            w = float(WINDOWS[q])
            own(g.tensor_scalar(pool_d[:, q, 0:SEQ], s[:, PH:PH + SEQ], 1 / w, None, ALU.mult))
            own(g.tensor_tensor(pool_d[:, q, 0:16], s[:, PH:PH + 16], const["count"][:, 16 * q:16 * q + 16], ALU.mult))
            own(g.tensor_scalar(pool_d[:, q, SEQ:T].rearrange("p (b i) -> p b i", i=STEP),
                                s[:, PH + SEQ:].rearrange("p (b i) -> p b i", i=PH + STEP)[:, :, PH:], 1 / w, None, ALU.mult))
            g.tensor_tensor(pool_d[:, q], pool_d[:, q], proj[:, 2 * KW + q], ALU.subtract).then_inc(pool_done, 1)

        for n in range(FIRST_D1):
            low_part(n % 2, n)
            if n == 6:
                pool.wait_ge(product, 12)
                pool.wait_ge(dve_took, D_SETUP)
            if n in (6, 7):
                window_sums(n - 6)
                less_token(n - 6)
            if n in (8, 10):
                window_sums(2 + (n - 8) // 2)
            if n in (9, 11):
                less_token(2 + (n - 9) // 2)
        for s in range(2):
            low_part(s, FIRST_D1 + s, KW)
        for h in range(KW):
            pool.wait_ge(sgu_high, h + 1)
            g.tensor_tensor(y_low[1][:, h], yb[:, h], y_high[1][:, h].bitcast(F32), ALU.subtract).then_inc(sgu_low, 1)
        with pool.Fori(0, NJ - 1) as i:
            for n in range(4):
                low_part(n % 2, i * 4 + (FIRST_D1 + 2 + n), KD if n < 2 else KW)
        for s in range(2):
            low_part(s, FIRST_D2 + s)
        with pool.Fori(0, NJ // 2) as i:
            for n in range(4):
                low_part(n % 2, i * 4 + (FIRST_D2 + 2 + n), KW if n < 2 else KD)
        for s in range(2):
            low_part(s, FIRST_OUT + 2 + s)

        def gather(e, s, turn, free):
            if free is not None:
                pool.wait_ge(xg_turned, free)
                pool.sem_inc(waits_met, 1)
            g.tensor_copy(idx_now[:, s:s + 1], gidx[:, bass.ds(e, 1)]).then_inc(gather_idx[s], 1)
            pool.wait_ge(gather_idx[s], turn + 1)
            pool.sem_inc(waits_met, 1)
            pool.indirect_dma_start(xg[s], None, xn2_dram.rearrange("t (h n) -> (t h) n", h=2),
                                    bass.IndirectOffsetOnAxis(ap=idx_now[:, s:s + 1], axis=0)).then_inc(xg_loaded[s], 16)

        def scatter(e, s, turn, free):
            if free is not None:
                pool.wait_ge(scattered[s], turn * 16)
                pool.sem_inc(waits_met, 1)
            g.tensor_copy(idx_now[:, 2 + s:3 + s], sidx[:, bass.ds(e, 1)]).then_inc(scatter_idx[s], 1)
            pool.wait_ge(scatter_idx[s], turn + 1)
            pool.wait_ge(yo_ready, e + 1)
            pool.sem_inc(waits_met, 1)
            pool.indirect_dma_start(y_dram, bass.IndirectOffsetOnAxis(ap=idx_now[:, 2 + s:3 + s], axis=0), yo[s], None,
                                    bounds_check=4 * T - 1, oob_is_err=False).then_inc(scattered[s], 16)

        pool.wait_ge(routed, 1)
        pool.wait_ge(xn2_stored, 16 * NCH)
        gather(0, 0, 0, None)
        gather(1, 1, 0, None)
        scatter(0, 0, 0, None)
        gather(2, 0, 1, 1)
        scatter(1, 1, 0, None)
        with pool.Fori(1, NE // 2 - 1) as i:
            for s in range(2):
                gather(2 * i + s + 1, 1 - s, i + s, 2 * i + s)
                scatter(2 * i + s, s, i, True)
        i = NE // 2 - 1
        gather(2 * i + 1, 1, i, 2 * i)
        scatter(2 * i, 0, i, True)
        scatter(2 * i + 1, 1, i, True)
        n_over = pool.value_load(ovf[0:1, NOVF:NOVF + 1], min_val=0, max_val=NOVF)
        with pool.Fori(0, NOVF) as j:
            with pool.If(n_over > j):
                gather(NE + j, 0, NE // 2 + j, NE + j)
                scatter(NE + j, 0, NE // 2 + j, True)


INPUTS = [
    "x_prompt", "x_sample", "state_pool", "state_conv", "mix_norm_g", "w_in", "pool_w", "pool_scale", "sgu_norm_g",
    "sgu_norm_b", "sgu_w", "sgu_b", "conv_w", "conv_b", "conv_norm_g", "conv_norm_b", "w_branch_pool",
    "w_branch_sgu", "w_branch_conv", "w_out", "ffn_norm_g", "w_group", "b_group", "w_router", "b_router",
    "w_gate_e", "w_up_e", "w_down_e", "final_norm_g",
]
OUTPUTS = [
    ("y_prompt", (1, SEQ, D)), ("y_sample", (NSEQ, STEP, D)), ("pool_prompt", (1, 1, PH, W)),
    ("pool_sample", (1, NSEQ, PH, W)), ("conv_prompt", (1, 1, CH, W)), ("conv_sample", (1, NSEQ, CH, W)),
    ("chunk_v_sample", (1, NSEQ, STEP, W)),
]


def kernel(**inputs):
    import concourse.bacc as bacc
    from concourse.bass_utils import run_bass_kernel_spmd

    nc = bacc.Bacc("TRN2", target_bir_lowering=False, num_devices=1)
    arrays = {name: np.ascontiguousarray(inputs[name]) for name in INPUTS}
    arrays["shape_constants"] = shape_constants()
    d = {name: nc.dram_tensor("in_" + name, a.shape, F32, kind="ExternalInput").ap() for name, a in arrays.items()}
    out = {name: nc.dram_tensor("out_" + name, shape, F32, kind="ExternalOutput").ap() for name, shape in OUTPUTS}
    build(nc, d, out)
    result = run_bass_kernel_spmd(nc, [{"in_" + name: a for name, a in arrays.items()}], core_ids=[0]).results[0]
    return tuple(result["out_" + name] for name, _ in OUTPUTS)
```

```python
from contextlib import ExitStack

import concourse.bass as bass
import concourse.mybir as mybir
import numpy as np
from concourse.alu_op_type import AluOpType as ALU

F32 = mybir.dt.float32
F32R = mybir.dt.float32r
I32 = mybir.dt.int32
ACT = mybir.ActivationFunctionType
AX = mybir.AxisListType.X

P = 128
D = 1024
KD = D // P
W = 512
KW = W // P
SEQ = 512
NSEQ, STEP = 8, 4
NS = NSEQ * STEP
T = SEQ + NS
HT = T // 2
NCH = SEQ // P + 1
PH, CH = 15, 30
TAPS = 31
WINDOWS = (2, 4, 8, 16)
NG, EPG, NE = 4, 8, 32
DE = 512
CAP = 64
MAXB = T // CAP
NOVF = (2 * T - 1) // CAP
NBLK = NE + NOVF
EPS = 1e-6
OFF = 8192.0
PEXT = PH + SEQ + NSEQ * (PH + STEP)
CEXT = CH + SEQ + NSEQ * (CH + STEP)


def chunk_rows(c):
    return P if c < NCH - 1 else NS


def _columns(parts):
    at, out = 0, {}
    for name, n in parts:
        out[name] = slice(at, at + n)
        at += n
    return out, at


CONST, NCONST = _columns([
    ("ident", P), ("causal", P), ("before", P), ("ones", P), ("blocks", NS),
    ("expert", NE), ("group_of", NE), ("group", NG), ("place", P), ("block", NBLK), ("gather_row", 2 * NCH), ("scatter_row", 2 * NCH),
    ("valid", NCH), ("half", 1), ("steps", MAXB), ("further", NOVF), ("count", NG * 16), ("pad", 1),
])


def shape_constants():
    c = np.zeros((P, NCONST), np.float32)
    p = np.arange(P)
    c[:, CONST["ident"]] = np.eye(P)
    c[:, CONST["causal"]] = p[:, None] <= p[None, :]
    c[:, CONST["before"]] = p[:, None] < p[None, :]
    c[:, CONST["ones"]] = 1
    s = np.arange(NS)
    c[:NS, CONST["blocks"]] = (s[:, None] // STEP == s[None, :] // STEP) & (s[:, None] <= s[None, :])
    c[:, CONST["expert"]] = np.arange(NE)
    c[:, CONST["group_of"]] = np.arange(NE) // EPG
    c[:, CONST["group"]] = np.arange(NG)
    c[:, CONST["place"]] = p % CAP
    c[:, CONST["block"]] = np.arange(NBLK)
    token = np.arange(NCH)[None, :] * P + p[:, None]
    for k in range(2):
        c[:, CONST["gather_row"].start + k * NCH:][:, :NCH] = (2 * token + 2) * (token < T)
        c[:, CONST["scatter_row"].start + k * NCH:][:, :NCH] = (4 * token + 2 * k + 2) * (token < T)
    c[:, CONST["valid"]] = token < T
    c[:, CONST["half"]] = (p >= CAP)[:, None]
    c[:, CONST["steps"]] = CAP * np.arange(1, MAXB + 1)
    c[:, CONST["further"]] = np.arange(NOVF)
    for g, w in enumerate(WINDOWS):
        c[:, CONST["count"].start + 16 * g:][:, :16] = 1 / np.minimum(np.arange(16) + 1, w)
    return c


def build(nc, d, out):
    ctx = ExitStack()
    with ctx:
        program(nc, d, out, ctx)


def program(nc, d, out, ctx):
    def sb(name, shape, dt=F32):
        return ctx.enter_context(nc.sbuf_tensor(name, shape, dt))

    def next_place():
        return (nc.sbuf_base + 31) // 32 * 32

    def over(name, shape, dt, tensor_at, first=0):
        return nc.alloc_sbuf_tensor_at(name, shape, dt, offset=tensor_at + 4 * first)

    def sem(name):
        return ctx.enter_context(nc.semaphore(name))

    ctx.enter_context(nc.allow_non_contiguous_dma(reason="block-diagonal corner of the SGU weights"))

    gu0_at = next_place()
    gu0 = sb("gu0", [P, 2, KD, DE])
    ring = sb("ring", [P, 4 * D])
    slot1_at = next_place()
    slot1 = sb("slot1", [P, 12 * D])
    xx_at = next_place()
    xx = sb("xx", [P, 2 * KD * T])
    xh = sb("xh", [P, NCH * D])
    ybr_at = next_place()
    MID = 4736
    work = sb("work", [P, 3 * KW * T + MID])
    cst = sb("cst", [P, NCONST])
    bias_rows = sb("bias_rows", [P, KW, P])
    pool_w = sb("pool_w", [P, KW, P])
    param = sb("param", [P, 160])
    row_a = sb("row_a", [P, T])
    router = sb("router", [P, KD, NG + NE])
    router_b = sb("router_b", [P, NG + NE])
    stat = sb("stat", [P, 112])
    gate_of = sb("gate_of", [P, 2, NCH])
    block_rows = sb("block_rows", [P, 2 * NBLK], I32)
    idx_now = sb("idx_now", [P, 4], I32)
    ovf = sb("ovf", [P, NOVF + 1], I32)
    ps = ctx.enter_context(nc.psum_tensor("ps", [P, 8, 512], F32))

    ybr = work[:, 0:3 * KW * T].rearrange("p (a q t) -> p a q t", a=3, t=T)
    mid = work[:, 3 * KW * T:]
    mid_at = ybr_at + 4 * 3 * KW * T

    w_high = [over(f"w_high{s}", [P, KD, 256], F32R, gu0_at, s * 2 * D) for s in range(2)]
    w_low = [over(f"w_low{s}", [P, KD, 256], F32R, gu0_at, (2 + s) * 2 * D) for s in range(2)]
    x_high = over("x_high", [P, KD, T], F32R, xx_at)
    x_low = over("x_low", [P, KD, T], F32R, xx_at, KD * T)
    y_high = [over(f"y_high{b}", [P, KW, T], F32R, slot1_at, q * KW * T) for b, q in enumerate((2, 0, 1))]
    y_low = [over(f"y_low{b}", [P, KW, T], F32R, ybr_at, b * KW * T) for b in range(3)]
    m_high = over("m_high", [P, KD, T], F32R, slot1_at, 12 * D - KD * T)
    m_low = over("m_low", [P, KD, T], F32R, mid_at)

    wring = [ring[:, s * 2 * D:(s + 1) * 2 * D].rearrange("p (k n) -> p k n", k=KD) for s in range(2)]
    late_rows = xx[:, KD * T:]
    gu = [m.rearrange("p (m k f) -> p m k f", m=2, k=KD) for m in (gu0[:].rearrange("p m k f -> p (m k f)"), slot1[:, 0:8 * D])]
    SPARE = (3 * KW * T + MID) // 2
    gu.append(work[:, 0:2 * SPARE].rearrange("p (m n) -> p m n", m=2)[:, :, 0:4 * D].rearrange("p m (k f) -> p m k f", k=KD))
    dn = [m.rearrange("p (k n) -> p k n", n=D) for m in (ring[:], slot1[:, 8 * D:12 * D], late_rows[:, 0:4 * D])]
    flat_y = work[:, 0:3 * KW * T]
    proj = slot1[:, 0:16 * T].rearrange("p (q t) -> p q t", t=T)
    cext = slot1[:, 16 * T:16 * T + KW * CEXT].rearrange("p (q t) -> p q t", t=CEXT)
    step_w = slot1[0:NS, 16 * T + KW * CEXT:][:, 0:KW * NS].rearrange("p (h s) -> p h s", s=NS)
    states = slot1[:, KW * T:KW * T + 4 * W].rearrange("p (q t) -> p q t", t=W)
    x = xh[:].rearrange("p (c n) -> p c n", n=D)
    squares = proj[:, 3 * KW:4 * KW]
    gates = xh[:, 0:4 * T].rearrange("p (q t) -> p q t", t=T)
    tmp = [xh[:, 4 * T + i * PEXT:][:, 0:PEXT] for i in range(2)]
    pool_hist = row_a[:, 0:KW * NSEQ * PH].rearrange("p (q t) -> p q t", t=NSEQ * PH)
    xT = xx[:, 0:KD * T].rearrange("p (k t) -> p k t", t=T)
    ffn_row = final_row = late_rows[:, 0:D]
    pool_d = mid[:, 0:KW * T].rearrange("p (q t) -> p q t", t=T)
    vn = mid[:, KW * T:KW * T + NCH * W].rearrange("p (c n) -> p c n", n=W)
    merged = mid[:, 0:KD * T].rearrange("p (q t) -> p q t", t=T)
    conv_rows = mid[:, 0:2 * W].rearrange("p (a n) -> p a n", n=W)
    pool_rows = mid[:, 2 * W:3 * W]
    sgu_w_rows = mid[:, 3 * W:4 * W].rearrange("p (h s) -> p h s", s=P)
    param_rows = mid[:, 4 * W:4 * W + 2 * P].rearrange("p (a n) -> p a n", n=P)
    junk = mid[:, 4 * W + 2 * P:4 * W + 2 * P + D]
    ya, yb, yc = (ybr[:, n] for n in range(3))
    sgu_rows = ybr[:, 1].rearrange("p q t -> p (q t)")[:, 0:2 * W].rearrange("p (a n) -> p a n", n=W)
    wsT = ybr[:, 1, KW - 1, 0:KW * P].rearrange("p (h t) -> p h t", t=P)
    xn2 = flat_y[:, 0:NCH * D].rearrange("p (c n) -> p c n", n=D)
    at = [0]

    def scratch(*shape):
        n = int(np.prod(shape))
        v = mid[:, at[0]:at[0] + n]
        at[0] += n
        assert at[0] <= MID
        if len(shape) == 2:
            v = v.rearrange("p (a b) -> p a b", b=shape[1])
        return v

    flat_x = xx[:, 0:KD * T]
    xg = [flat_x[:, s * 512:(s + 1) * 512] for s in range(2)]
    yo = [flat_x[:, 1024 + s * 512:][:, 0:512] for s in range(2)]
    hid = [flat_x[:, 2048 + s * 256:][:, 0:256] for s in range(2)]
    hT = [flat_x[:, 2560 + s * 256:][:, 0:256].rearrange("p (c m) -> p c m", c=2) for s in range(2)]
    sig = [flat_x[:, 3072 + s * 256:][:, 0:256] for s in range(2)]
    xgT = [work[:, SPARE + 4 * D + s * 512:][:, 0:512].rearrange("p (c m) -> p c m", c=4) for s in range(2)]

    const = {k: cst[:, v] for k, v in CONST.items()}
    ident = const["ident"]
    MG, PSC, CB, CG, CNB, TAP, FG = 0, 8, 12, 16, 20, 24, 24 + 4 * TAPS

    xn2_dram = nc.dram_tensor("xn2_rows", (T, D), F32, kind="Internal").ap()
    y_dram = nc.dram_tensor("expert_rows", (T * 2 * 2, W), F32, kind="Internal").ap()

    def slot(r):
        return ps[:, 2 * r:2 * r + 2, 0:HT]

    def slot_flat(r, n=T):
        return ps[:, 2 * r:2 * r + 2, :].rearrange("p b n -> p (b n)")[:, 0:n]

    def halves(v):
        return v.rearrange("p (b n) -> p b n", b=2)

    def y_place(c):
        if c < 4:
            return gu0[:].rearrange("p m k f -> p (m k f)")[:, c * 2 * D:(c + 1) * 2 * D]
        return slot1[:, 0:2 * D]

    def halves_at(t, q):
        return t[:, bass.ds(q, 1)].rearrange("p a (b n) -> p (a b) n", b=2)

    logits = scratch(NCH, NG + NE)
    group_exp = scratch(NCH, NG)
    cand = scratch(NCH, NE)
    masked = scratch(NCH, NE)
    both_hot = scratch(2 * NCH, NE)
    one_hot = [both_hot[:, k * NCH:(k + 1) * NCH] for k in range(2)]
    chosen_mask = scratch(NCH, NE)
    rank = scratch(NCH, NE)
    before_chunk = scratch(NCH + 1, NE)
    small = scratch(40, NCH)
    pair_exp = small[:, 0]
    at_place = over("at_place", [P, 2 * NCH, P], F32R, mid_at, at[0])[:]
    scratch(2 * NCH, P)
    in_block = over("in_block", [P, 2 * NCH, 2 * NBLK], F32R, xx_at)[:]
    assert 4 * T < 1 << 13
    junk_h = bias_rows[:].rearrange("p h t -> p (h t)")
    further = scratch(4, NE)
    compare = scratch(NE, MAXB)
    compare_e = scratch(NOVF, NE)
    at_further = scratch(1, NOVF)[:, 0]
    both_cand = scratch(2 * NCH, NE)
    cand_b = scratch(2 * NCH, NBLK)
    by_step = scratch(2 * NCH, MAXB)
    both = scratch(5, 2 * NCH)
    empty = cand_b[:, 0:2].rearrange("p a b -> p (a b)")

    x_loaded = [sem(f"x_loaded{c}") for c in range(NCH)]
    const_loaded = sem("const_loaded")
    param_loaded = sem("param_loaded")
    rows_loaded = sem("rows_loaded")
    late_loaded = sem("late_loaded")
    norm_rows_loaded = sem("norm_rows_loaded")
    high_ready = sem("high_ready")
    low_ready = sem("low_ready")
    step_loaded = sem("step_loaded")
    zeroed = sem("zeroed")
    wring_loaded = [sem(f"wring_loaded{s}") for s in range(2)]
    half_rows = sem("half_rows")
    product = sem("product")
    act_took = sem("act_took")
    dve_took = sem("dve_took")
    act_step = sem("act_step")
    dve_step = sem("dve_step")
    pool_step = sem("pool_step")
    mean_sq = sem("mean_sq")
    root = sem("root")
    root_in = sem("root_in")
    x_normed = sem("x_normed")
    glu_gate = sem("glu_gate")
    glu_done = sem("glu_done")
    pool_done = sem("pool_done")
    v_normed = sem("v_normed")
    sgu_done = sem("sgu_done")
    centred = sem("centred")
    squared = sem("squared")
    swish_in = sem("swish_in")
    swish_sig = sem("swish_sig")
    yc_done = sem("yc_done")
    merged_done = sem("merged_done")
    x_again = sem("x_again")
    merged_part = sem("merged_part")
    merged_high = sem("merged_high")
    merged_low = sem("merged_low")
    sgu_high = sem("sgu_high")
    sgu_low = sem("sgu_low")
    conv_high = sem("conv_high")
    conv_low = sem("conv_low")
    tap_step = sem("tap_step")
    xn2_done = sem("xn2_done")
    rstd_in = sem("rstd_in")
    h_scaled = sem("h_scaled")
    xn2_stored = sem("xn2_stored")
    exp_in = sem("exp_in")
    exp_done = sem("exp_done")
    chosen = sem("chosen")
    tables_in = sem("tables_in")
    routed = sem("routed")
    states_stored = sem("states_stored")
    outs_stored = sem("outs_stored")
    gu_loaded = [sem(f"gu_loaded{s}") for s in range(3)]
    dn_loaded = [sem(f"dn_loaded{s}") for s in range(3)]
    xg_loaded = [sem(f"xg_loaded{s}") for s in range(2)]
    waits_met = sem("waits_met")
    scattered = [sem(f"scattered{s}") for s in range(2)]
    xg_turned = sem("xg_turned")
    xgT_ready = sem("xgT_ready")
    gu_done = sem("gu_done")
    sig_ready = sem("sig_ready")
    hid_ready = sem("hid_ready")
    hid_turned = sem("hid_turned")
    hT_ready = sem("hT_ready")
    dn_done = sem("dn_done")
    yo_ready = sem("yo_ready")
    gather_idx = [sem(f"gather_idx{s}") for s in range(2)]
    scatter_idx = [sem(f"scatter_idx{s}") for s in range(2)]
    y_loaded = [sem(f"y_loaded{c}") for c in range(NCH)]
    summed = sem("summed")
    final_root = sem("final_root")
    final_done = sem("final_done")
    pool_summed = sem("pool_summed")

    block = ctx.enter_context(nc.Block())

    N_SETUP = KD + 4
    A_SETUP, D_SETUP = KD + 3, KD + 1
    N_PROJ, A_PROJ = N_SETUP + 16, A_SETUP + 16
    N_V, A_V = N_PROJ + NCH, A_PROJ + NCH
    N_G0, A_G0 = N_V + 4, A_V + 4
    N_S, A_S, D_S = N_G0 + 11, A_G0 + 2 + KW, D_SETUP + 5 + KW
    NJ = D // (2 * P)
    N_D1, A_D1, D_D1 = N_S + 8 * (NJ - 1), A_S + 4 * (NJ - 1), D_S + 4 * (NJ - 1)
    N_D2, D_D2 = N_D1 + 6, D_D1 + 6
    N_B, A_B, D_B = N_D2 + 16, A_D1 + 8, D_D2 + 8
    N_O, D_O = N_B + 2 * NCH, D_B + 2 * NCH
    N_T, A_T, D_T = N_O + KD, A_B + KD // 2, D_O + KD // 2
    N_L = N_T + 2

    w_in = d["w_in"][0]
    proj_cols = [3 * W, 3 * W + 256, 4 * W, 4 * W + 256, 0, 256, W, W + 256, 2 * W, 2 * W + 256]

    def gate_pair(b, j):
        return w_in[:, 5 * W + b * D + j * 256:][:, 0:256]

    def branch_pair(b, j):
        return d[("w_branch_pool", "w_branch_sgu", "w_branch_conv")[b]][0][:, j * 256:(j + 1) * 256]

    pairs = [w_in[:, c:c + 256] for c in proj_cols] + [gate_pair(b, 0) for b in range(2)]
    for j in range(NJ):
        pairs += [branch_pair(b, j) for b in range(2)]
        if j + 1 < NJ:
            pairs += [gate_pair(b, j + 1) for b in range(2)]
    for i in range(NJ // 2):
        pairs += [gate_pair(2, 2 * i + c) for c in range(2)] + [branch_pair(2, 2 * i + c) for c in range(2)]
    pairs += [d["w_out"][0][:, j * 256:(j + 1) * 256] for j in range(4)]
    FIRST_G0, FIRST_D1, FIRST_D2 = 10, 12, 12 + 4 * NJ - 2
    FIRST_OUT = len(pairs) - 4
    LATE_TAPS = 3
    EARLY_TAPS = TAPS - LATE_TAPS * (NJ - 1)

    FINAL_ORDER = (0, 1, 2, 3, 4)

    logit_halves = [(slice(0, NG + NE), slice(0, 2 * P)), (slice(CAP, CAP + NG + NE), slice(2 * P, T))]

    def expert_gu(m, e):
        w = d["w_gate_e" if m == 0 else "w_up_e"][0]
        return w[bass.ds(e, 1)].rearrange("e (h p c) f -> p (e h) (c f)", h=2, c=4)

    def expert_dn(e):
        return d["w_down_e"][0][bass.ds(e, 1)].rearrange("e (h p c) n -> p (e h) (c n)", h=2, c=2)

    @block.sync
    def _(sp):
        for c in range(NCH):
            src = d["x_prompt"][0][c * P:(c + 1) * P] if c < NCH - 1 else d["x_sample"].rearrange("b i n -> (b i) n")
            sp.dma_start(x[0:chunk_rows(c), c], src).then_inc(x_loaded[c], 16)
        sp.dma_start(cst[:], d["shape_constants"]).then_inc(const_loaded, 16)
        sp.dma_start(param_rows[0:124, 0], d["conv_w"][0].rearrange("k (q c) -> (k q) c", c=P)).then_inc(param_loaded, 16)
        for first, name in ((MG, "mix_norm_g"), (PSC, "pool_scale"), (CB, "conv_b"), (CG, "conv_norm_g"),
                            (CNB, "conv_norm_b"), (24, "ffn_norm_g")):
            rows = d[name][0].rearrange("(k c) -> k c", c=P)
            sp.dma_start(param_rows[first:first + rows.shape[0], 1], rows).then_inc(param_loaded, 16)
        for n in range(2):
            sp.dma_start(wring[n], pairs[n].rearrange("(k p) n -> p k n", p=P)).then_inc(wring_loaded[n], 16)
        for a in range(2):
            sp.dma_start(conv_rows[0:120, a], d["state_conv"][0][4 * a:4 * a + 4].rearrange("b i c -> (b i) c")).then_inc(rows_loaded, 16)
        sp.dma_start(pool_rows[0:120], d["state_pool"][0].rearrange("b i c -> (b i) c")).then_inc(rows_loaded, 16)
        sp.dma_start(sgu_w_rows, d["sgu_w"][0].rearrange("h t s -> t h s")).then_inc(rows_loaded, 16)
        sp.wait_ge(zeroed, 1)
        for b in range(NSEQ):
            for h in range(KW):
                sp.dma_start(step_w[b * STEP:(b + 1) * STEP, h, b * STEP:(b + 1) * STEP],
                             d["sgu_w"][0][h, 0:STEP, 0:STEP].rearrange("t s -> s t")).then_inc(step_loaded, 16)
        late = [
            (pool_w[:], d["pool_w"][0].rearrange("g c n -> c g n")),
            (sgu_rows[:, 0], d["sgu_norm_g"][0].partition_broadcast(P)),
            (sgu_rows[:, 1], d["sgu_norm_b"][0].partition_broadcast(P)),
            (bias_rows[:], d["sgu_b"][0].partition_broadcast(P)),
            (router[:, :, 0:NG], d["w_group"][0].rearrange("(k p) n -> p k n", p=P)),
            (router[:, :, NG:], d["w_router"][0].rearrange("(k p) n -> p k n", p=P)),
            (router_b[:, 0:NG], d["b_group"][0].partition_broadcast(P)),
            (router_b[:, NG:], d["b_router"][0].partition_broadcast(P)),
        ]
        for dst, src in late:
            sp.dma_start(dst, src).then_inc(late_loaded, 16)
        sp.dma_start(out["pool_sample"][0][:, 0:PH - STEP], d["state_pool"][0][:, STEP:PH]).then_inc(states_stored, 16)
        sp.dma_start(out["conv_sample"][0][:, 0:CH - STEP], d["state_conv"][0][:, STEP:CH]).then_inc(states_stored, 16)
        for n in range(2, len(pairs)):
            if n == FIRST_D1 + 2:
                sp.wait_ge(v_normed, NCH)
                sp.dma_start(out["chunk_v_sample"][0].rearrange("b i c -> (b i) c"), vn[0:NS, NCH - 1]).then_inc(outs_stored, 16)
                sp.wait_ge(act_took, A_G0 + 2)
                sp.dma_start(out["pool_prompt"][0][0], states[0:PH, 0]).then_inc(states_stored, 16)
                sp.dma_start(out["conv_prompt"][0][0], states[0:CH, 2]).then_inc(states_stored, 16)
                for b in range(NSEQ):
                    r = slice(b * STEP, (b + 1) * STEP)
                    sp.dma_start(out["pool_sample"][0][b, PH - STEP:PH], states[r, 1]).then_inc(states_stored, 16)
                    sp.dma_start(out["conv_sample"][0][b, CH - STEP:CH], states[r, 3]).then_inc(states_stored, 16)
            if n == FIRST_OUT + 2:
                sp.wait_ge(merged_done, KD)
                sp.dma_start(x[:, 0:4], d["x_prompt"][0].rearrange("(c p) n -> p c n", p=P)).then_inc(x_again, 16)
                sp.dma_start(x[0:NS, 4], d["x_sample"].rearrange("b i n -> (b i) n")).then_inc(x_again, 16)
                sp.dma_start(ffn_row, d["ffn_norm_g"][0].partition_broadcast(P)).then_inc(norm_rows_loaded, 16)
            sp.wait_ge(low_ready, n - 1)
            rows = pairs[n].rearrange("(k p) n -> p k n", p=P)
            sp.dma_start(wring[n % 2][:, 0:rows.shape[1]], rows).then_inc(wring_loaded[n % 2], 16)

        def load_gate_up(e, s, m):
            rows = gu[s][:, m].rearrange("p (h c) f -> p h (c f)", h=2)
            sp.dma_start(rows, expert_gu(m, e)).then_inc(gu_loaded[s], 16)

        def load_down(e, s):
            sp.dma_start(dn[s].rearrange("p (h c) n -> p h (c n)", h=2), expert_dn(e)).then_inc(dn_loaded[s], 16)

        load_gate_up(1, 1, 0)
        sp.wait_ge(low_ready, len(pairs))
        load_down(0, 0)
        sp.wait_ge(product, N_O)
        load_gate_up(0, 0, 0)
        load_gate_up(0, 0, 1)
        load_gate_up(1, 1, 1)
        load_down(1, 1)
        for c in range(NCH):
            sp.wait_ge(xn2_done, c + 1)
            n = chunk_rows(c)
            sp.dma_start(xn2_dram[c * P:c * P + n], xn2[0:n, c]).then_inc(xn2_stored, 16)
        load_down(2, 2)
        sp.wait_ge(xn2_stored, 16 * NCH)
        for c in range(2):
            sp.wait_ge(xg_loaded[c], 16)
        for m in range(2):
            load_gate_up(2, 2, m)

        def load_expert(e, s, after):
            sp.wait_ge(gu_done, after)
            for m in range(2):
                load_gate_up(e, s, m)
            sp.wait_ge(dn_done, after)
            load_down(e, s)

        for s in range(2):
            load_expert(3 + s, s, 1 + s)
        sp.wait_ge(dn_done, 3)
        sp.dma_start(final_row, d["final_norm_g"].partition_broadcast(P)).then_inc(norm_rows_loaded, 16)
        with sp.Fori(0, NE // 2 - 3) as i:
            for s in range(2):
                load_expert(2 * i + 5 + s, s, 2 * i + 4 + s)
        load_expert(NE - 1, 0, NE - 2)
        n_over = sp.value_load(ovf[0:1, NOVF:NOVF + 1], min_val=0, max_val=NOVF)
        with sp.Fori(0, NOVF) as j:
            with sp.If(n_over > j):
                e = sp.value_load(ovf[0:1, bass.ds(j, 1)], min_val=0, max_val=NE - 1)
                load_expert(e, 0, NE + j)
        sp.wait_ge(gu_done, n_over + NE)
        sp.wait_ge(dn_done, n_over + NE)
        sp.wait_ge(scattered[0], n_over * 16 + 16 * (NE // 2))
        sp.wait_ge(scattered[1], 16 * (NE // 2))
        y_rows = y_dram.rearrange("(t f) n -> t (f n)", f=4)
        for c in (4, 0, 1, 2, 3):
            n = chunk_rows(c)
            sp.dma_start(y_place(c)[0:n], y_rows[c * P:c * P + n]).then_inc(y_loaded[c], 16)
        for i, c in enumerate(FINAL_ORDER):
            sp.wait_ge(final_done, i + 1)
            n = chunk_rows(c)
            dst = out["y_prompt"][0][c * P:(c + 1) * P] if c < NCH - 1 else out["y_sample"].rearrange("b i n -> (b i) n")
            sp.dma_start(dst, x[0:n, c]).then_inc(outs_stored, 16)
        sp.wait_ge(outs_stored, 16 * (1 + NCH))
        sp.wait_ge(states_stored, 16 * (4 + 2 * NSEQ))

    @block.tensor
    def _(pe):
        pe.wait_ge(const_loaded, 16)
        pe.wait_ge(param_loaded, 16 * 7)
        pe.transpose(ps[:, 6, 0:124], param_rows[0:124, 0], ident[0:124, 0:124])
        pe.transpose(ps[:, 6, 124:124 + 32], param_rows[0:32, 1], ident[0:32, 0:32]).then_inc(product, 1)
        pe.wait_ge(x_normed, NCH)
        for k in range(KD):
            if k == 3:
                pe.wait_ge(act_took, 1)
            if k >= 4:
                pe.wait_ge(dve_took, k - 3)
            for c in range(NCH):
                n = chunk_rows(c)
                last = pe.transpose(ps[:, 2 * (k % 4) + c // 4, (c % 4) * P:(c % 4) * P + n],
                                    x[0:n, c, k * P:(k + 1) * P], ident[0:n, 0:n])
            last.then_inc(product, 1)
        pe.wait_ge(rows_loaded, 16 * 4)
        pe.wait_ge(dve_took, KD - 1)
        for q in range(KW):
            for a in range(2):
                last = pe.transpose(ps[:, 4 + q // 2, (q % 2) * 240 + a * 120:][:, 0:120],
                                    conv_rows[0:120, a, q * P:(q + 1) * P], ident[0:120, 0:120])
        last.then_inc(product, 1)
        pe.wait_ge(dve_took, KD)
        for q in range(KW):
            last = pe.transpose(ps[:, 6, q * 120:(q + 1) * 120], pool_rows[0:120, q * P:(q + 1) * P], ident[0:120, 0:120])
        last.then_inc(product, 1)
        for h in range(KW):
            last = pe.transpose(ps[:, 7, h * P:(h + 1) * P], sgu_w_rows[:, h], ident)
        last.then_inc(product, 1)

        def column_tiles(s, rhs, kt, r, c):
            high, low = rhs
            for k in range(kt):
                for w, parts in ((w_high[s], (high, low)), (w_low[s], (high,))):
                    for half in range(2):
                        for part in parts:
                            last = pe.matmul(ps[:, 2 * r + half, 0:HT], w[:, k, c * P:(c + 1) * P],
                                             part[:, k, half * HT:(half + 1) * HT],
                                             start=(k == 0 and len(parts) == 2 and part is high),
                                             stop=(k == kt - 1 and len(parts) == 1))
            return last

        xs = (x_high, x_low)

        with pe.Fori(0, 4) as i:
            for s in range(2):
                pe.wait_ge(low_ready, i * 2 + (s + 1))
                for c in range(2):
                    r = 2 * s + c
                    pe.wait_ge(act_took, i * 4 + (A_SETUP - 3 + r))
                    if r == 3:
                        pe.wait_ge(dve_took, D_SETUP)
                    last = column_tiles(s, xs, KD, r, c)
                    last.then_inc(product, 1)

        def token_chunks(lhs, w, s):
            for c in range(NCH):
                n = chunk_rows(c)
                for k in range(KD):
                    last = pe.matmul(ps[0:n, c, s * 256:(s + 1) * 256], lhs[:, k, c * P:c * P + n], w[:, k],
                                     start=(k == 0), stop=(k == KD - 1))
                if s == 1:
                    last.then_inc(product, 1)
            if s == 0:
                last.then_inc(half_rows, 1)

        def token_chunks(lhs, s, tiles_ready=None):
            high, low = lhs
            for c in range(NCH):
                n = chunk_rows(c)
                for k in range(KD):
                    if c == 0 and k >= KD - 2 and tiles_ready is not None:
                        pe.wait_ge(tiles_ready, k + 1)
                    for part, w in ((high, w_high[s]), (high, w_low[s]), (low, w_high[s])):
                        last = pe.matmul(ps[0:n, c, s * 256:(s + 1) * 256], part[:, k, c * P:c * P + n], w[:, k],
                                         start=(k == 0 and part is high and w is w_high[s]),
                                         stop=(k == KD - 1 and part is low))
                if s == 1:
                    last.then_inc(product, 1)
            if s == 0:
                last.then_inc(half_rows, 1)

        pe.wait_ge(act_took, A_PROJ)
        for s in range(2):
            pe.wait_ge(low_ready, 8 + s + 1)
            token_chunks(xs, s)

        for g in range(4):
            if g % 2 == 0:
                pe.wait_ge(low_ready, FIRST_G0 + g // 2 + 1)
            if g == 1:
                pe.wait_ge(act_took, A_V)
            column_tiles(g // 2, xs, KD, (g + 3) % 4, g % 2).then_inc(product, 1)

        for n, (rows, prompt, sample) in enumerate([
            (PH, lambda q: proj[:, 8 + q, SEQ - PH:SEQ], lambda q: proj[:, 8 + q, SEQ:T]),
            (CH, lambda q: cext[:, q, SEQ:SEQ + CH], lambda q: proj[:, q, SEQ:T]),
        ]):
            pe.wait_ge(act_took, A_V + 1 + n)
            if n == 1:
                pe.wait_ge(glu_done, 2 * KW)
            bank = (6, 0)[n]
            for q in range(KW):
                pe.transpose(ps[0:rows, bank, q * P:(q + 1) * P], prompt(q), ident)
                last = pe.transpose(ps[0:NS, bank + 1, q * P:(q + 1) * P], sample(q), ident)
            last.then_inc(product, 1)

        pe.wait_ge(act_took, A_G0)
        pe.wait_ge(v_normed, NCH)
        pe.wait_ge(step_loaded, 16 * NSEQ * KW)
        for h in range(KW):
            if h >= 2:
                pe.wait_ge(act_took, A_G0 + h - 1)
            for c in range(NCH - 1):
                last = pe.matmul(ps[:, 2 * ((h + 1) % 4), c * P:(c + 1) * P], vn[:, c, h * P:(h + 1) * P], wsT[:, h],
                                 start=True, stop=True)
            last.then_inc(product, 1)
        pe.wait_ge(dve_took, D_SETUP + 1)
        for h in range(KW):
            last = pe.matmul(ps[:, 2, h * NS:(h + 1) * NS], vn[0:NS, NCH - 1, h * P:(h + 1) * P], step_w[:, h],
                             start=True, stop=True)
        last.then_inc(product, 1)
        pe.wait_ge(pool_done, KW)
        pe.wait_ge(late_loaded, 16 * 8)
        for g in range(KW):
            r = (g + 2) % 4
            pe.wait_ge(dve_took, D_SETUP + g + 2)
            for half in range(2):
                last = pe.matmul(ps[:, 2 * r + half, 0:HT], pool_w[:, g], pool_d[:, g, half * HT:(half + 1) * HT],
                                 start=True, stop=True)
            last.then_inc(product, 1)

        def branches(i, first_slot):
            for b in range(4):
                if b % 2 == 0:
                    pe.wait_ge(low_ready, i * 4 + (FIRST_D1 + b // 2 + 1))
                if b == 2:
                    pe.wait_ge(sgu_low, KW)
                if first_slot == 0:
                    pe.wait_ge(act_took, i * 4 + (A_S - 3 + b))
                elif b < 3:
                    pe.wait_ge(act_took, A_D1 - 2 + b)
                else:
                    pe.wait_ge(dve_took, D_D1 + 1)
                column_tiles(b // 2, (y_high[b // 2], y_low[b // 2]), KW, (first_slot + b) % 4, b % 2).then_inc(product, 1)

        def channel_sum(r, src):
            for half in range(2):
                for q in range(KW):
                    last = pe.matmul(ps[:, 2 * r + half, 0:HT], const["ones"], src[:, q, half * HT:(half + 1) * HT],
                                     start=(q == 0), stop=(q == KW - 1))
            last.then_inc(product, 1)

        pe.wait_ge(dve_took, D_S)
        with pe.Fori(0, NJ - 1) as i:
            branches(i, 0)
            for g in range(4):
                if g % 2 == 0:
                    pe.wait_ge(low_ready, i * 4 + (FIRST_D1 + 2 + g // 2 + 1))
                pe.wait_ge(dve_took, i * 4 + (D_S + g + 1))
                column_tiles(g // 2, xs, KD, g, g % 2).then_inc(product, 1)
        pe.wait_ge(tap_step, 2 * KW * TAPS)
        pe.wait_ge(act_took, A_D1 - 3)
        channel_sum(0, yc)
        branches(NJ - 1, 1)
        pe.wait_ge(squared, KW)
        pe.wait_ge(dve_took, D_D1 + 2)
        channel_sum(1, squares)

        with pe.Fori(0, NJ // 2) as i:
            for g in range(4):
                if g % 2 == 0:
                    pe.wait_ge(low_ready, i * 4 + (FIRST_D2 + g // 2 + 1))
                pe.wait_ge(dve_took, i * 4 + (D_D2 - 3 + g))
                column_tiles(g // 2, xs, KD, (g + 2) % 4, g % 2).then_inc(product, 1)
            pe.wait_ge(conv_low, KW)
            for b in range(4):
                if b % 2 == 0:
                    pe.wait_ge(low_ready, i * 4 + (FIRST_D2 + 2 + b // 2 + 1))
                pe.wait_ge(act_took, i * 4 + (A_D1 + b + 1))
                column_tiles(b // 2, (y_high[2], y_low[2]), KW, (b + 2) % 4, b % 2).then_inc(product, 1)

        pe.wait_ge(merged_low, KD - 2)
        with pe.Fori(0, 2) as i:
            for s in range(2):
                pe.wait_ge(low_ready, i * 2 + (FIRST_OUT + s + 1))
                if s == 0:
                    pe.wait_ge(dve_took, i * NCH + D_B)
                token_chunks((m_high, m_low), s, merged_low)

        def logit_part(k):
            pe.wait_ge(*((act_took, A_B + k // 2 + 1) if k % 2 == 0 else (dve_took, D_O + k // 2 + 1)))
            for half, (rows, tokens) in enumerate(logit_halves):
                last = pe.matmul(ps[rows, 6 + half, 0:tokens.stop - tokens.start], router[:, k], xT[:, k, tokens],
                                 start=(k == 0), stop=(k == KD - 1))
            return last

        for k in range(KD):
            pe.wait_ge(dve_took, D_B + NCH + min(2 * k + 2, NCH) if k < 3 else D_O)
            if k >= 3:
                pe.wait_ge(*((act_took, A_B + (k - 3) // 2 + 1) if k % 2 == 1 else (dve_took, D_O + (k - 3 + 1) // 2)))
            for c in range(NCH):
                n = chunk_rows(c)
                last = pe.transpose(ps[:, 2 * (k % 3) + c // 4, (c % 4) * P:(c % 4) * P + n],
                                    x[0:n, c, k * P:(k + 1) * P], ident[0:n, 0:n])
            last.then_inc(product, 1)
            if k >= 1:
                logit_part(k - 1)
        logit_part(KD - 1).then_inc(product, 1)
        pe.wait_ge(dve_took, D_T + 1)
        pe.wait_ge(act_took, A_T + 1)
        for c in range(NCH):
            n = chunk_rows(c)
            rows = logit_halves[0 if c < 2 else 1][0]
            last = pe.transpose(ps[0:n, 0 if c < 2 else 1, c * (NG + NE):(c + 1) * (NG + NE)], row_a[rows, c * P:c * P + n],
                                ident[rows, rows])
        last.then_inc(product, 1)
        pe.wait_ge(chosen, 1)
        pe.matmul(ps[:, 2, 0:NCH * NE], const["before"], chosen_mask.rearrange("p c e -> p (c e)"), start=True, stop=True)
        pe.matmul(ps[:, 3, 0:NCH * NE], const["ones"], chosen_mask.rearrange("p c e -> p (c e)"),
                  start=True, stop=True).then_inc(product, 1)
        pe.wait_ge(tables_in, 1)
        for c in range(2 * NCH):
            last = pe.matmul(ps[:, 4, 0:2 * NBLK], at_place[:, c], in_block[:, c], start=(c == 0), stop=(c == 2 * NCH - 1))
        last.then_inc(product, 1)

        def turn_rows(e, s, turn, free):
            pe.wait_ge(xg_loaded[s], turn * 16 + 16)
            if free is not None:
                pe.wait_ge(xgT_ready, free)
            v = xg[s].rearrange("p (m c) -> p m c", c=4)
            for c in range(4):
                last = pe.transpose(ps[:, s, c * P:(c + 1) * P], v[:, :, c], ident)
            last.then_inc(xg_turned, 1)

        def gate_up(e, s, w, loads, free):
            pe.wait_ge(xgT_ready, e + 1)
            pe.wait_ge(gu_loaded[w], loads * 32)
            if free is not None:
                pe.wait_ge(hid_ready, free)
            for k in range(KD):
                for g in range(2):
                    last = pe.matmul(ps[g * CAP:(g + 1) * CAP, 2 + s].rearrange("p (m f) -> p m f", m=2),
                                     xgT[s][:, k % 4, (k // 4) * CAP:(k // 4 + 1) * CAP],
                                     gu[w][:, :, k, g * 256:(g + 1) * 256], start=(k == 0), stop=(k == KD - 1))
            last.then_inc(gu_done, 1)

        def turn_hidden(e, s, turn, free):
            pe.wait_ge(hid_ready, e + 1)
            if free is not None:
                pe.wait_ge(hT_ready, free)
            v = hid[s].rearrange("p (m c) -> p m c", c=2)
            for c in range(2):
                last = pe.transpose(ps[:, 4 + s, c * P:(c + 1) * P], v[:, :, c], ident)
            last.then_inc(hid_turned, 1)

        def down(e, s, w, loads, free):
            pe.wait_ge(hT_ready, e + 1)
            pe.wait_ge(dn_loaded[w], loads * 16)
            if free is not None:
                pe.wait_ge(yo_ready, free)
            for k in range(4):
                for g in range(2):
                    last = pe.matmul(ps[g * CAP:(g + 1) * CAP, 6 + s], hT[s][:, k % 2, (k // 2) * CAP:(k // 2 + 1) * CAP],
                                     dn[w][:, k, g * W:(g + 1) * W], start=(k == 0), stop=(k == 3))
            last.then_inc(dn_done, 1)

        pe.wait_ge(routed, 1)
        turn_rows(0, 0, 0, None)
        gate_up(0, 0, 0, 1, None)
        turn_rows(1, 1, 0, None)
        for e in range(2):
            gate_up(e + 1, 1 - e, e + 1, 1, 1 if e else None)
            turn_hidden(e, e, 0, None)
            down(e, e, e, 1, None)
            turn_rows(e + 2, e, 1, e + 1)
        turn_hidden(2, 0, 1, 1)
        down(2, 0, 2, 1, 1)
        with pe.Fori(0, NE // 2 - 2) as i:
            for w in range(2):
                e = 2 * i + 3 + w
                gate_up(e, 1 - w, w, i + 2, e - 1)
                turn_rows(e + 1, w, i + 2, e)
                turn_hidden(e, 1 - w, i + 1 + w, e - 1)
                down(e, 1 - w, w, i + 2, e - 1)
        e = NE - 1
        gate_up(e, 1, 0, NE // 2, e - 1)
        turn_hidden(e, 1, e // 2, e - 1)
        down(e, 1, 0, NE // 2, e - 1)
        n_over = pe.value_load(ovf[0:1, NOVF:NOVF + 1], min_val=0, max_val=NOVF)
        with pe.Fori(0, NOVF) as j:
            with pe.If(n_over > j):
                turn_rows(NE + j, 0, NE // 2 + j, NE + j)
                gate_up(NE + j, 0, 0, NE // 2 + 1 + j, NE + j)
                turn_hidden(NE + j, 0, NE // 2 + j, NE + j)
                down(NE + j, 0, 0, NE // 2 + 1 + j, NE + j)

    @block.scalar
    def _(act):
        n_own = [0]

        def own(instruction):
            n_own[0] += 1
            instruction.then_inc(act_step, 1)
            act.wait_ge(act_step, n_own[0])

        def high_part(s, turn, kt=KD):
            act.wait_ge(wring_loaded[s], turn * 16 + 16)
            nc.scalar.copy(w_high[s][:, 0:kt], wring[s][:, 0:kt]).then_inc(high_ready, 1)

        act.wait_ge(zeroed, 2)
        for c in range(NCH):
            n = chunk_rows(c)
            act.wait_ge(x_loaded[c], 16)
            own(nc.scalar.activation(junk[0:n], x[0:n, c], ACT.Square, accum_out=stat[0:n, c:c + 1]))
        nc.scalar.copy(stat[:, 10:10 + NCH], stat[:, 0:NCH]).then_inc(mean_sq, 1)
        act.wait_ge(root_in, 1)
        nc.scalar.activation(stat[:, 5:5 + NCH], stat[:, 0:NCH], ACT.Sqrt).then_inc(root, 1)
        act.wait_ge(product, 1)
        nc.scalar.copy(param[:, TAP:TAP + 4 * TAPS], ps[:, 6, 0:124])
        nc.scalar.copy(param[:, FG:FG + KD], ps[:, 6, 148:156])
        nc.scalar.copy(param[:, 0:24], ps[:, 6, 124:148]).then_inc(act_took, 1)
        act.wait_ge(act_took, 1)
        for k in range(KD):
            act.wait_ge(product, 1 + k + 1)
            nc.scalar.activation(x_high[:, k], slot_flat(k % 4), ACT.Identity, scale=param[:, MG + k:MG + k + 1]).then_inc(act_took, 1)
        act.wait_ge(product, KD + 2)
        for q in range(KW):
            last = nc.scalar.copy(
                cext[:, q, CH + SEQ:].rearrange("p (b i) -> p b i", i=CH + STEP)[:, :, 0:CH],
                ps[:, 4 + q // 2, (q % 2) * 240:(q % 2) * 240 + 240].rearrange("p (b i) -> p b i", i=CH))
        last.then_inc(act_took, 1)
        act.wait_ge(product, KD + 3)
        nc.scalar.copy(pool_hist.rearrange("p q t -> p (q t)"), ps[:, 6, 0:480]).then_inc(act_took, 1)
        high_part(1, 0)

        def take_projections(lo, hi):
            with act.Fori(lo, hi) as i:
                for r in range(4):
                    act.wait_ge(product, i * 4 + (N_SETUP + r + 1))
                    nc.scalar.copy(halves_at(proj, i * 4 + r), slot(r)).then_inc(act_took, 1)
                    if r % 2 == 1:
                        high_part(r // 2, i + 1)

        take_projections(0, 2)
        act.wait_ge(act_took, A_SETUP + 8)
        for q in range(KW):
            nc.scalar.activation(proj[:, KW + q], proj[:, KW + q], ACT.Sigmoid).then_inc(glu_gate, 1)
        take_projections(2, 4)
        act.wait_ge(half_rows, 1)
        high_part(0, 5)
        for c in range(NCH):
            n = chunk_rows(c)
            act.wait_ge(product, N_PROJ + c + 1)
            nc.scalar.copy(vn[0:n, c], ps[0:n, c]).then_inc(act_took, 1)

        high_part(1, 5)

        def take_gate(g, r):
            return nc.scalar.activation(halves(gates[:, g]), slot(r), ACT.Sigmoid).then_inc(act_took, 1)

        for g in range(4):
            act.wait_ge(product, N_V + g + 1)
            take_gate(g, (g + 3) % 4)
            if g % 2 == 1:
                high_part(g // 2, 6, KW)
            if g == 0:
                act.wait_ge(root_in, 2)
                nc.scalar.activation(stat[:, 20:20 + NCH], stat[:, 15:15 + NCH], ACT.Sqrt).then_inc(root, 1)
        for n, rows in enumerate((PH, CH)):
            act.wait_ge(product, N_G0 + n + 1)
            bank = (6, 0)[n]
            nc.scalar.copy(states[0:rows, 2 * n], ps[0:rows, bank])
            nc.scalar.copy(states[0:NS, 2 * n + 1], ps[0:NS, bank + 1]).then_inc(act_took, 1)
        for g in range(KW):
            act.wait_ge(product, N_G0 + 7 + g + 1)
            nc.scalar.activation(halves(y_high[0][:, g]), slot((g + 2) % 4), ACT.Identity,
                                 scale=param[:, PSC + g:PSC + g + 1]).then_inc(act_took, 1)
        act.wait_ge(sgu_done, 2 * KW)
        for h in range(KW):
            nc.scalar.copy(y_high[1][:, h], yb[:, h]).then_inc(sgu_high, 1)
        with act.Fori(0, NJ - 1) as i:
            for b in range(2):
                act.wait_ge(product, i * 8 + (N_S + 2 * b + 2))
                high_part(b, i * 2 + 7)
            for g in range(4):
                act.wait_ge(product, i * 8 + (N_S + 4 + g + 1))
                act.wait_ge(dve_took, i * 4 + (D_S + g + 1))
                take_gate(g, g)
                if g % 2 == 1:
                    high_part(g // 2, i * 2 + 8, KW)
        for q in range(KW):
            act.wait_ge(*((centred, q + 1) if q < KW - 1 else (dve_took, D_D1 + 1)))
            nc.scalar.activation(squares[:, q], yc[:, q], ACT.Square).then_inc(squared, 1)
        for b in range(2):
            act.wait_ge(product, N_D1 + 1 + 2 * b + 2)
            high_part(b, FIRST_D2 // 2)
        act.wait_ge(dve_took, D_D2)
        nc.scalar.activation(row_a[:], row_a[:], ACT.Sqrt).then_inc(root, 1)
        for q in range(KW):
            act.wait_ge(swish_in, q + 1)
            if q >= 2:
                act.wait_ge(yc_done, q - 1)
            nc.scalar.activation(tmp[q % 2][:, 0:T], yc[:, q], ACT.Sigmoid).then_inc(swish_sig, 1)
        act.wait_ge(states_stored, 16 * (4 + 2 * NSEQ))
        for q in range(KW):
            act.wait_ge(yc_done, q + 1)
            nc.scalar.copy(y_high[2][:, q], yc[:, q]).then_inc(conv_high, 1)
        with act.Fori(0, NJ // 2) as i:
            for g in range(4):
                act.wait_ge(product, i * 8 + (N_D2 + g + 1))
                act.wait_ge(dve_took, i * 4 + (D_D2 - 3 + g))
                take_gate(g, (g + 2) % 4)
                if g % 2 == 1:
                    high_part(g // 2, i * 2 + (FIRST_D2 // 2 + 1), KW)
            for b in range(4):
                if b % 2 == 1:
                    act.wait_ge(product, i * 8 + (N_D2 + 4 + b + 1))
                    high_part(b // 2, i * 2 + (FIRST_D2 // 2 + 2))
                act.wait_ge(merged_done, i * 4 + b + 1)
                nc.scalar.copy(m_high[:, bass.ds(i * 4 + b, 1)].rearrange("p a t -> p (a t)"),
                               merged[:, bass.ds(i * 4 + b, 1)].rearrange("p a t -> p (a t)")).then_inc(merged_high, 1)
        act.wait_ge(half_rows, 2)
        high_part(0, FIRST_OUT // 2 + 1)
        act.wait_ge(product, N_B + NCH)
        high_part(1, FIRST_OUT // 2 + 1)

        for i in range(2):
            for c in range(NCH):
                n = chunk_rows(c)
                act.wait_ge(dve_took, D_B + i * NCH + c + 1)
                if i == 1 and c == NCH - 1:
                    act.wait_ge(product, N_O + 1)
                    nc.scalar.copy(xT[:, 0], slot_flat(0)).then_inc(act_took, 1)
                own(nc.scalar.activation(junk_h[0:n], x[0:n, c, i * W:(i + 1) * W], ACT.Square,
                                         accum_out=stat[0:n, 30 + i * NCH + c:][:, 0:1]))
        nc.scalar.copy(stat[:, 40:50], stat[:, 30:40]).then_inc(mean_sq, 1)
        for k in range(2, KD, 2):
            act.wait_ge(product, N_O + k + 1)
            nc.scalar.copy(xT[:, k], slot_flat(k % 3)).then_inc(act_took, 1)
        act.wait_ge(root_in, 3)
        nc.scalar.activation(stat[:, 55:60], stat[:, 50:55], ACT.Sqrt).then_inc(root, 1)
        act.wait_ge(product, N_T + 1)
        rows, tokens = logit_halves[1]
        nc.scalar.copy(row_a[rows, tokens], ps[rows, 7, 0:T - 2 * P]).then_inc(act_took, 1)
        act.wait_ge(rstd_in, 1)
        for c in range(NCH):
            n = chunk_rows(c)
            nc.scalar.activation(xn2[0:n, c], x[0:n, c], ACT.Identity, scale=stat[0:n, 60 + c:61 + c]).then_inc(h_scaled, 1)
        act.wait_ge(exp_in, 1)
        nc.scalar.activation(group_exp, group_exp, ACT.Exp).then_inc(exp_done, 1)
        act.wait_ge(exp_in, 2)
        nc.scalar.activation(pair_exp, pair_exp, ACT.Exp).then_inc(exp_done, 1)

        def silu(e, s, turn, free):
            act.wait_ge(gu_done, e + 1)
            if free is not None:
                act.wait_ge(hid_ready, free)
            nc.scalar.activation(sig[s], ps[:, 2 + s, 0:256], ACT.Silu).then_inc(sig_ready, 1)

        def take_hidden(e, s, turn, free):
            act.wait_ge(hid_turned, e + 1)
            if free is not None:
                act.wait_ge(dn_done, free)
            nc.scalar.copy(hT[s].rearrange("p c m -> p (c m)"), ps[:, 4 + s, 0:256]).then_inc(hT_ready, 1)

        def take_output(e, s, turn, free):
            act.wait_ge(dn_done, e + 1)
            if free is not None:
                act.wait_ge(scattered[s], turn * 16)
            nc.scalar.copy(yo[s], ps[:, 6 + s]).then_inc(yo_ready, 1)

        for e in range(2):
            for stage in (silu, take_hidden, take_output):
                stage(e, e, 0, None)
        with act.Fori(1, NE // 2) as i:
            for s in range(2):
                for stage in (silu, take_hidden, take_output):
                    stage(2 * i + s, s, i, 2 * i + s - 1)
        act.wait_ge(routed, 1)
        n_over = act.value_load(ovf[0:1, NOVF:NOVF + 1], min_val=0, max_val=NOVF)
        with act.Fori(0, NOVF) as j:
            with act.If(n_over > j):
                for stage in (silu, take_hidden, take_output):
                    stage(NE + j, 0, NE // 2 + j, NE + j)

        for c in FINAL_ORDER:
            n = chunk_rows(c)
            act.wait_ge(*((summed, c + 1) if c < NCH - 1 else (pool_summed, 1)))
            own(nc.scalar.activation(flat_y[0:n, 0:D], x[0:n, c], ACT.Square, accum_out=stat[0:n, 60 + c:61 + c]))
            nc.scalar.activation(stat[0:n, 65 + c:66 + c], stat[0:n, 60 + c:61 + c], ACT.Sqrt,
                                 scale=1.0 / D, bias=stat[0:n, 95:96]).then_inc(final_root, 1)

    @block.vector
    def _(dve):
        v = nc.vector
        n_own = [0]

        def own(instruction):
            n_own[0] += 1
            instruction.then_inc(dve_step, 1)
            dve.wait_ge(dve_step, n_own[0])

        def wide(a, shape):
            return a.broadcast_to(shape)

        dve.wait_ge(mean_sq, 1)
        v.tensor_scalar(stat[:, 0:NCH], stat[:, 10:10 + NCH], 1.0 / D, EPS, ALU.mult, ALU.add).then_inc(root_in, 1)
        dve.wait_ge(root, 1)
        own(v.reciprocal(stat[:, 10:10 + NCH], stat[:, 5:5 + NCH]))
        for c in range(NCH):
            n = chunk_rows(c)
            v.tensor_scalar(x[0:n, c], x[0:n, c], stat[0:n, 10 + c:11 + c], None, ALU.mult).then_inc(x_normed, 1)
        for k in range(KD):
            dve.wait_ge(act_took, 1 + k + 1)
            v.scalar_tensor_tensor(x_low[:, k], slot_flat(k % 4), param[:, MG + k:MG + k + 1], x_high[:, k].bitcast(F32),
                                   ALU.mult, ALU.subtract).then_inc(dve_took, 1)
        dve.wait_ge(product, N_SETUP)
        v.tensor_tensor(wsT, ps[:, 7].rearrange("p (h t) -> p h t", h=KW),
                        wide(const["causal"].unsqueeze(1), [P, KW, P]), ALU.mult).then_inc(dve_took, 1)
        dve.wait_ge(step_loaded, 16 * NSEQ * KW)
        own(v.tensor_tensor(step_w, step_w, wide(const["blocks"][0:NS].unsqueeze(1), [NS, KW, NS]), ALU.mult))

        dve.wait_ge(late_loaded, 16 * 8)
        for k in range(KD):
            v.tensor_scalar(router[:, k], router[:, k], param[:, FG + k:FG + k + 1], None, ALU.mult)

        dve.wait_ge(zeroed, 3)
        for q in range(KW):
            dve.wait_ge(glu_gate, q + 1)
            v.tensor_tensor(cext[:, q, CH:CH + SEQ], proj[:, q, 0:SEQ], proj[:, KW + q, 0:SEQ], ALU.mult).then_inc(glu_done, 1)
            v.tensor_tensor(proj[:, q, SEQ:T], proj[:, q, SEQ:T], proj[:, KW + q, SEQ:T], ALU.mult).then_inc(glu_done, 1)
            dve.wait_ge(glu_done, 2 * q + 2)
            own(v.tensor_copy(cext[:, q, CH + SEQ:].rearrange("p (b i) -> p b i", i=CH + STEP)[:, :, CH:],
                              proj[:, q, SEQ:T].rearrange("p (b i) -> p b i", i=STEP)))
        def tap(k, n_before):
            for q in range(KW):
                w = param[:, bass.ds(k * KW + (TAP + q), 1)]
                for part, (src, acc) in enumerate((
                    (cext[:, q, bass.ds(k, SEQ)], yc[:, q, 0:SEQ]),
                    (cext[:, q, CH + SEQ:].rearrange("p (b i) -> p b i", i=CH + STEP)[:, :, bass.ds(k, STEP)],
                     yc[:, q, SEQ:T].rearrange("p (b i) -> p b i", i=STEP)),
                )):
                    if n_before is None:
                        last = v.tensor_scalar(acc, src, w, param[:, CB + q:CB + q + 1], ALU.mult, ALU.add)
                    else:
                        dve.wait_ge(tap_step, n_before * (2 * KW) + (1 - 2 * KW + 2 * q + part))
                        last = v.scalar_tensor_tensor(acc, src, w, acc, ALU.mult, ALU.add)
                    last.then_inc(tap_step, 1)

        for k in range(EARLY_TAPS):
            tap(k, k if k else None)

        mv = stat[:, 96:106].rearrange("p (c m) -> p c m", m=2)
        bn6 = stat[:, 106:112]
        for c in range(NCH):
            n = chunk_rows(c)
            dve.wait_ge(act_took, A_PROJ + c + 1)
            own(v.bn_stats(bn6[0:n], vn[0:n, c]))
            own(v.bn_aggr(mv[0:n, c], bn6[0:n]))
        v.tensor_scalar(stat[:, 15:15 + NCH], mv[:, :, 1], EPS, None, ALU.add).then_inc(root_in, 1)
        dve.wait_ge(late_loaded, 16 * 8)
        dve.wait_ge(root, 2)
        own(v.reciprocal(stat[:, 25:25 + NCH], stat[:, 20:20 + NCH]))
        for c in range(NCH):
            n = chunk_rows(c)
            own(v.tensor_scalar(vn[0:n, c], vn[0:n, c], mv[0:n, c, 0:1], stat[0:n, 25 + c:26 + c], ALU.subtract, ALU.mult))
            own(v.tensor_tensor(vn[0:n, c], vn[0:n, c], sgu_rows[0:n, 0], ALU.mult))
            v.tensor_tensor(vn[0:n, c], vn[0:n, c], sgu_rows[0:n, 1], ALU.add).then_inc(v_normed, 1)

        for h in range(KW):
            dve.wait_ge(product, N_G0 + 2 + h + 1)
            v.tensor_tensor(yb[:, h, 0:SEQ].rearrange("p (c t) -> p c t", t=P),
                                ps[:, 2 * ((h + 1) % 4)].rearrange("p (c t) -> p c t", t=P),
                                wide(bias_rows[:, h:h + 1], [P, SEQ // P, P]), ALU.add).then_inc(dve_took, 1)
            dve.wait_ge(dve_took, D_SETUP + h + 1)
            v.tensor_tensor(yb[:, h, 0:SEQ], yb[:, h, 0:SEQ], proj[:, 3 * KW + h, 0:SEQ], ALU.mult).then_inc(sgu_done, 1)
        dve.wait_ge(product, N_G0 + 2 + KW + 1)
        for h in range(KW):
            last = (v.tensor_tensor(yb[:, h, SEQ:T].rearrange("p (b i) -> p b i", i=STEP),
                                ps[:, 2, h * NS:(h + 1) * NS].rearrange("p (b i) -> p b i", i=STEP),
                                wide(bias_rows[:, h:h + 1, 0:STEP], [P, NSEQ, STEP]), ALU.add))
        last.then_inc(dve_took, 1)
        dve.wait_ge(dve_took, D_SETUP + KW + 1)
        for h in range(KW):
            v.tensor_tensor(yb[:, h, SEQ:T], yb[:, h, SEQ:T], proj[:, 3 * KW + h, SEQ:T], ALU.mult).then_inc(sgu_done, 1)
        for g in range(KW):
            dve.wait_ge(act_took, A_S - KW + g + 1)
            v.scalar_tensor_tensor(halves(y_low[0][:, g]), slot((g + 2) % 4), param[:, PSC + g:PSC + g + 1],
                                   halves(y_high[0][:, g].bitcast(F32)), ALU.mult, ALU.subtract).then_inc(dve_took, 1)

        def merge(i, first_slot, taken):
            dve.wait_ge(act_took, i * 4 + A_S)
            for b in range(4):
                m = halves_at(merged, i * 2 + b % 2)
                t = halves(tmp[b % 2][:, 0:T])
                dve.wait_ge(product, i * 8 + (N_S + b + 1) if first_slot == 0 else N_D1 + 1 + b + 1)
                v.tensor_tensor(m if b < 2 else t, slot((first_slot + b) % 4), halves(gates[:, b]), ALU.mult).then_inc(dve_took, 1)
                if b >= 2:
                    dve.wait_ge(dve_took, i * 4 + (taken + b + 1))
                    v.tensor_tensor(m, m, t, ALU.add).then_inc(merged_part, 1)
            dve.wait_ge(merged_part, i * 2 + 2)

        dve.wait_ge(outs_stored, 16)
        with dve.Fori(0, NJ - 1) as i:
            merge(i, 0, D_S)
            for k in range(LATE_TAPS):
                tap(i * LATE_TAPS + (EARLY_TAPS + k), i * LATE_TAPS + (EARLY_TAPS + k))
        dve.wait_ge(tap_step, 2 * KW * TAPS)

        dve.wait_ge(product, N_D1 + 1)
        for q in range(KW):
            v.scalar_tensor_tensor(halves(yc[:, q]), slot(0), -1.0 / W, halves(yc[:, q]), ALU.mult, ALU.add).then_inc(
                centred if q < KW - 1 else dve_took, 1)
        merge(NJ - 1, 1, D_S + 1)
        dve.wait_ge(product, N_D2)
        v.tensor_scalar(halves(row_a[:]), slot(1), 1.0 / W, EPS, ALU.mult, ALU.add).then_inc(dve_took, 1)
        dve.wait_ge(root, 3)
        own(v.reciprocal(row_a[:], row_a[:]))
        for q in range(KW):
            own(v.tensor_tensor(yc[:, q], yc[:, q], row_a[:], ALU.mult))
            v.tensor_scalar(yc[:, q], yc[:, q], param[:, CG + q:CG + q + 1], param[:, CNB + q:CNB + q + 1],
                            ALU.mult, ALU.add).then_inc(swish_in, 1)
        for q in range(KW):
            dve.wait_ge(swish_sig, q + 1)
            dve.wait_ge(swish_in, q + 1)
            v.tensor_tensor(yc[:, q], yc[:, q], tmp[q % 2][:, 0:T], ALU.mult).then_inc(yc_done, 1)
        for q in range(KW):
            dve.wait_ge(conv_high, q + 1)
            v.tensor_tensor(y_low[2][:, q], yc[:, q], y_high[2][:, q].bitcast(F32), ALU.subtract).then_inc(conv_low, 1)
        with dve.Fori(0, NJ // 2) as i:
            for b in range(4):
                m = halves_at(merged, i * 4 + b)
                t = halves(tmp[b % 2][:, 0:T])
                dve.wait_ge(act_took, i * 4 + (A_D1 + b + 1))
                dve.wait_ge(product, i * 8 + (N_D2 + 4 + b + 1))
                v.tensor_tensor(t, slot((b + 2) % 4), halves(gates[:, b]), ALU.mult).then_inc(dve_took, 1)
                dve.wait_ge(dve_took, i * 4 + (D_D2 + b + 1))
                v.tensor_tensor(m, m, t, ALU.add).then_inc(merged_done, 1)
                dve.wait_ge(merged_high, i * 4 + b + 1)
                v.tensor_tensor(halves_at(m_low, i * 4 + b), m, halves_at(m_high, i * 4 + b).bitcast(F32),
                                ALU.subtract).then_inc(merged_low, 1)

        dve.wait_ge(merged_done, KD)
        dve.wait_ge(x_again, 32)
        for i in range(2):
            for c in range(NCH):
                n = chunk_rows(c)
                dve.wait_ge(product, N_B + i * NCH + c + 1)
                v.tensor_tensor(x[0:n, c, i * W:(i + 1) * W], ps[0:n, c], x[0:n, c, i * W:(i + 1) * W],
                                ALU.add).then_inc(dve_took, 1)
        for k in range(1, KD, 2):
            dve.wait_ge(product, N_O + k + 1)
            v.tensor_copy(xT[:, k], slot_flat(k % 3)).then_inc(dve_took, 1)
            if k == 1:
                dve.wait_ge(mean_sq, 2)
                own(v.tensor_tensor(stat[:, 50:55], stat[:, 40:45], stat[:, 45:50], ALU.add))
                v.tensor_scalar(stat[:, 50:55], stat[:, 50:55], 1.0 / D, EPS, ALU.mult, ALU.add).then_inc(root_in, 1)
        dve.wait_ge(root, 4)
        v.reciprocal(stat[:, 60:65], stat[:, 55:60]).then_inc(rstd_in, 1)
        dve.wait_ge(rstd_in, 1)
        own(v.memset(logits, 0.0))
        dve.wait_ge(product, N_T + 1)
        rows, tokens = logit_halves[0]
        v.tensor_copy(row_a[rows, tokens], ps[rows, 6, 0:2 * P]).then_inc(dve_took, 1)
        dve.wait_ge(product, N_T + 2)
        for c in range(NCH):
            n = chunk_rows(c)
            rows = ps[0:n, 0 if c < 2 else 1, c * (NG + NE):(c + 1) * (NG + NE)]
            last = v.scalar_tensor_tensor(logits[0:n, c], rows, stat[0:n, 60 + c:61 + c], router_b[0:n], ALU.mult, ALU.add)
        own(last)

        def s5(i):
            return small[:, i]

        def w5(i, n):
            return wide(small[:, i].unsqueeze(2), [P, NCH, n])

        def c5(name, n):
            return wide(const[name].unsqueeze(1), [P, NCH, n])

        gl, el = logits[:, :, 0:NG], logits[:, :, NG:]
        own(v.tensor_reduce(s5(1), gl, AX, ALU.max))
        v.tensor_tensor(group_exp, gl, w5(1, NG), ALU.subtract).then_inc(exp_in, 1)
        own(v.tensor_tensor(cand[:, :, 0:NG], gl, w5(1, NG), ALU.not_equal))
        own(v.scalar_tensor_tensor(cand[:, :, 0:NG], cand[:, :, 0:NG], 64.0, c5("group", NG), ALU.mult, ALU.add))
        own(v.tensor_reduce(s5(2), cand[:, :, 0:NG], AX, ALU.min))
        own(v.tensor_tensor(cand, c5("group_of", NE), w5(2, NE), ALU.is_equal))
        own(v.tensor_tensor(masked, el, cand, ALU.mult))
        own(v.tensor_scalar(cand, cand, -1.0, 1e30, ALU.add, ALU.mult))
        own(v.tensor_tensor(masked, masked, cand, ALU.add))
        for k in range(2):
            own(v.tensor_reduce(s5(3 + k), masked, AX, ALU.max))
            own(v.tensor_tensor(cand, masked, w5(3 + k, NE), ALU.not_equal))
            own(v.scalar_tensor_tensor(cand, cand, 64.0, c5("expert", NE), ALU.mult, ALU.add))
            own(v.tensor_reduce(s5(5 + k), cand, AX, ALU.min))
            own(v.tensor_tensor(one_hot[k], c5("expert", NE), w5(5 + k, NE), ALU.is_equal))
            if k == 0:
                own(v.scalar_tensor_tensor(masked, one_hot[0], -1e31, masked, ALU.mult, ALU.add))
        v.tensor_tensor(pair_exp, s5(4), s5(3), ALU.subtract).then_inc(exp_in, 1)
        own(v.tensor_tensor(chosen_mask, one_hot[0], one_hot[1], ALU.add))
        v.tensor_tensor(chosen_mask, chosen_mask, wide(const["valid"].unsqueeze(2), [P, NCH, NE]), ALU.mult).then_inc(chosen, 1)
        dve.wait_ge(exp_done, 2)
        own(v.tensor_reduce(s5(7), group_exp, AX, ALU.add))
        own(v.tensor_scalar(s5(8), pair_exp, 1.0, None, ALU.add))
        own(v.tensor_tensor(s5(7), s5(7), s5(8), ALU.mult))
        own(v.reciprocal(gate_of[:, 0], s5(7)))
        own(v.tensor_tensor(gate_of[:, 1], gate_of[:, 0], pair_exp, ALU.mult))
        dve.wait_ge(product, N_L + 1)
        own(v.memset(before_chunk[:, 0], 0.0))
        for c in range(NCH):
            own(v.tensor_tensor(before_chunk[:, c + 1], ps[:, 3, c * NE:(c + 1) * NE], before_chunk[:, c], ALU.add))
        own(v.tensor_tensor(rank, ps[:, 2, 0:NCH * NE].rearrange("p (c e) -> p c e", e=NE), before_chunk[:, 0:NCH], ALU.add))
        own(v.tensor_tensor(compare, wide(before_chunk[:, NCH].unsqueeze(2), [P, NE, MAXB]),
                            wide(const["steps"].unsqueeze(1), [P, NE, MAXB]), ALU.is_gt))
        own(v.tensor_reduce(further[:, 0], compare, AX, ALU.add))
        own(v.tensor_tensor_scan(further[:, 1], const["ones"][:, 0:NE], further[:, 0], 0.0, ALU.mult, ALU.add))
        own(v.tensor_tensor(further[:, 2], further[:, 1], further[:, 0], ALU.subtract))
        def b10(i, n):
            return wide(both[:, i].unsqueeze(2), [P, 2 * NCH, n])

        def c10(name, n):
            return wide(const[name].unsqueeze(1), [P, 2 * NCH, n])

        chosen_e = small[:, 5:7].rearrange("p k c -> p (k c)")
        own(v.tensor_tensor(both_cand.rearrange("p (k c) e -> p k (c e)", k=2), both_hot.rearrange("p (k c) e -> p k (c e)", k=2),
                            wide(rank.rearrange("p c e -> p (c e)").unsqueeze(1), [P, 2, NCH * NE]), ALU.mult))
        own(v.tensor_reduce(both[:, 0], both_cand, AX, ALU.add))
        own(v.tensor_tensor(both_cand, both_hot, wide(further[:, 2:3], [P, 2 * NCH, NE]), ALU.mult))
        own(v.tensor_reduce(both[:, 1], both_cand, AX, ALU.add))
        own(v.tensor_tensor(by_step, b10(0, MAXB), c10("steps", MAXB), ALU.is_ge))
        own(v.tensor_reduce(both[:, 2], by_step, AX, ALU.add))
        own(v.scalar_tensor_tensor(both[:, 3], both[:, 2], -float(CAP), both[:, 0], ALU.mult, ALU.add))
        own(v.tensor_tensor(at_place, c10("place", P), b10(3, P), ALU.is_equal))
        own(v.tensor_tensor(both[:, 4], both[:, 1], both[:, 2], ALU.add))
        own(v.scalar_tensor_tensor(both[:, 4], both[:, 4], float(NE - 1), chosen_e, ALU.add, ALU.subtract))
        own(v.scalar_tensor_tensor(both[:, 4], both[:, 2], 0.0, both[:, 4], ALU.is_gt, ALU.mult))
        own(v.tensor_tensor(both[:, 4], both[:, 4], chosen_e, ALU.add))
        own(v.tensor_tensor(cand_b, c10("block", NBLK), b10(4, NBLK), ALU.is_equal))
        own(v.tensor_tensor(in_block[:, :, 0:NBLK], cand_b, wide(const["gather_row"].unsqueeze(2), [P, 2 * NCH, NBLK]), ALU.mult))
        v.tensor_tensor(in_block[:, :, NBLK:], cand_b, wide(const["scatter_row"].unsqueeze(2), [P, 2 * NCH, NBLK]),
                        ALU.mult).then_inc(tables_in, 1)
        own(v.tensor_tensor(compare_e, wide(further[:, 1:2], [P, NOVF, NE]),
                            wide(const["further"].unsqueeze(2), [P, NOVF, NE]), ALU.is_le))
        own(v.tensor_reduce(at_further, compare_e, AX, ALU.add))
        own(v.tensor_scalar(ovf[:, 0:NOVF], at_further, float(NE - 1), None, ALU.min))
        own(v.tensor_copy(ovf[:, NOVF:], further[:, 1, NE - 1:NE]))
        dve.wait_ge(product, N_L + 2)
        rows = ps[:, 4, 0:2 * NBLK]
        own(v.tensor_scalar(empty, rows, 0.0, OFF, ALU.is_equal, ALU.mult))
        own(v.scalar_tensor_tensor(empty, empty, const["half"], rows, ALU.add, ALU.add))
        v.tensor_scalar(block_rows[:], empty, -2.0, None, ALU.add).then_inc(routed, 1)

        def take_rows(e, s, turn, free):
            dve.wait_ge(xg_turned, e + 1)
            if free is not None:
                dve.wait_ge(gu_done, free)
            v.tensor_copy(xgT[s].rearrange("p c m -> p (c m)"), ps[:, s]).then_inc(xgT_ready, 1)

        def times_up(e, s, turn, free):
            dve.wait_ge(sig_ready, e + 1)
            if free is not None:
                dve.wait_ge(hid_turned, free)
            v.tensor_tensor(hid[s], sig[s], ps[:, 2 + s, 256:512], ALU.mult).then_inc(hid_ready, 1)

        dve.wait_ge(xn2_stored, 16 * NCH)
        take_rows(0, 0, 0, None)
        for e in range(2):
            take_rows(e + 1, 1 - e, e, None if e == 0 else 1)
            times_up(e, e, 0, None)
        with dve.Fori(1, NE // 2 - 1) as i:
            for s in range(2):
                take_rows(2 * i + s + 1, 1 - s, i + s, 2 * i + s)
                times_up(2 * i + s, s, i, 2 * i + s - 1)
        i = NE // 2 - 1
        take_rows(2 * i + 1, 1, i, 2 * i)
        times_up(2 * i, 0, i, 2 * i - 1)
        times_up(2 * i + 1, 1, i, 2 * i)
        n_over = dve.value_load(ovf[0:1, NOVF:NOVF + 1], min_val=0, max_val=NOVF)
        with dve.Fori(0, NOVF) as j:
            with dve.If(n_over > j):
                take_rows(NE + j, 0, NE // 2 + j, NE + j)
                times_up(NE + j, 0, NE // 2 + j, NE + j)

        own(v.memset(stat[:, 95:96], EPS))
        dve.wait_ge(norm_rows_loaded, 32)

        def last_sum(c):
            dve.wait_ge(y_loaded[c], 16)
            yr = y_place(c).rearrange("p (k n) -> p k n", k=2)
            own(v.scalar_tensor_tensor(x[:, c], yr[:, 0], gate_of[:, 0, c:c + 1], x[:, c], ALU.mult, ALU.add))
            v.scalar_tensor_tensor(x[:, c], yr[:, 1], gate_of[:, 1, c:c + 1], x[:, c], ALU.mult, ALU.add).then_inc(summed, 1)

        def last_norm(c):
            n = chunk_rows(c)
            dve.wait_ge(final_root, FINAL_ORDER.index(c) + 1)
            own(v.reciprocal(stat[0:n, 70 + c:71 + c], stat[0:n, 65 + c:66 + c]))
            v.scalar_tensor_tensor(x[0:n, c], x[0:n, c], stat[0:n, 70 + c:71 + c], final_row[0:n], ALU.mult, ALU.mult).then_inc(final_done, 1)

        last_sum(0)
        last_sum(1)
        last_norm(0)
        last_sum(2)
        last_norm(1)
        last_sum(3)
        last_norm(2)
        last_norm(3)
        last_norm(4)

    @block.gpsimd
    def _(pool):
        g = nc.gpsimd
        n_own = [0]

        def own(instruction):
            n_own[0] += 1
            instruction.then_inc(pool_step, 1)
            pool.wait_ge(pool_step, n_own[0])

        g.memset(step_w, 0.0).then_inc(zeroed, 1)
        g.memset(stat[:], 1.0).then_inc(zeroed, 1)
        g.memset(cext[:, :, 0:CH], 0.0).then_inc(zeroed, 1)

        def low_part(s, n, kt=KD, first=False):
            if not first:
                pool.wait_ge(high_ready, n)
            g.tensor_tensor(w_low[s][:, 0:kt], wring[s][:, 0:kt], w_high[s][:, 0:kt].bitcast(F32), ALU.subtract).then_inc(low_ready, 1)

        def window_sums(q):
            pool.wait_ge(act_took, A_SETUP + 8 + q + 1)
            p_q = proj[:, 2 * KW + q]
            own(g.memset(tmp[0][:, 0:PH], 0.0))
            own(g.tensor_copy(tmp[0][:, PH:PH + SEQ], p_q[:, 0:SEQ]))
            ext = tmp[0][:, PH + SEQ:].rearrange("p (b i) -> p b i", i=PH + STEP)
            own(g.tensor_copy(ext[:, :, 0:PH], pool_hist[:, q].rearrange("p (b i) -> p b i", i=PH)))
            own(g.tensor_copy(ext[:, :, PH:], p_q[:, SEQ:T].rearrange("p (b i) -> p b i", i=STEP)))
            for level in range(q + 1):
                src, dst, shift = tmp[level % 2], tmp[(level + 1) % 2], 1 << level
                own(g.tensor_tensor(dst[:, shift:], src[:, shift:], src[:, 0:PEXT - shift], ALU.add))
                own(g.tensor_copy(dst[:, 0:shift], src[:, 0:shift]))

        def less_token(q):
            s = tmp[(q + 1) % 2]
            w = float(WINDOWS[q])
            own(g.tensor_scalar(pool_d[:, q, 0:SEQ], s[:, PH:PH + SEQ], 1 / w, None, ALU.mult))
            own(g.tensor_tensor(pool_d[:, q, 0:16], s[:, PH:PH + 16], const["count"][:, 16 * q:16 * q + 16], ALU.mult))
            own(g.tensor_scalar(pool_d[:, q, SEQ:T].rearrange("p (b i) -> p b i", i=STEP),
                                s[:, PH + SEQ:].rearrange("p (b i) -> p b i", i=PH + STEP)[:, :, PH:], 1 / w, None, ALU.mult))
            g.tensor_tensor(pool_d[:, q], pool_d[:, q], proj[:, 2 * KW + q], ALU.subtract).then_inc(pool_done, 1)

        pool.wait_ge(wring_loaded[0], 16)
        own(g.tensor_copy(w_high[0][:], wring[0]))
        for n in range(FIRST_D1):
            low_part(n % 2, n, first=(n == 0))
            if n == 6:
                pool.wait_ge(product, N_SETUP)
                pool.wait_ge(dve_took, D_SETUP)
            if n in (6, 7):
                window_sums(n - 6)
                less_token(n - 6)
            if n in (8, 10):
                window_sums(2 + (n - 8) // 2)
            if n in (9, 11):
                less_token(2 + (n - 9) // 2)
        for s in range(2):
            low_part(s, FIRST_D1 + s, KW)
        for h in range(KW):
            pool.wait_ge(sgu_high, h + 1)
            g.tensor_tensor(y_low[1][:, h], yb[:, h], y_high[1][:, h].bitcast(F32), ALU.subtract).then_inc(sgu_low, 1)
        with pool.Fori(0, NJ - 1) as i:
            for n in range(4):
                low_part(n % 2, i * 4 + (FIRST_D1 + 2 + n), KD if n < 2 else KW)
        for s in range(2):
            low_part(s, FIRST_D2 + s)
        with pool.Fori(0, NJ // 2) as i:
            for n in range(4):
                low_part(n % 2, i * 4 + (FIRST_D2 + 2 + n), KW if n < 2 else KD)
        for s in range(2):
            low_part(s, FIRST_OUT + 2 + s)

        pool.wait_ge(norm_rows_loaded, 16)
        for c in range(NCH):
            n = chunk_rows(c)
            pool.wait_ge(h_scaled, c + 1)
            g.tensor_tensor(xn2[0:n, c], xn2[0:n, c], ffn_row[0:n], ALU.mult).then_inc(xn2_done, 1)

        def gather(e, s, turn, free):
            if free is not None:
                pool.wait_ge(xg_turned, free)
                pool.sem_inc(waits_met, 1)
            g.tensor_copy(idx_now[:, s:s + 1], block_rows[:, bass.ds(e, 1)]).then_inc(gather_idx[s], 1)
            pool.wait_ge(gather_idx[s], turn + 1)
            pool.sem_inc(waits_met, 1)
            pool.indirect_dma_start(xg[s], None, xn2_dram.rearrange("t (h n) -> (t h) n", h=2),
                                    bass.IndirectOffsetOnAxis(ap=idx_now[:, s:s + 1], axis=0),
                                    bounds_check=2 * T - 1, oob_is_err=False).then_inc(xg_loaded[s], 16)

        def scatter(e, s, turn, free):
            if free is not None:
                pool.wait_ge(scattered[s], turn * 16)
                pool.sem_inc(waits_met, 1)
            g.tensor_copy(idx_now[:, 2 + s:3 + s], block_rows[:, bass.ds(NBLK + e, 1)]).then_inc(scatter_idx[s], 1)
            pool.wait_ge(scatter_idx[s], turn + 1)
            pool.wait_ge(yo_ready, e + 1)
            pool.sem_inc(waits_met, 1)
            pool.indirect_dma_start(y_dram, bass.IndirectOffsetOnAxis(ap=idx_now[:, 2 + s:3 + s], axis=0), yo[s], None,
                                    bounds_check=4 * T - 1, oob_is_err=False).then_inc(scattered[s], 16)

        pool.wait_ge(routed, 1)
        pool.wait_ge(xn2_stored, 16 * NCH)
        for e in range(2):
            gather(e, e, 0, None)
        for e in range(2):
            gather(e + 2, e, 1, e + 1)
            scatter(e, e, 0, None)
        with pool.Fori(1, NE // 2 - 1) as i:
            for s in range(2):
                gather(2 * i + s + 2, s, i + 1, 2 * i + s + 1)
                scatter(2 * i + s, s, i, True)
        i = NE // 2 - 1
        for s in range(2):
            scatter(2 * i + s, s, i, True)
        n_over = pool.value_load(ovf[0:1, NOVF:NOVF + 1], min_val=0, max_val=NOVF)
        with pool.Fori(0, NOVF) as j:
            with pool.If(n_over > j):
                gather(NE + j, 0, NE // 2 + j, NE + j)
                scatter(NE + j, 0, NE // 2 + j, True)
        pool.wait_ge(y_loaded[NCH - 1], 16)
        rows = y_place(NCH - 1)[0:NS].rearrange("p (k n) -> p k n", k=2)
        for k in range(2):
            own(g.tensor_scalar(rows[:, k], rows[:, k], gate_of[0:NS, k, NCH - 1:NCH], None, ALU.mult))
            last = g.tensor_tensor(x[0:NS, NCH - 1], x[0:NS, NCH - 1], rows[:, k], ALU.add)
            if k == 0:
                own(last)
        last.then_inc(pool_summed, 1)


INPUTS = [
    "x_prompt", "x_sample", "state_pool", "state_conv", "mix_norm_g", "w_in", "pool_w", "pool_scale", "sgu_norm_g",
    "sgu_norm_b", "sgu_w", "sgu_b", "conv_w", "conv_b", "conv_norm_g", "conv_norm_b", "w_branch_pool",
    "w_branch_sgu", "w_branch_conv", "w_out", "ffn_norm_g", "w_group", "b_group", "w_router", "b_router",
    "w_gate_e", "w_up_e", "w_down_e", "final_norm_g",
]
OUTPUTS = [
    ("y_prompt", (1, SEQ, D)), ("y_sample", (NSEQ, STEP, D)), ("pool_prompt", (1, 1, PH, W)),
    ("pool_sample", (1, NSEQ, PH, W)), ("conv_prompt", (1, 1, CH, W)), ("conv_sample", (1, NSEQ, CH, W)),
    ("chunk_v_sample", (1, NSEQ, STEP, W)),
]


def kernel(**inputs):
    import concourse.bacc as bacc
    from concourse.bass_utils import run_bass_kernel_spmd

    nc = bacc.Bacc("TRN2", target_bir_lowering=False, num_devices=1)
    arrays = {name: np.ascontiguousarray(inputs[name]) for name in INPUTS}
    arrays["shape_constants"] = shape_constants()
    d = {name: nc.dram_tensor("in_" + name, a.shape, F32, kind="ExternalInput").ap() for name, a in arrays.items()}
    out = {name: nc.dram_tensor("out_" + name, shape, F32, kind="ExternalOutput").ap() for name, shape in OUTPUTS}
    build(nc, d, out)
    result = run_bass_kernel_spmd(nc, [{"in_" + name: a for name, a in arrays.items()}], core_ids=[0]).results[0]
    return tuple(result["out_" + name] for name, _ in OUTPUTS)
```
